# Optimizing a Trainium2 kernel written in Bass

```python
import jax, jax.numpy as jnp
from jax import lax
import numpy as np

D_MODEL = 2048
BATCH = 1
SEQ = 512
DEPTH = 2

CTX_LEN = 256
GRID_W = 64

D_MIX = D_MODEL
POOL_WIDTH = D_MIX // 4
POOL_WINDOWS = (2, 4, 8, 16)
POOL_GROUPS = 4
FNET_WIDTH = D_MIX // 4
FNET_HEADS = 4
MLA_HEADS = 8
QK_NOPE_DIM = 128
QK_ROPE_DIM = 64
QK_HEAD_DIM = QK_NOPE_DIM + QK_ROPE_DIM
V_HEAD_DIM = 128
MLA_WIDTH = MLA_HEADS * V_HEAD_DIM
Q_LORA_RANK = D_MODEL // 4
KV_LORA_RANK = D_MODEL // 4
N_FREQ_PER_AXIS = QK_ROPE_DIM // 4
ROPE_THETA = 10000.0
EPS = 1e-6
Q_BLOCK = 128
SM_SCALE = QK_HEAD_DIM ** -0.5

OFF_POOL = 0
OFF_POOL_GATE = OFF_POOL + POOL_WIDTH
OFF_FNET = OFF_POOL_GATE + POOL_WIDTH
OFF_FNET_GATE = OFF_FNET + FNET_WIDTH
OFF_CQ = OFF_FNET_GATE + FNET_WIDTH
OFF_CKV = OFF_CQ + Q_LORA_RANK
OFF_KROPE = OFF_CKV + KV_LORA_RANK
OFF_MLA_GATE = OFF_KROPE + QK_ROPE_DIM
D_IN = OFF_MLA_GATE + MLA_WIDTH

kernel_name = 'hybrid_pool_fnet_mla_diffusion_block'

def _rmsnorm(x, w):
    xf = x.astype(jnp.float32)
    y = xf * lax.rsqrt(jnp.mean(xf * xf, axis=-1, keepdims=True) + EPS)
    return (y * w.astype(jnp.float32)).astype(x.dtype)

def _rotate_half(x):
    x1, x2 = jnp.split(x, 2, axis=-1)
    return jnp.concatenate([-x2, x1], axis=-1)

def _axial_rope_tables(n_tokens):
    rows = n_tokens // GRID_W
    r, col = jnp.meshgrid(jnp.arange(rows, dtype=jnp.float32),
                          jnp.arange(GRID_W, dtype=jnp.float32), indexing='ij')
    inv_freq = ROPE_THETA ** (-jnp.arange(N_FREQ_PER_AXIS, dtype=jnp.float32) / N_FREQ_PER_AXIS)
    ang_r = r.reshape(-1)[:, None] * inv_freq
    ang_c = col.reshape(-1)[:, None] * inv_freq
    ang = jnp.concatenate([ang_r, ang_r, ang_c, ang_c], axis=-1)
    return jnp.cos(ang), jnp.sin(ang)

def _apply_axial_rope(x, cos, sin):
    half = QK_ROPE_DIM // 2
    xf = x.astype(jnp.float32)
    rot = jnp.concatenate([_rotate_half(xf[..., :half]), _rotate_half(xf[..., half:])], axis=-1)
    return (xf * cos[:, None, :] + rot * sin[:, None, :]).astype(x.dtype)

def _rope_tail(x, cos, sin):
    return jnp.concatenate([x[..., :QK_NOPE_DIM], _apply_axial_rope(x[..., QK_NOPE_DIM:], cos, sin)], axis=-1)

def _window_mean_minus_self(x, w):
    n = x.shape[1]
    lo = w // 2
    hi = w - lo - 1
    xf = x.astype(jnp.float32)
    csum = jnp.concatenate([jnp.zeros_like(xf[:, :1]), jnp.cumsum(xf, axis=1)], axis=1)
    t = jnp.arange(n)
    start = jnp.clip(t - lo, 0, n)
    end = jnp.clip(t + hi + 1, 0, n)
    count = (end - start).astype(jnp.float32)[None, :, None]
    return ((csum[:, end] - csum[:, start]) / count - xf).astype(x.dtype)

def _pool_mixer(u, pool_w, pool_scale):
    b, n, _ = u.shape
    g = u.reshape(b, n, POOL_GROUPS, POOL_WIDTH // POOL_GROUPS)
    pooled = jnp.stack([_window_mean_minus_self(g[:, :, i], w) for i, w in enumerate(POOL_WINDOWS)], axis=2)
    y = jnp.einsum('blgc,gcd->blgd', pooled, pool_w).reshape(b, n, POOL_WIDTH)
    return y * pool_scale

def _fourier_mixer(u, fnet_w):
    b, n, _ = u.shape
    g = u.reshape(b, n, FNET_HEADS, FNET_WIDTH // FNET_HEADS).astype(jnp.float32)
    f = jnp.fft.fft2(g, axes=(1, 3), norm='ortho').real.astype(u.dtype)
    return jnp.einsum('blgc,gcd->blgd', f, fnet_w).reshape(b, n, FNET_WIDTH)

def _mla_q(p, q_norm_w, w_uq, q_head_norm_w):
    cq = _rmsnorm(p[..., OFF_CQ:OFF_CKV], q_norm_w)
    q = cq @ w_uq
    q = q.reshape(q.shape[0], q.shape[1], MLA_HEADS, QK_HEAD_DIM)
    return _rmsnorm(q, q_head_norm_w)

def _mla_kv(kv_in, kv_norm_w, w_ukv, k_head_norm_w):
    b, n, _ = kv_in.shape
    ckv = _rmsnorm(kv_in[..., :KV_LORA_RANK], kv_norm_w)
    k_rope = kv_in[..., KV_LORA_RANK:]
    kv = (ckv @ w_ukv).reshape(b, n, MLA_HEADS, QK_NOPE_DIM + V_HEAD_DIM)
    k_nope, v = kv[..., :QK_NOPE_DIM], kv[..., QK_NOPE_DIM:]
    k = jnp.concatenate([k_nope, jnp.broadcast_to(k_rope[:, :, None, :], (b, n, MLA_HEADS, QK_ROPE_DIM))], axis=-1)
    return _rmsnorm(k, k_head_norm_w), v

def _softmax_attend(q, k, v):
    s = jnp.einsum('bqhd,bkhd->bhqk', q, k).astype(jnp.float32) * SM_SCALE
    p = jax.nn.softmax(s, axis=-1).astype(v.dtype)
    return jnp.einsum('bhqk,bkhd->bqhd', p, v)

def _attend_blocked(q, k, v):
    b, n, h, dq = q.shape
    nb = n // Q_BLOCK
    qb = q.reshape(b, nb, Q_BLOCK, h, dq).transpose(1, 0, 2, 3, 4)
    o = lax.map(lambda blk: _softmax_attend(blk, k, v), qb)
    return o.transpose(1, 0, 2, 3, 4).reshape(b, n, h * V_HEAD_DIM)

def _mixer_concat(p, mla_out, pool_w, pool_scale, fnet_w):
    a = jax.nn.silu(p[..., OFF_POOL_GATE:OFF_FNET]) * _pool_mixer(p[..., OFF_POOL:OFF_POOL_GATE], pool_w, pool_scale)
    f = jax.nn.silu(p[..., OFF_FNET_GATE:OFF_CQ]) * _fourier_mixer(p[..., OFF_FNET:OFF_FNET_GATE], fnet_w)
    m = jax.nn.silu(p[..., OFF_MLA_GATE:D_IN]) * mla_out
    return jnp.concatenate([a, f, m], axis=-1)

def _layer(x, ctx, c, c_ctx, norm_w, w_ada, b_ada, w_in, pool_w, pool_scale, fnet_w,
           q_norm_w, w_uq, kv_norm_w, w_ukv, q_head_norm_w, k_head_norm_w, w_out, ctx_out):
    shift, scale, gate = jnp.split(jax.nn.silu(c) @ w_ada + b_ada, 3, axis=-1)
    shift_c, scale_c, gate_c = jnp.split(jax.nn.silu(c_ctx) @ w_ada + b_ada, 3, axis=-1)
    h = _rmsnorm(x, norm_w) * (1.0 + scale[:, None, :]) + shift[:, None, :]
    hc = _rmsnorm(ctx, norm_w) * (1.0 + scale_c) + shift_c

    if ctx_out:
        pc = hc @ w_in
        kvc_in = pc[..., OFF_CKV:OFF_MLA_GATE]
    else:
        kvc_in = hc @ w_in[:, OFF_CKV:OFF_MLA_GATE]
    k_c, v_c = _mla_kv(kvc_in, kv_norm_w, w_ukv, k_head_norm_w)

    p = h @ w_in
    cos, sin = _axial_rope_tables(x.shape[1])
    q = _rope_tail(_mla_q(p, q_norm_w, w_uq, q_head_norm_w), cos, sin)
    k_l, v_l = _mla_kv(p[..., OFF_CKV:OFF_MLA_GATE], kv_norm_w, w_ukv, k_head_norm_w)
    k_l = _rope_tail(k_l, cos, sin)
    attn = _attend_blocked(q, jnp.concatenate([k_c, k_l], axis=1), jnp.concatenate([v_c, v_l], axis=1))
    y = _mixer_concat(p, attn, pool_w, pool_scale, fnet_w) @ w_out
    x = x + gate[:, None, :] * y

    if ctx_out:
        q_c = _mla_q(pc, q_norm_w, w_uq, q_head_norm_w)
        attn_c = _softmax_attend(q_c, k_c, v_c).reshape(ctx.shape[0], ctx.shape[1], MLA_WIDTH)
        yc = _mixer_concat(pc, attn_c, pool_w, pool_scale, fnet_w) @ w_out
        ctx = ctx + gate_c * yc
    return x, ctx

def setup_inputs(seed: int = 0) -> dict:
    key = jax.random.key(seed)
    ks = jax.random.split(key, 20)
    f32 = jnp.float32
    nrm = lambda k, shape, s: jax.random.normal(k, shape, f32) * s
    gpc = POOL_WIDTH // POOL_GROUPS
    gfc = FNET_WIDTH // FNET_HEADS
    return {
        'x': nrm(ks[0], (BATCH, SEQ, D_MODEL), 1.0),
        'c': nrm(ks[1], (BATCH, D_MODEL), 1.0),
        'ctx': nrm(ks[2], (BATCH, CTX_LEN, D_MODEL), 1.0),
        'c_ctx': nrm(ks[3], (D_MODEL,), 1.0),
        'norm_w': 1.0 + nrm(ks[4], (DEPTH, D_MODEL), 0.02),
        'w_ada': nrm(ks[5], (DEPTH, D_MODEL, 3 * D_MODEL), 0.5 * D_MODEL ** -0.5),
        'b_ada': nrm(ks[6], (DEPTH, 3 * D_MODEL), 0.02),
        'w_in': nrm(ks[7], (DEPTH, D_MODEL, D_IN), D_MODEL ** -0.5),
        'pool_w': nrm(ks[8], (DEPTH, POOL_GROUPS, gpc, gpc), gpc ** -0.5),
        'pool_scale': 1.0 + nrm(ks[9], (DEPTH, POOL_WIDTH), 0.1),
        'fnet_w': nrm(ks[10], (DEPTH, FNET_HEADS, gfc, gfc), gfc ** -0.5),
        'q_norm_w': 1.0 + nrm(ks[11], (DEPTH, Q_LORA_RANK), 0.02),
        'w_uq': nrm(ks[12], (DEPTH, Q_LORA_RANK, MLA_HEADS * QK_HEAD_DIM), Q_LORA_RANK ** -0.5),
        'kv_norm_w': 1.0 + nrm(ks[13], (DEPTH, KV_LORA_RANK), 0.02),
        'w_ukv': nrm(ks[14], (DEPTH, KV_LORA_RANK, MLA_HEADS * (QK_NOPE_DIM + V_HEAD_DIM)), KV_LORA_RANK ** -0.5),
        'q_head_norm_w': 1.0 + nrm(ks[15], (DEPTH, QK_HEAD_DIM), 0.02),
        'k_head_norm_w': 1.0 + nrm(ks[16], (DEPTH, QK_HEAD_DIM), 0.02),
        'w_out': nrm(ks[17], (DEPTH, D_MIX, D_MODEL), D_MIX ** -0.5),
    }

def reference(x, c, ctx, c_ctx, norm_w, w_ada, b_ada, w_in, pool_w, pool_scale, fnet_w,
              q_norm_w, w_uq, kv_norm_w, w_ukv, q_head_norm_w, k_head_norm_w, w_out):
    for i in range(DEPTH):
        x, ctx = _layer(x, ctx, c, c_ctx, norm_w[i], w_ada[i], b_ada[i], w_in[i], pool_w[i], pool_scale[i],
                        fnet_w[i], q_norm_w[i], w_uq[i], kv_norm_w[i], w_ukv[i], q_head_norm_w[i],
                        k_head_norm_w[i], w_out[i], i < DEPTH - 1)
    return x


_drawn_inputs = setup_inputs


def setup_inputs(seed=0):
    import zlib

    import numpy as np

    out = dict(_drawn_inputs(seed))
    spreads = {}
    factors = {'ctx': 8.0,
     'c_ctx': 3.013,
     'norm_w': 8.0,
     'b_ada': 4.193,
     'pool_scale': 4.31,
     'q_norm_w': 8.0,
     'w_uq': 4.451,
     'kv_norm_w': 8.0,
     'q_head_norm_w': 8.0,
     'k_head_norm_w': 8.0}
    for name, (base, spread) in spreads.items():
        noise = np.random.default_rng([zlib.crc32(name.encode()), seed]).standard_normal(out[name].shape)
        drawn = base * np.exp(spread * noise) if base else spread * noise
        out[name] = __import__('jax').numpy.asarray(drawn.astype(out[name].dtype))
    for name, factor in factors.items():
        out[name] = (out[name] * factor).astype(out[name].dtype)
    return out
```

```python
from contextlib import ExitStack

import numpy as np

import concourse.bass as bass
from concourse import mybir

F32 = mybir.dt.float32
ALU = mybir.AluOpType
ACT = mybir.ActivationFunctionType
AX_X = mybir.AxisListType.X

P = 128
D_MODEL = 2048
SEQ = 512
CTX = 256
TOK = SEQ + CTX
DEPTH = 2
KT = D_MODEL // P
GRID_W = 64
GROUPS = 4
HEADS = 8
NOPE = 128
ROPE = 64
HEAD = NOPE + ROPE
VDIM = 128
RANK = 512
RT = RANK // P
EPS = 1e-6
SM_SCALE = HEAD ** -0.5
TT = TOK // P
LT = SEQ // P
SLOT_N = 256

COL_POOL, COL_POOL_GATE, COL_FNET, COL_FNET_GATE = 0, 512, 1024, 1536
COL_CQ, COL_CKV, COL_KROPE, COL_MLA_GATE = 2048, 2560, 3072, 3136

PR_ADA, PR_NORM, PR_POOL, PR_QN, PR_KVN = 0, 48, 64, 68, 72
PR_QH, PR_QHR, PR_KH, PR_KHR, PR_N = 76, 77, 78, 79, 80

T_GATE, T_POOL, T_FNET, T_CQ, T_CKV, T_KROPE, T_MLA = 0, 8, 12, 16, 20, 24, 25
MM_IN = 33


class Link:

    def __init__(self, engine, sem, base=0):
        self.engine, self.sem, self.base, self.n = engine, sem, base, 0

    def __call__(self, ins):
        self.n += 1
        ins.then_inc(self.sem, 1)
        self.engine.wait_ge(self.sem, self.base + self.n)


def build(nc, x, c, ctx, c_ctx, norm_w, w_ada, b_ada, w_in, pool_w, pool_scale, fnet_w, q_norm_w,
          w_uq, kv_norm_w, w_ukv, q_head_norm_w, k_head_norm_w, w_out,
          k_ident, k_sel, k_dup, k_rope, k_chan, k_pos_lat, k_pos_ctx, k_inv, out):
    xt_dram = [nc.dram_tensor(f"xt{l}", (D_MODEL, TOK if l == 0 else SEQ), F32, kind="Internal").ap()
               for l in range(DEPTH)]

    with ExitStack() as stack:
        def sb(name, n):
            return stack.enter_context(nc.sbuf_tensor(name, [P, n], F32))

        def sem(name):
            return stack.enter_context(nc.semaphore(name))

        def per_layer(name):
            return [sem(f"{name}{l}") for l in range(DEPTH)]

        def pair(name):
            return [[sem(f"{name}{l}_{b}") for b in range(2)] for l in range(DEPTH)]

        H_ = sb("h_region", KT * TOK)
        G_ = sb("g_region", KT * TOK)
        W_ = sb("w_region", 2 * KT * SLOT_N)
        C_ = sb("c_region", (2 * RT + 1) * TOK)
        F_ = sb("f_region", 10496)

        def view(region, at, n, k=None):
            v = region[:, at:at + n]
            return v if k is None else v.rearrange("p (k n) -> p k n", k=k)

        h = view(H_, 0, KT * TOK, KT)
        mix = view(G_, 0, KT * TOK, KT)
        w_slot = [view(W_, b * KT * SLOT_N, KT * SLOT_N, KT) for b in range(2)]
        cq = view(C_, 0, RT * TOK, RT)
        ckv = view(C_, RT * TOK, RT * TOK, RT)
        ckk = view(C_, 0, 2 * RT * TOK, 2 * RT)
        kr = view(C_, 2 * RT * TOK, TOK)
        inv = view(C_, 0, GROUPS * TOK, GROUPS)
        PAD = 8
        PW = PAD + SEQ + 2 * PAD + CTX + PAD
        LAT0, CTX0 = PAD, PAD + SEQ + 2 * PAD
        pad_u = view(C_, 3072, PW)
        win = [view(C_, 3072 + PW, PW), view(C_, 3072 + 2 * PW, PW)]
        pooled = view(C_, 3072 + 3 * PW, TOK)
        x_nat = [view(F_, 6400 + b * D_MODEL, D_MODEL) for b in range(2)]
        ada_row = [view(F_, b * 512, 512) for b in range(2)]
        cond = view(F_, 1024, KT * 32, KT)
        ada_slot = [view(W_, 0, 4096, 8), view(W_, 4096, 4096, 8), view(G_, 0, 4096, 8), view(G_, 4096, 4096, 8)]
        xt = [view(F_, b * TOK, TOK) for b in range(4)]
        sq = view(F_, 3072, TOK)
        sq_t = [view(F_, 3840 + b * TOK, TOK) for b in range(2)]
        n_diag = view(F_, 5376, TOK)
        o_nat = [view(F_, 5376, LT * P, LT), view(F_, 7424, LT * P, LT)]
        x_out = [view(F_, 9472 + b * SEQ, SEQ) for b in range(2)]
        pos_lat = view(F_, 0, 2 * LT * SEQ).rearrange("p (s k n) -> p s k n", s=2, k=LT)
        pos_ctx = view(F_, 4096, 2 * 2 * CTX).rearrange("p (s k n) -> p s k n", s=2, k=2)
        chan = view(F_, 5120, 256)
        chan_w = view(F_, 5376, GROUPS * 256, GROUPS)
        f_u = [view(F_, 6400 + b * TOK, TOK) for b in range(2)]
        f_ab = view(F_, 7936, TT * 256, TT)
        fw = view(F_, 9472, GROUPS * P)
        pw = view(F_, 9984, GROUPS * P, GROUPS)
        kr_w = view(F_, 0, KT * P, KT)
        prob = [view(F_, b * TOK, TOK) for b in range(2)]
        prob_t = view(F_, 1536, TT * SEQ, TT)
        prob_tc = view(F_, 4608, 2 * CTX, 2)
        sq_q, sq_k, sq_r = view(F_, 5120, TOK), view(F_, 5888, TOK), view(F_, 6656, TOK)
        diag = view(F_, 7424, TOK)
        kr_sq = view(F_, 8192, TOK)
        vh = [view(F_, 8960 + b * TOK, TOK, TT) for b in range(2)]
        u_kr = prob[0]
        sq_c = [prob[1], sq_r]
        q_diag = view(F_, 1536, TOK)
        v_all = view(H_, 0, TT * HEADS * VDIM, TT)
        qn, qr, kn, krh = ([view(H_, 6144 + (4 * b + j) * TOK, TOK) for b in range(2)] for j in range(4))
        v_w = view(W_, 0, 4096, RT)
        wq = [view(W_, 4096 + b * 1536, 1024, RT) for b in range(2)]
        wk = [view(W_, 4096 + b * 1536 + 1024, 512, RT) for b in range(2)]

        ident, dup, ones = sb("ident", P), sb("dup", P), sb("ones", P)
        sel = sb("sel", 2)
        rope = sb("rope", TOK)
        c_in = sb("c_in", 2 * KT)
        par_row = [sb(f"par_row{l}", P) for l in range(DEPTH)]
        par = [sb(f"par{l}", PR_N) for l in range(DEPTH)]
        ada = [sb(f"ada{l}", 2 * 48) for l in range(DEPTH)]
        gain = [sb(f"gain{l}", 2 * KT) for l in range(DEPTH)]
        eps = sb("eps", 1)
        root, inv_root = sb("root", 12), sb("inv_root", 12)
        h_root = [sb(f"h_root{b}", 12) for b in range(2)]
        h_inv = [sb(f"h_inv{b}", 12) for b in range(2)]
        q_pos = [sb(f"q_pos{b}", 6) for b in range(2)]
        q_neg = [sb(f"q_neg{b}", 6) for b in range(2)]
        top, bias, total, inv_total = sb("top", 6), sb("bias", 6), sb("total", 6), sb("inv_total", 6)
        ada_v = [a[:, :].rearrange("p (t j) -> p t j", t=2) for a in ada]
        gain_v = [g[:, :].rearrange("p (t j) -> p t j", t=2) for g in gain]

        ps = [stack.enter_context(nc.psum_tensor(f"ps{i}", [P, 1024], F32)) for i in range(4)]
        A, B, C, D = ps

        def bank(i):
            return ps[i // 2][:, (i % 2) * 512:(i % 2) * 512 + 512]

        s_const, s_par, s_zero, s_cond = sem("s_const"), sem("s_par"), sem("s_zero"), sem("s_cond")
        s_xn = [sem(f"s_xn{b}") for b in range(2)]
        s_part, s_parc = sem("s_part"), sem("s_parc")
        s_xt, s_xt_dve, s_xt_act = sem("s_xt"), sem("s_xt_dve"), sem("s_xt_act")
        s_adw = [sem(f"s_adw{b}") for b in range(4)]
        s_ada_mm, s_ada_row, s_ada_col, s_ada_b = sem("s_ada_mm"), sem("s_ada_row"), sem("s_ada_col"), sem("s_ada_b")
        s_gain = sem("s_gain")
        s_spill = sem("s_spill")
        s_link = sem("s_link")
        s_sqt, s_sqa = per_layer("s_sqt"), per_layer("s_sqa")
        s_h = per_layer("s_h")
        s_ncol, s_nroot, s_ndiag, s_nrb, s_hx = map(sem, ("s_ncol", "s_nroot", "s_ndiag", "s_nrb", "s_hx"))
        s_w, s_mm, s_ev = pair("s_w"), per_layer("s_mm"), pair("s_ev")
        s_tab, s_inv = per_layer("s_tab"), sem("s_inv")
        s_pl, s_pmm, s_pg = per_layer("s_pl"), sem("s_pmm"), sem("s_pg")
        s_cw, s_cwc, s_fch, s_fpos, s_fg = map(sem, ("s_cw", "s_cwc", "s_fch", "s_fpos", "s_fg"))
        s_fab = per_layer("s_fab")
        s_kw, s_kws, s_ukr, s_krsq = map(sem, ("s_kw", "s_kws", "s_ukr", "s_krsq"))
        s_csq, s_csa, s_ccol, s_croot, s_crb, s_cn = map(sem, ("s_csq", "s_csa", "s_ccol", "s_croot", "s_crb", "s_cn"))
        s_cdiag = per_layer("s_cdiag")
        s_krm, s_kr, s_vmm, s_v = map(sem, ("s_krm", "s_kr", "s_vmm", "s_v"))
        s_wh = pair("s_wh")
        s_sw, s_vh = per_layer("s_sw"), per_layer("s_vh")
        s_pqn, s_pqr, s_pkn, s_eqn, s_eqr, s_esr, s_ekn, s_addq, s_addk = map(
            per_layer, ("s_pqn", "s_pqr", "s_pkn", "s_eqn", "s_eqr", "s_esr", "s_ekn", "s_addq", "s_addk"))
        s_col, s_root, s_qs, s_diag, s_rb, s_kn = map(
            per_layer, ("s_col", "s_root", "s_qs", "s_diag", "s_rb", "s_kn"))
        s_s, s_nb, s_exp, s_sc, s_t, s_pt, s_pv, s_om = map(
            per_layer, ("s_s", "s_nb", "s_exp", "s_sc", "s_t", "s_pt", "s_pv", "s_om"))
        s_xin = [sem(f"s_xin{l}_{b}") for l in range(DEPTH) for b in range(4)]
        s_cmm, s_xnew = per_layer("s_cmm"), sem("s_xnew")
        s_cev, s_own = pair("s_cev"), per_layer("s_own")
        s_xst, s_otr, s_oev = sem("s_xst"), sem("s_otr"), sem("s_oev")
        s_out = [sem(f"s_out{b}") for b in range(2)]

        N_CONST = 6
        N_PAR = 2 * (5 + 2 * 6)

        def q_tok(l):
            return TOK if l < DEPTH - 1 else SEQ

        def q_tiles(l):
            return q_tok(l) // P

        def parts(n):
            return [(a, min(n - a, 512)) for a in range(0, n, 512)]

        block = stack.enter_context(nc.Block())

        @block.sync
        def _(sp):
            for dst, src in ((ident[:, :], k_ident), (dup[:, :], k_dup), (sel[:, :], k_sel), (rope[:, :], k_rope),
                             (c_in[:, 0:KT], c.rearrange("a (p k) -> (a p) k", k=KT)),
                             (c_in[:, KT:2 * KT], c_ctx.rearrange("(p k) -> p k", k=KT))):
                sp.dma_start(dst, src).then_inc(s_const, 16)
            for t in range(TT):
                if t >= 2:
                    sp.wait_ge(s_xt, 4 * (t - 1))
                src = x[0, t * P:(t + 1) * P, :] if t < LT else ctx[0, (t - LT) * P:(t - LT + 1) * P, :]
                sp.dma_start(x_nat[t % 2], src).then_inc(s_xn[t % 2], 16)

            def ada_load(l, i, s):
                src = w_ada[l].rearrange("(p k) n -> p k n", k=KT)
                sp.dma_start(ada_slot[s], src[:, (s % 2) * 8:(s % 2) * 8 + 8, bass.ds((2 * i + s // 2) * 512, 512)])\
                  .then_inc(s_adw[s], 16)

            for s in range(4):
                ada_load(0, 0, s)
            for l in range(DEPTH):
                with sp.Fori(1 - l, 6) as i:
                    for s in range(4):
                        sp.wait_ge(s_ada_mm, 24 * l + 4 * i + s - 3)
                        ada_load(l, i, s)

            for l in range(DEPTH):
                src = w_in[l].rearrange("(k p) n -> p k n", p=P)

                def load_in(m, col, done, b):
                    if m >= 2:
                        sp.wait_ge(s_mm[l], done)
                    sp.dma_start(w_slot[b], src[:, :, bass.ds(col, SLOT_N)]).then_inc(s_w[l][b], 16)

                if l == 0:
                    sp.wait_ge(s_ada_mm, 24 * DEPTH)
                else:
                    sp.wait_ge(s_cmm[l - 1], KT - 2)
                load_in(0, COL_POOL_GATE, 0, 0)
                if l > 0:
                    sp.wait_ge(s_cmm[l - 1], KT)
                load_in(1, COL_POOL_GATE + SLOT_N, 0, 1)
                load_in(2, COL_FNET_GATE, 2, 0)
                load_in(3, COL_FNET_GATE + SLOT_N, 4, 1)
                for m, col in ((4, COL_POOL), (6, COL_FNET), (8, COL_CQ), (10, COL_CKV)):
                    load_in(m, col, 2 * m - 2, 0)
                    load_in(m + 1, col + SLOT_N, 2 * m, 1)
                sp.wait_ge(s_fpos, (l + 1) * GROUPS)
                sp.dma_start(kr_w[:, :, 0:ROPE], src[:, :, COL_KROPE:COL_KROPE + ROPE]).then_inc(s_kw, 16)
                for j, done in enumerate((22, 24, 27, 29)):
                    load_in(12 + j, COL_MLA_GATE + j * SLOT_N, done, j % 2)
                sp.wait_ge(s_mm[l], 31)
                for k in range(RT):
                    src_v = w_ukv[l, k * P:(k + 1) * P, :].rearrange("p (h n) -> p h n", h=HEADS)[:, :, NOPE:]
                    sp.dma_start(v_w[:, k, :].rearrange("p (h n) -> p h n", h=HEADS), src_v).then_inc(s_w[l][0], 16)

                def head_load(hd, b):
                    sp.dma_start(wq[b][:, :, 0:HEAD],
                                 w_uq[l].rearrange("(k p) n -> p k n", p=P)[:, :, bass.ds(hd * HEAD, HEAD)]).then_inc(s_wh[l][b], 16)
                    sp.dma_start(wk[b],
                                 w_ukv[l].rearrange("(k p) n -> p k n", p=P)[:, :, bass.ds(hd * (NOPE + VDIM), NOPE)])\
                      .then_inc(s_wh[l][b], 16)

                sp.wait_ge(s_mm[l], MM_IN)
                for b in range(2):
                    head_load(b, b)
                with sp.Fori(1, HEADS // 2) as i:
                    for b in range(2):
                        sp.wait_ge(s_pkn[l], 2 * i + b - 1)
                        head_load(2 * i + b, b)
                src_o = w_out[l].rearrange("(k p) n -> p k n", p=P)
                sp.wait_ge(s_vmm, (l + 1) * TT)
                sp.dma_start(w_slot[0], src_o[:, :, 0:SLOT_N]).then_inc(s_w[l][0], 16)
                sp.wait_ge(s_pkn[l], HEADS)
                sp.dma_start(w_slot[1], src_o[:, :, SLOT_N:2 * SLOT_N]).then_inc(s_w[l][1], 16)
                with sp.Fori(1, 4) as i:
                    for b in range(2):
                        sp.wait_ge(s_cmm[l], 4 * i + 2 * b - 2)
                        sp.dma_start(w_slot[b], src_o[:, :, bass.ds((2 * i + b) * SLOT_N, SLOT_N)]).then_inc(s_w[l][b], 16)

        @block.gpsimd
        def _(pool):
            for l in range(DEPTH):
                row = par_row[l]

                def load(r, n, src):
                    pool.dma_start(row[r:r + n, :], src.rearrange("(r n) -> r n", n=P)).then_inc(s_par, 16)

                load(PR_ADA, 48, b_ada[l])
                load(PR_NORM, KT, norm_w[l])
                load(PR_POOL, GROUPS, pool_scale[l])
                load(PR_QN, RT, q_norm_w[l])
                load(PR_KVN, RT, kv_norm_w[l])
                for r, src in ((PR_QH, q_head_norm_w[l]), (PR_KH, k_head_norm_w[l])):
                    load(r, 1, src[0:NOPE])
                    pool.dma_start(row[r + 1:r + 2, 0:ROPE], src[NOPE:HEAD].rearrange("(r n) -> r n", r=1)).then_inc(s_par, 16)
                    for q in range(4):
                        a = NOPE + 16 * (q ^ 1)
                        pool.dma_start(row[r + 1:r + 2, ROPE + 16 * q:ROPE + 16 * q + 16],
                                       src[a:a + 16].rearrange("(r n) -> r n", r=1)).then_inc(s_par, 16)
            pool.wait_ge(s_xt_dve, 2 * TT)
            pool.wait_ge(s_xt_act, 2 * TT)
            pool.dma_start(xt_dram[0].rearrange("(k p) t -> p k t", p=P), h).then_inc(s_spill, 16)

            for l in range(DEPTH):
                pool.wait_ge(s_nrb, l + 1)
                if l > 0:
                    pool.wait_ge(s_om[l - 1], HEADS)
                pool.dma_start(inv, k_inv.rearrange("p (g t) -> p g t", g=GROUPS)).then_inc(s_inv, 16)
                pool.dma_start(pw, pool_w[l].rearrange("g c d -> c g d")).then_inc(s_inv, 16)
                pool.dma_start(fw.rearrange("p (g d) -> p g d", g=GROUPS), fnet_w[l].rearrange("g c d -> c g d")).then_inc(s_tab[l], 16)
                pool.dma_start(chan, k_chan).then_inc(s_tab[l], 16)
                for s in range(2):
                    pool.dma_start(pos_lat[:, s], k_pos_lat[s].rearrange("(k p) n -> p k n", p=P)).then_inc(s_tab[l], 16)
                    if l < DEPTH - 1:
                        pool.dma_start(pos_ctx[:, s], k_pos_ctx[s].rearrange("(k p) n -> p k n", p=P)).then_inc(s_tab[l], 16)

                def swap(dst, src, s):
                    d = dst.rearrange("p k (a b c) -> p k a b c", a=2, b=2)
                    o = src.rearrange("p k (a b c) -> p k a b c", a=2, b=2)
                    for b in range(2):
                        nc.gpsimd.tensor_copy(d[:, :, :, b], o[:, :, :, 1 - b]).then_inc(s, 1)

                pool.wait_ge(s_kw, (l + 1) * 16)
                swap(kr_w[:, :, ROPE:P], kr_w[:, :, 0:ROPE], s_kws)

                for hd in range(HEADS):
                    b = hd % 2
                    pool.wait_ge(s_wh[l][b], 32 * (hd // 2) + 32)
                    swap(wq[b][:, :, HEAD:HEAD + ROPE], wq[b][:, :, NOPE:HEAD], s_sw[l])
                    if hd == 0:
                        pool.wait_ge(s_v, (l + 1) * TT)
                    if hd >= 2:
                        pool.wait_ge(s_pv[l], hd - 1)
                    nc.gpsimd.tensor_copy(vh[b], v_all[:, :, hd * VDIM:(hd + 1) * VDIM]).then_inc(s_vh[l], 1)

                nt = q_tok(l)
                if l == 0:
                    pool.wait_ge(s_spill, 16)
                else:
                    pool.wait_ge(s_xst, 16 * KT)
                pool.wait_ge(s_pv[l], HEADS)
                for b in range(4):
                    pool.dma_start(xt[b][:, 0:nt], xt_dram[l][b * P:(b + 1) * P, 0:nt]).then_inc(s_xin[4 * l + b], 16)

                def tile_out(i, b, load_next):
                    n = 4 * i + b
                    if l == 0:
                        pool.wait_ge(s_xnew, n + 1)
                        pool.dma_start(xt_dram[1][bass.ds(n * P, P), :],
                                       h[:, bass.ds(n, 1), 0:SEQ].rearrange("p a t -> p (a t)")).then_inc(s_xst, 16)
                    if load_next:
                        pool.wait_ge(s_cev[l][b % 2], 2 * i + b // 2 + 1)
                        pool.dma_start(xt[b][:, 0:nt], xt_dram[l][bass.ds(n * P + 4 * P, P), 0:nt])\
                            .then_inc(s_xin[4 * l + b], 16)
                    if l == 1:
                        pool.wait_ge(s_oev, n + 1)
                        pool.dma_start(out[0].rearrange("(t p) n -> p t n", p=P)[:, :, bass.ds(n * P, P)],
                                       o_nat[b % 2]).then_inc(s_out[b % 2], 16)

                with pool.Fori(0, 3) as i:
                    for b in range(4):
                        tile_out(i, b, True)
                for b in range(4):
                    tile_out(3, b, False)
            for b in range(2):
                pool.wait_ge(s_out[b], 16 * KT // 2)

        @block.scalar
        def _(act):
            def copy(o, i):
                return nc.scalar.activation(o, i, ACT.Copy)

            def square(o, i):
                return nc.scalar.activation(o, i, ACT.Square)

            act.wait_ge(s_zero, 3)
            act.wait_ge(s_const, 16 * N_CONST)
            for t in range(2):
                nc.scalar.activation(cond[:, :, t], c_in[:, t * KT:(t + 1) * KT], ACT.Silu).then_inc(s_cond, 1)
            with act.Fori(0, TT // 2) as i:
                for g in range(1, 8, 2):
                    act.wait_ge(s_xt, 8 * i + g + 1)
                    copy(h[:, 4 * (g % 4):4 * (g % 4) + 4, bass.ds((2 * i + g // 4) * P, P)],
                         bank(g % 4).rearrange("p (k t) -> p k t", k=4)).then_inc(s_xt_act, 1)
            act.wait_ge(s_xt_dve, 2 * TT)
            act.wait_ge(s_xt_act, 2 * TT)
            with act.Fori(0, KT // 2) as i:
                for b in range(2):
                    act.wait_ge(s_sqa[0], 2 * i)
                    square(sq_t[b], h[:, bass.ds(2 * i + b, 1), :].rearrange("p a t -> p (a t)")).then_inc(s_sqt[0], 1)
            with act.Fori(0, 12) as i:
                for b in range(2):
                    act.wait_ge(s_ada_mm, 4 * i + 2 * b + 2)
                    act.wait_ge(s_ada_col, 2 * i)
                    copy(ada_row[b], C[:, b * 512:(b + 1) * 512]).then_inc(s_ada_row, 1)

            for l in range(DEPTH):
                nq = q_tok(l)
                qt_n = q_tiles(l)
                act.wait_ge(s_ncol, l + 1)
                nc.scalar.activation(root[:, 0:TT], A[:, 0:TT], ACT.Sqrt, bias=eps[:, 0:1], scale=1.0 / D_MODEL).then_inc(s_nroot, 1)
                act.wait_ge(s_gain, 2 * (l + 1))
                for k in range(KT):
                    act.wait_ge(s_hx, KT * l + k + 1)
                    for t, (a, n) in enumerate(((0, SEQ), (SEQ, CTX))):
                        nc.scalar.activation(h[:, k, a:a + n], h[:, k, a:a + n], ACT.Identity,
                                             bias=ada[l][:, t * 48 + k:t * 48 + k + 1],
                                             scale=gain[l][:, t * KT + k:t * KT + k + 1]).then_inc(s_h[l], 1)

                with act.Fori(0, 2) as i:
                    for j in range(4):
                        act.wait_ge(s_mm[l], 4 * i + j + 1)
                        nc.scalar.activation(mix[:, bass.ds(4 * i + j, 1), 0:nq].rearrange("p a t -> p (a t)"),
                                             ps[j % 2][:, 0:nq], ACT.Silu).then_inc(s_ev[l][j % 2], 1)
                act.wait_ge(s_cw, l + 1)
                for s in range(2):
                    copy(chan_w[:, :, s * P:(s + 1) * P], C[:, s * 512:(s + 1) * 512].rearrange("p (g d) -> p g d", g=GROUPS))\
                        .then_inc(s_cwc, 1)

                def fourier_ab(g):
                    act.wait_ge(s_fch, GROUPS * l + g + 1)
                    act.wait_ge(s_fpos, GROUPS * l + g)
                    copy(f_ab[:, 0:4, :], C[:, :].rearrange("p (t n) -> p t n", t=4)).then_inc(s_fab[l], 1)
                    if l == 0:
                        copy(f_ab[:, 4:6, :], D[:, 0:512].rearrange("p (t n) -> p t n", t=2)).then_inc(s_fab[l], 1)

                for j in range(GROUPS):
                    act.wait_ge(s_mm[l], T_FNET + j + 1)
                    if j >= 2:
                        act.wait_ge(s_fch, GROUPS * l + j - 1)
                    copy(f_u[j % 2][:, 0:nq], ps[j % 2][:, 0:nq]).then_inc(s_ev[l][j % 2], 1)
                    if j >= 1:
                        fourier_ab(j - 1)
                act.wait_ge(s_pmm, (l + 1) * GROUPS)
                for j in range(2 * RT):
                    n = nq if j < RT else TOK
                    act.wait_ge(s_mm[l], T_CQ + j + 1)
                    copy(ckk[:, j, 0:n], ps[j % 2][:, 0:n]).then_inc(s_ev[l][j % 2], 1)
                    if j == 0:
                        fourier_ab(GROUPS - 1)
                act.wait_ge(s_mm[l], T_KROPE + 1)
                act.wait_ge(s_ukr, l + 1)
                square(kr_sq[0:ROPE, :], A[0:ROPE, 0:TOK]).then_inc(s_krsq, 1)
                act.wait_ge(s_ev[l][0], T_KROPE // 2)
                act.wait_ge(s_ev[l][1], T_KROPE // 2)
                n_tmp = 0
                for j in range(2 * RT):
                    n = nq if j < RT else TOK
                    if j % RT == 0:
                        dst = (sq_q, sq_k)[j // RT]
                    else:
                        if n_tmp >= 2:
                            act.wait_ge(s_csa, 2 * (RT - 1) * l + n_tmp - 1)
                        dst = sq_c[n_tmp % 2]
                        n_tmp += 1
                    square(dst[:, 0:n], ckk[:, j, 0:n]).then_inc(s_csq, 1)

                def gate(n):
                    act.wait_ge(s_mm[l], n + 1)
                    nc.scalar.activation(mix[:, 2 * GROUPS + n - T_MLA, 0:nq], ps[n % 2][:, 0:nq], ACT.Silu).then_inc(s_ev[l][n % 2], 1)

                gate(T_MLA)
                gate(T_MLA + 1)
                act.wait_ge(s_ccol, l + 1)
                nc.scalar.activation(root[:, TT - qt_n:2 * TT], D[:, TT - qt_n:2 * TT], ACT.Sqrt,
                                     bias=eps[:, 0:1], scale=1.0 / RANK).then_inc(s_croot, 1)
                for n in range(T_MLA + 2, MM_IN):
                    gate(n)
                act.wait_ge(s_krm, l + 1)
                copy(kr, A[:, 0:TOK]).then_inc(s_kr, 1)
                for t in range(TT):
                    act.wait_ge(s_vmm, TT * l + t + 1)
                    copy(v_all[:, t, :], (B, A)[t % 2][:, :]).then_inc(s_v, 1)

                def queries(p, b):
                    act.wait_ge(s_pqn[l], p + 1)
                    nc.scalar.activation(qn[b][:, 0:nq], C[:, 0:nq], ACT.Identity, scale=par[l][:, PR_QH:PR_QH + 1]).then_inc(s_eqn[l], 1)
                    square(sq_q[:, 0:nq], C[:, 0:nq]).then_inc(s_eqn[l], 1)

                def rotary_squares(p):
                    act.wait_ge(s_eqr[l], p + 1)
                    square(sq_r[0:ROPE, 0:nq], C[0:ROPE, 0:nq]).then_inc(s_esr[l], 1)

                def keys(p, b):
                    act.wait_ge(s_pkn[l], p + 1)
                    nc.scalar.activation(kn[b], C[:, 0:TOK], ACT.Identity, scale=par[l][:, PR_KH:PR_KH + 1]).then_inc(s_ekn[l], 1)
                    square(sq_k, C[:, 0:TOK]).then_inc(s_ekn[l], 1)

                def roots(p, b):
                    act.wait_ge(s_col[l], p + 1)
                    nc.scalar.activation(h_root[b][:, TT - qt_n:2 * TT], C[:, TT - qt_n:2 * TT], ACT.Sqrt,
                                         bias=eps[:, 0:1], scale=1.0 / HEAD).then_inc(s_root[l], 1)

                def attend(hd, b, proj):
                    p, pb = hd + 1, 1 - b

                    def exp(q):
                        lo = 0 if q < LT else SEQ
                        n = TOK if q < LT else CTX
                        act.wait_ge(s_nb[l], hd * qt_n + q + 1)
                        act.wait_ge(s_t[l], hd * qt_n + max(q - 1, 0))
                        nc.scalar.activation(prob[q % 2][:, 0:n], ps[q % 2][:, 0:n], ACT.Exp, bias=bias[:, q:q + 1],
                                             scale=q_pos[b][:, q:q + 1], accum_out=total[:, q:q + 1]).then_inc(s_exp[l], 1)

                    def turned(q):
                        act.wait_ge(s_t[l], hd * qt_n + q + 1)
                        if q < LT:
                            act.wait_ge(s_pv[l], hd)
                            copy(prob_t[:, :, q * P:(q + 1) * P], D[:, 0:TOK].rearrange("p (k q) -> p k q", k=TT)).then_inc(s_pt[l], 1)
                        else:
                            q -= LT
                            copy(prob_tc[:, :, q * P:(q + 1) * P], D[:, 0:CTX].rearrange("p (k q) -> p k q", k=2)).then_inc(s_pt[l], 1)

                    if proj:
                        queries(p, pb)
                    act.wait_ge(s_qs[l], 2 * hd + 2)
                    exp(0)
                    exp(1)
                    if proj:
                        rotary_squares(p)
                    turned(0)
                    exp(2)
                    turned(1)
                    if proj:
                        keys(p, pb)
                    exp(3)
                    turned(2)
                    for q in range(LT, qt_n):
                        exp(q)
                    for q in range(3, qt_n):
                        turned(q)
                    if proj:
                        roots(p, pb)

                queries(0, 0)
                rotary_squares(0)
                keys(0, 0)
                roots(0, 0)
                with act.Fori(0, HEADS // 2 - 1) as i:
                    for b in range(2):
                        attend(2 * i + b, b, True)
                attend(HEADS - 2, 0, True)
                attend(HEADS - 1, 1, False)

                if l == 0:
                    with act.Fori(0, 4) as i:
                        for j in range(4):
                            n = 4 * i + j
                            act.wait_ge(s_cev[l][j % 2], 2 * i + j // 2 + 1)
                            act.wait_ge(s_xnew, n + 1)
                            act.wait_ge(s_sqa[1], 4 * i + max(j - 1, 0))
                            square(sq_t[j % 2], h[:, bass.ds(n, 1), :].rearrange("p a t -> p (a t)")).then_inc(s_sqt[1], 1)
                else:
                    with act.Fori(0, 4) as i:
                        for j in range(4):
                            n = 4 * i + j
                            act.wait_ge(s_otr, n + 1)
                            act.wait_ge(s_out[j % 2], 32 * i + 16 * (j // 2))
                            copy(o_nat[j % 2], (C, D)[j % 2][:, 0:512].rearrange("p (t n) -> p t n", t=LT)).then_inc(s_oev, 1)

        @block.vector
        def _(dve):
            link = Link(dve, s_link)
            tt, ts, stt = nc.vector.tensor_tensor, nc.vector.tensor_scalar, nc.vector.scalar_tensor_tensor
            nc.vector.memset(cond, 0.0).then_inc(s_zero, 1)
            nc.vector.memset(eps[:, :], EPS).then_inc(s_zero, 1)
            nc.vector.memset(ones[:, :], 1.0).then_inc(s_zero, 1)
            link(nc.vector.memset(sq, 0.0))
            with dve.Fori(0, TT // 2) as i:
                for g in range(0, 8, 2):
                    dve.wait_ge(s_xt, 8 * i + g + 1)
                    nc.vector.tensor_copy(h[:, 4 * (g % 4):4 * (g % 4) + 4, bass.ds((2 * i + g // 4) * P, P)],
                                          bank(g % 4).rearrange("p (k t) -> p k t", k=4)).then_inc(s_xt_dve, 1)
            dve.wait_ge(s_part, 2)
            for l in range(DEPTH):
                nc.vector.tensor_copy(par[l][:, :], ps[2 + l][:, 0:PR_N]).then_inc(s_parc, 1)
            dve.wait_ge(s_parc, 2)
            with dve.Fori(0, KT // 2) as i:
                for b in range(2):
                    dve.wait_ge(s_sqt[0], 2 * i + b + 1)
                    dve.wait_ge(s_sqa[0], 2 * i + b)
                    tt(sq, sq, sq_t[b], ALU.add).then_inc(s_sqa[0], 1)
            for l in range(DEPTH):
                with dve.Fori(0, 6) as i:
                    for b in range(2):
                        dve.wait_ge(s_ada_col, 12 * l + 2 * i + b + 1)
                        for t in range(2):
                            tt(ada_v[l][:, t, bass.ds(8 * i + 4 * b, 4)],
                               D[:, b * 512:b * 512 + 8].rearrange("p (j t) -> p t j", t=2)[:, t],
                               par[l][:, bass.ds(8 * i + 4 * b, 4)], ALU.add).then_inc(s_ada_b, 1)
                dve.wait_ge(s_ada_b, 24 * (l + 1))
                for t in range(2):
                    stt(gain_v[l][:, t], ada_v[l][:, t, KT:2 * KT], 1.0, par[l][:, PR_NORM:PR_NORM + KT],
                        ALU.add, ALU.mult).then_inc(s_gain, 1)

            for l in range(DEPTH):
                nq = q_tok(l)
                qt_n = q_tiles(l)
                dve.wait_ge(s_nroot, l + 1)
                link(nc.vector.reciprocal(inv_root[:, 0:TT], root[:, 0:TT]))
                for t in range(TT):
                    ts(n_diag[:, t * P:(t + 1) * P], ident[:, :], inv_root[:, t:t + 1], None, ALU.mult).then_inc(s_ndiag, 1)
                if l == 0:
                    dve.wait_ge(s_spill, 16)
                else:
                    dve.wait_ge(s_xst, 16 * KT)
                dve.wait_ge(s_nrb, l + 1)
                for k in range(KT):
                    tt(h[:, k, :], h[:, k, :], D[:, 0:TOK], ALU.mult).then_inc(s_hx, 1)

                for b in range(2):
                    dve.wait_ge(s_ev[l][b], T_POOL // 2)
                dve.wait_ge(s_inv, (l + 1) * 32)
                link(nc.vector.memset(pad_u, 0.0))
                seqs = ((0, SEQ, LAT0), (SEQ, CTX, CTX0))[:1 if l else 2]
                width = PW if l == 0 else LAT0 + SEQ + PAD

                def pool_gate(g):
                    dve.wait_ge(s_pmm, GROUPS * l + g + 1)
                    stt(mix[:, g, 0:nq], D[:, 0:nq], par[l][:, PR_POOL + g:PR_POOL + g + 1], mix[:, g, 0:nq],
                        ALU.mult, ALU.mult).then_inc(s_pg, 1)

                for g in range(GROUPS):
                    dve.wait_ge(s_mm[l], T_POOL + g + 1)
                    if g >= 1:
                        dve.wait_ge(s_pl[l], g * len(seqs))
                    for k, (a, n, at) in enumerate(seqs):
                        ins = nc.vector.tensor_copy(pad_u[:, at:at + n], ps[g % 2][:, a:a + n])
                        if k < len(seqs) - 1:
                            link(ins)
                    ins.then_inc(s_ev[l][g % 2], 1)
                    dve.wait_ge(s_ev[l][g % 2], (T_POOL + g) // 2 + 1)
                    if g >= 1:
                        pool_gate(g - 1)
                    src, dst = pad_u, win[0]
                    link(tt(dst[:, 1:width], src[:, 0:width - 1], src[:, 1:width], ALU.add))
                    lo = 1
                    for lev in range(g):
                        step = 1 << lev
                        src, dst = dst, win[(lev + 1) % 2]
                        a, e = 2 << lev, width - (2 << lev) + 1
                        link(tt(dst[:, a:e], src[:, a - step:e - step], src[:, a + step:e + step], ALU.add))
                    if g >= 1:
                        dve.wait_ge(s_pmm, GROUPS * l + g)
                    for a, n, at in seqs:
                        link(tt(pooled[:, a:a + n], dst[:, at:at + n], inv[:, g, a:a + n], ALU.mult))
                    for k, (a, n, at) in enumerate(seqs):
                        ins = tt(pooled[:, a:a + n], pooled[:, a:a + n], pad_u[:, at:at + n], ALU.subtract)
                        ins.then_inc(s_pl[l], 1)
                pool_gate(GROUPS - 1)
                for g in range(GROUPS):
                    dve.wait_ge(s_fpos, GROUPS * l + g + 1)
                    tt(mix[:, GROUPS + g, 0:nq], D[:, 0:nq], mix[:, GROUPS + g, 0:nq], ALU.mult).then_inc(s_fg, 1)

                dve.wait_ge(s_mm[l], T_KROPE + 1)
                stt(u_kr, A[:, 0:TOK], par[l][:, PR_KHR:PR_KHR + 1], rope[:, :], ALU.mult, ALU.mult).then_inc(s_ukr, 1)
                n_tmp = 0
                for j in range(2 * RT):
                    if j % RT:
                        n = nq if j < RT else TOK
                        acc = (sq_q, sq_k)[j // RT]
                        dve.wait_ge(s_csq, 2 * RT * l + j + 1)
                        if n_tmp:
                            dve.wait_ge(s_csa, 2 * (RT - 1) * l + n_tmp)
                        tt(acc[:, 0:n], acc[:, 0:n], sq_c[n_tmp % 2][:, 0:n], ALU.add).then_inc(s_csa, 1)
                        n_tmp += 1
                dve.wait_ge(s_croot, l + 1)
                link(nc.vector.reciprocal(inv_root[:, TT - qt_n:2 * TT], root[:, TT - qt_n:2 * TT]))
                for t in range(qt_n):
                    ts(q_diag[:, t * P:(t + 1) * P], ident[:, :], inv_root[:, TT - qt_n + t:TT - qt_n + t + 1], None,
                       ALU.mult).then_inc(s_cdiag[l], 1)
                for t in range(TT):
                    ts(diag[:, t * P:(t + 1) * P], ident[:, :], inv_root[:, TT + t:TT + t + 1], None, ALU.mult).then_inc(s_cdiag[l], 1)
                dve.wait_ge(s_crb, l + 1)
                for j in range(2 * RT):
                    n, src = (nq, C) if j < RT else (TOK, D)
                    stt(ckk[:, j, 0:n], ckk[:, j, 0:n], par[l][:, PR_QN + j:PR_QN + j + 1], src[:, 0:n],
                        ALU.mult, ALU.mult).then_inc(s_cn, 1)
                for b in range(2):
                    dve.wait_ge(s_ev[l][b], MM_IN // 2)

                def rotary(p, b):
                    dve.wait_ge(s_pqr[l], p + 1)
                    stt(qr[b][:, 0:nq], C[:, 0:nq], par[l][:, PR_QHR:PR_QHR + 1], rope[:, 0:nq], ALU.mult, ALU.mult).then_inc(s_eqr[l], 1)
                    dve.wait_ge(s_esr[l], p + 1)
                    dve.wait_ge(s_eqn[l], 2 * p + 2)
                    tt(sq_q[0:ROPE, 0:nq], sq_q[0:ROPE, 0:nq], sq_r[0:ROPE, 0:nq], ALU.add).then_inc(s_addq[l], 1)

                def key_squares(p):
                    dve.wait_ge(s_ekn[l], 2 * p + 2)
                    tt(sq_k[0:ROPE, :], sq_k[0:ROPE, :], kr_sq[0:ROPE, :], ALU.add).then_inc(s_addk[l], 1)

                def inverses(p, b, own):
                    dve.wait_ge(s_root[l], p + 1)
                    own(nc.vector.reciprocal(h_inv[b][:, TT - qt_n:2 * TT], h_root[b][:, TT - qt_n:2 * TT]))
                    ts(q_pos[b][:, 0:qt_n], h_inv[b][:, TT - qt_n:TT], SM_SCALE, None, ALU.mult).then_inc(s_qs[l], 1)
                    ts(q_neg[b][:, 0:qt_n], h_inv[b][:, TT - qt_n:TT], -SM_SCALE, None, ALU.mult).then_inc(s_qs[l], 1)
                    for t in range(TT):
                        ts(diag[:, t * P:(t + 1) * P], ident[:, :], h_inv[b][:, TT + t:TT + t + 1], None, ALU.mult).then_inc(s_diag[l], 1)

                def scale_keys(p, b):
                    dve.wait_ge(s_rb[l], p + 1)
                    tt(kn[b], kn[b], B[:, 0:TOK], ALU.mult).then_inc(s_kn[l], 1)
                    tt(krh[b], kr, B[:, 0:TOK], ALU.mult).then_inc(s_kn[l], 1)

                def attend(hd, b, proj):
                    p, pb = hd + 1, 1 - b
                    own = Link(dve, s_own[l], 1 + (2 * qt_n + 1) * hd)

                    def maxima(q):
                        n = TOK if q < LT else CTX
                        dve.wait_ge(s_s[l], hd * qt_n + q + 1)
                        own(nc.vector.tensor_reduce(top[:, q:q + 1], ps[q % 2][:, 0:n], AX_X, ALU.max))
                        tt(bias[:, q:q + 1], top[:, q:q + 1], q_neg[b][:, q:q + 1], ALU.mult).then_inc(s_nb[l], 1)

                    def normalise(q):
                        n = TOK if q < LT else CTX
                        dve.wait_ge(s_exp[l], hd * qt_n + q + 1)
                        own(nc.vector.reciprocal(inv_total[:, q:q + 1], total[:, q:q + 1]))
                        ts(prob[q % 2][:, 0:n], prob[q % 2][:, 0:n], inv_total[:, q:q + 1], None, ALU.mult).then_inc(s_sc[l], 1)

                    dve.wait_ge(s_qs[l], 2 * hd + 2)
                    maxima(0)
                    maxima(1)
                    normalise(0)
                    if proj:
                        rotary(p, pb)
                    normalise(1)
                    maxima(2)
                    normalise(2)
                    if proj:
                        key_squares(p)
                    maxima(3)
                    normalise(3)
                    for q in range(LT, qt_n):
                        maxima(q)
                    for q in range(LT, qt_n):
                        normalise(q)
                    if proj:
                        inverses(p, pb, own)
                    dve.wait_ge(s_pv[l], hd + 1)
                    m = mix[:, bass.ds(2 * GROUPS + hd, 1), 0:nq].rearrange("p a t -> p (a t)")
                    tt(m, A[:, 0:nq], m, ALU.mult).then_inc(s_om[l], 1)
                    if proj:
                        scale_keys(p, pb)

                dve.wait_ge(s_kr, l + 1)
                dve.wait_ge(s_krsq, l + 1)
                rotary(0, 0)
                key_squares(0)
                inverses(0, 0, Link(dve, s_own[l]))
                scale_keys(0, 0)
                with dve.Fori(0, HEADS // 2 - 1) as i:
                    for b in range(2):
                        attend(2 * i + b, b, True)
                attend(HEADS - 2, 0, True)
                attend(HEADS - 1, 1, False)

                if l == 0:
                    link(nc.vector.memset(sq, 0.0))
                with dve.Fori(0, 4) as i:
                    for j in range(4):
                        n = 4 * i + j
                        src = (B, A)[j % 2]
                        dve.wait_ge(s_cmm[l], n + 1)
                        dve.wait_ge(s_xin[4 * l + j], 16 * i + 16)
                        if l == 0:
                            hn = h[:, bass.ds(n, 1), :].rearrange("p a t -> p (a t)")
                            stt(hn[:, 0:SEQ], src[:, 0:SEQ], ada[l][:, bass.ds(n + 2 * KT, 1)], xt[j][:, 0:SEQ],
                                ALU.mult, ALU.add).then_inc(s_xnew, 1)
                            stt(hn[:, SEQ:TOK], src[:, SEQ:TOK], ada[l][:, bass.ds(n + 48 + 2 * KT, 1)], xt[j][:, SEQ:TOK],
                                ALU.mult, ALU.add).then_inc(s_cev[l][j % 2], 1)
                            dve.wait_ge(s_sqt[1], n + 1)
                            dve.wait_ge(s_sqa[1], n)
                            tt(sq, sq, sq_t[j % 2], ALU.add).then_inc(s_sqa[1], 1)
                        else:
                            dve.wait_ge(s_otr, 4 * i + max(j - 1, 0))
                            stt(x_out[j % 2], src[:, 0:SEQ], ada[l][:, bass.ds(n + 2 * KT, 1)], xt[j][:, 0:SEQ],
                                ALU.mult, ALU.add).then_inc(s_cev[l][j % 2], 1)

        @block.tensor
        def _(pe):
            mm, tr = nc.tensor.matmul, nc.tensor.transpose
            pe.wait_ge(s_const, 16 * N_CONST)
            with pe.Fori(0, TT // 2) as i:
                for g in range(8):
                    if g % 4 == 0:
                        pe.wait_ge(s_xn[g // 4], 16 * i + 16)
                    pe.wait_ge((s_xt_dve, s_xt_act)[g % 2], 4 * i + max(g - 2, 0) // 2)
                    for j in range(4):
                        k = 4 * (g % 4) + j
                        ins = tr(bank(g % 4)[:, j * P:(j + 1) * P], x_nat[g // 4][:, k * P:(k + 1) * P], ident[:, :])
                    ins.then_inc(s_xt, 1)
            pe.wait_ge(s_par, 16 * N_PAR)
            for l in range(DEPTH):
                tr(ps[2 + l][:, 0:PR_N], par_row[l][0:PR_N, :], ident[0:PR_N, 0:PR_N]).then_inc(s_part, 1)
            pe.wait_ge(s_parc, 2)
            pe.wait_ge(s_cond, 2)
            with pe.Fori(0, 12) as i:
                for b in range(2):
                    pe.wait_ge(s_ada_row, 2 * i)
                    for hf in range(2):
                        s = 2 * b + hf
                        pe.wait_ge(s_adw[s], 16 * i + 16)
                        for k in range(8):
                            q = k % 4
                            ins = mm(C[32 * q:32 * q + 32, b * 512:(b + 1) * 512], cond[:, 8 * hf + k, :], ada_slot[s][:, k, :],
                                     start=(hf == 0 and k < 4), stop=(hf == 1 and k >= 4))
                        ins.then_inc(s_ada_mm, 1)
                    pe.wait_ge(s_ada_row, 2 * i + b + 1)
                    pe.wait_ge(s_ada_b, 4 * i)
                    for j in range(4):
                        ins = mm(D[:, b * 512 + 2 * j:b * 512 + 2 * j + 2], ada_row[b][:, j * P:(j + 1) * P], sel[:, :],
                                 start=True, stop=True)
                    ins.then_inc(s_ada_col, 1)

            for l in range(DEPTH):
                nq = q_tok(l)
                qt_n = q_tiles(l)
                pe.wait_ge(s_sqa[l], KT)
                for t in range(TT):
                    ins = mm(A[:, t:t + 1], sq[:, t * P:(t + 1) * P], ones[:, 0:1], start=True, stop=True)
                ins.then_inc(s_ncol, 1)
                pe.wait_ge(s_ndiag, (l + 1) * TT)
                if l == 0:
                    pe.wait_ge(s_ada_b, 48)
                for a, n in parts(TOK):
                    ins = mm(D[:, a:a + n], ones[:, :], n_diag[:, a:a + n], start=True, stop=True)
                ins.then_inc(s_nrb, 1)

                def tile(n_free, n_ready, sem_free, w, b_ps, ntok, done, first=False):
                    if sem_free is not None:
                        pe.wait_ge(sem_free, n_free)
                    for k in range(KT):
                        if first:
                            pe.wait_ge(s_h[l], 2 * k + 2)
                        for a, n in parts(ntok):
                            ins = mm(ps[b_ps][:, a:a + n], w(k), h[:, k, a:a + n], start=(k == 0), stop=(k == KT - 1))
                    ins.then_inc(done, 1)

                def w_cols(j):
                    return lambda k: w_slot[j // 2][:, k, (j % 2) * P:(j % 2) * P + P]

                with pe.Fori(0, 2) as i:
                    for j in range(4):
                        if j % 2 == 0:
                            pe.wait_ge(s_w[l][j // 2], 16 * i + 16)
                        tile(2 * i + j // 2, None, s_ev[l][j % 2], w_cols(j), j % 2, nq, s_mm[l], first=(j == 0))

                def in_tile(n, ntok):
                    at = n - 1 if n > T_KROPE else n
                    j = at % 4
                    if j % 2 == 0:
                        pe.wait_ge(s_w[l][j // 2], 16 * (at // 4) + 16)
                    if n == T_KROPE + 2:
                        pe.wait_ge(s_krsq, l + 1)
                        free = None
                    else:
                        free = n // 2
                        if n > T_KROPE and n % 2 == 0:
                            free -= 1
                    tile(free, None, None if free is None else s_ev[l][n % 2], w_cols(j), n % 2, ntok, s_mm[l])

                pe.wait_ge(s_tab[l], 16 * (6 if l == 0 else 4))
                for s in range(2):
                    ins = mm(C[:, s * 512:(s + 1) * 512], chan[:, s * P:(s + 1) * P], fw, start=True, stop=True)
                ins.then_inc(s_cw, 1)
                pe.wait_ge(s_inv, (l + 1) * 32)

                def pool_product(g):
                    pe.wait_ge(s_pl[l], (g + 1) * (1 if l else 2))
                    pe.wait_ge(s_pg, GROUPS * l + g)
                    if g == 0:
                        pe.wait_ge(s_hx, (l + 1) * KT)
                    for a, n in parts(nq):
                        ins = mm(D[:, a:a + n], pw[:, g, :], pooled[:, a:a + n], start=True, stop=True)
                    ins.then_inc(s_pmm, 1)

                def fourier_channels(g):
                    n = T_FNET + g
                    pe.wait_ge(s_ev[l][n % 2], n // 2 + 1)
                    if g == 0:
                        pe.wait_ge(s_cwc, (l + 1) * 2)
                    pe.wait_ge(s_fab[l], g * (1 if l else 2))
                    for t in range(qt_n):
                        if t == LT:
                            pe.wait_ge(s_pg, (l + 1) * GROUPS)
                            pe.wait_ge(s_fg, GROUPS * l + g)
                        dst = C[:, t * 256:(t + 1) * 256] if t < LT else D[:, (t - LT) * 256:(t - LT + 1) * 256]
                        ins = mm(dst, f_u[g % 2][:, t * P:(t + 1) * P], chan_w[:, g, :], start=True, stop=True)
                    ins.then_inc(s_fch, 1)

                def fourier_positions(g):
                    pe.wait_ge(s_fab[l], (g + 1) * (1 if l else 2))
                    pe.wait_ge(s_pg, (l + 1) * GROUPS)
                    pe.wait_ge(s_fg, GROUPS * l + g)
                    for a, n, first_t, n_t, tab in ((0, SEQ, 0, LT, pos_lat), (SEQ, CTX, LT, 2, pos_ctx))[:1 if l else 2]:
                        for t in range(n_t):
                            for s in range(2):
                                ins = mm(D[:, a:a + n], f_ab[:, first_t + t, s * P:(s + 1) * P], tab[:, s, t, :],
                                         start=(t == 0 and s == 0), stop=(t == n_t - 1 and s == 1))
                    ins.then_inc(s_fpos, 1)

                for g in range(GROUPS):
                    in_tile(T_POOL + g, nq)
                    if g >= 1:
                        pool_product(g - 1)
                for m in range(GROUPS + 2):
                    in_tile(T_FNET + m, nq)
                    if m == 0:
                        pool_product(GROUPS - 1)
                    if m >= 2:
                        fourier_positions(m - 2)
                    if 1 <= m <= GROUPS:
                        fourier_channels(m - 1)
                for n in range(T_CQ + 2, T_KROPE):
                    in_tile(n, nq if n < T_CKV else TOK)
                pe.wait_ge(s_kw, (l + 1) * 16)
                pe.wait_ge(s_kws, (l + 1) * 2)
                tile(T_KROPE // 2, None, s_ev[l][0], lambda k: kr_w[:, k, :], 0, TOK, s_mm[l])
                in_tile(T_MLA, nq)
                in_tile(T_MLA + 1, nq)
                pe.wait_ge(s_csa, (l + 1) * (2 * (RT - 1)))
                pe.wait_ge(s_fg, (l + 1) * GROUPS)
                for t in range(qt_n):
                    mm(D[:, TT - qt_n + t:TT - qt_n + t + 1], sq_q[:, t * P:(t + 1) * P], ones[:, 0:1], start=True, stop=True)
                for t in range(TT):
                    ins = mm(D[:, TT + t:TT + t + 1], sq_k[:, t * P:(t + 1) * P], ones[:, 0:1], start=True, stop=True)
                ins.then_inc(s_ccol, 1)
                in_tile(T_MLA + 2, nq)
                pe.wait_ge(s_cdiag[l], qt_n + TT)
                for dst, src, ntok in ((C, q_diag, nq), (D, diag, TOK)):
                    for a, n in parts(ntok):
                        ins = mm(dst[:, a:a + n], ones[:, :], src[:, a:a + n], start=True, stop=True)
                ins.then_inc(s_crb, 1)
                for n in range(T_MLA + 3, MM_IN):
                    in_tile(n, nq)

                pe.wait_ge(s_ev[l][0], MM_IN // 2)
                pe.wait_ge(s_ukr, l + 1)
                for a, n in parts(TOK):
                    ins = mm(A[:, a:a + n], dup[:, :], u_kr[:, a:a + n], start=True, stop=True)
                ins.then_inc(s_krm, 1)
                pe.wait_ge(s_cn, (l + 1) * (2 * RT))
                pe.wait_ge(s_w[l][0], 192)
                pe.wait_ge(s_ev[l][1], MM_IN // 2)
                for t in range(TT):
                    if t == 1:
                        pe.wait_ge(s_kr, l + 1)
                    if t >= 2:
                        pe.wait_ge(s_v, TT * l + t - 1)
                    for k in range(RT):
                        for a in range(0, HEADS * VDIM, 512):
                            ins = mm((B, A)[t % 2][:, a:a + 512], ckv[:, k, t * P:(t + 1) * P], v_w[:, k, a:a + 512],
                                     start=(k == 0), stop=(k == RT - 1))
                    ins.then_inc(s_vmm, 1)

                def project(w, src, ntok, done):
                    for k in range(RT):
                        for a, n in parts(ntok):
                            ins = mm(C[:, a:a + n], w(k), src[:, k, a:a + n], start=(k == 0), stop=(k == RT - 1))
                    ins.then_inc(done, 1)

                def queries(p, b, first=False):
                    pe.wait_ge(s_wh[l][b], 16 * p + 32 - 16 * b)
                    if not first:
                        pe.wait_ge(s_root[l], p)
                    project(lambda k: wq[b][:, k, 0:NOPE], cq, nq, s_pqn[l])

                def rotary(p, b):
                    pe.wait_ge(s_sw[l], 2 * p + 2)
                    pe.wait_ge(s_eqn[l], 2 * p + 2)
                    project(lambda k: wq[b][:, k, NOPE:NOPE + P], cq, nq, s_pqr[l])

                def keys(p, b):
                    pe.wait_ge(s_esr[l], p + 1)
                    project(lambda k: wk[b][:, k, :], ckv, TOK, s_pkn[l])

                def sums(p):
                    pe.wait_ge(s_addq[l], p + 1)
                    pe.wait_ge(s_addk[l], p + 1)
                    for t in range(qt_n):
                        mm(C[:, TT - qt_n + t:TT - qt_n + t + 1], sq_q[:, t * P:(t + 1) * P], ones[:, 0:1], start=True, stop=True)
                    for t in range(TT):
                        ins = mm(C[:, TT + t:TT + t + 1], sq_k[:, t * P:(t + 1) * P], ones[:, 0:1], start=True, stop=True)
                    ins.then_inc(s_col[l], 1)

                def key_row(p):
                    pe.wait_ge(s_diag[l], TT * p + TT)
                    for a, n in parts(TOK):
                        ins = mm(B[:, a:a + n], ones[:, :], diag[:, a:a + n], start=True, stop=True)
                    ins.then_inc(s_rb[l], 1)

                def attend(hd, b, proj):
                    p, pb = hd + 1, 1 - b

                    def scores(q):
                        if q == 0:
                            pe.wait_ge(s_kn[l], 2 * hd + 2)
                            pe.wait_ge(s_eqr[l], hd + 1)
                            pe.wait_ge(s_om[l], hd)
                        if q >= 2:
                            pe.wait_ge(s_exp[l], hd * qt_n + q - 1)
                        for a, n, o in (((0, 512, 0), (512, CTX, 512)) if q < LT else ((SEQ, CTX, 0),)):
                            mm(ps[q % 2][:, o:o + n], qn[b][:, q * P:(q + 1) * P], kn[b][:, a:a + n], start=True, stop=False)
                            ins = mm(ps[q % 2][:, o:o + n], qr[b][:, q * P:(q + 1) * P], krh[b][:, a:a + n], start=False, stop=True)
                        ins.then_inc(s_s[l], 1)

                    def turn(q):
                        pe.wait_ge(s_sc[l], hd * qt_n + q + 1)
                        pe.wait_ge(s_pt[l], hd * qt_n + q)
                        for t in range(TT if q < LT else 2):
                            ins = tr(D[:, t * P:(t + 1) * P], prob[q % 2][:, t * P:(t + 1) * P], ident[:, :])
                        ins.then_inc(s_t[l], 1)

                    if proj:
                        queries(p, pb)
                    scores(0)
                    scores(1)
                    if proj:
                        rotary(p, pb)
                    turn(0)
                    scores(2)
                    turn(1)
                    if proj:
                        keys(p, pb)
                    scores(3)
                    turn(2)
                    for q in range(LT, qt_n):
                        scores(q)
                    if proj:
                        sums(p)
                    for q in range(3, qt_n):
                        turn(q)
                    pe.wait_ge(s_pt[l], hd * qt_n + qt_n)
                    pe.wait_ge(s_vh[l], hd + 1)
                    for t in range(TT):
                        ins = mm(A[:, 0:SEQ], vh[b][:, t, :], prob_t[:, t, :], start=(t == 0), stop=(t == TT - 1))
                    if qt_n > LT:
                        for t in range(2):
                            ins = mm(A[:, SEQ:TOK], vh[b][:, LT + t, :], prob_tc[:, t, :], start=(t == 0), stop=(t == 1))
                    ins.then_inc(s_pv[l], 1)
                    if proj:
                        key_row(p)

                queries(0, 0, first=True)
                rotary(0, 0)
                keys(0, 0)
                sums(0)
                pe.wait_ge(s_v, (l + 1) * TT)
                key_row(0)
                with pe.Fori(0, HEADS // 2 - 1) as i:
                    for b in range(2):
                        attend(2 * i + b, b, True)
                attend(HEADS - 2, 0, True)
                attend(HEADS - 1, 1, False)

                def out_turn(i, j):
                    pe.wait_ge(s_cev[l][j % 2], 2 * i + j // 2 + 1)
                    pe.wait_ge(s_oev, 4 * i + max(j - 1, 0))
                    for t in range(LT):
                        ins = tr((C, D)[j % 2][:, t * P:(t + 1) * P], x_out[j % 2][:, t * P:(t + 1) * P], ident[:, :])
                    ins.then_inc(s_otr, 1)

                with pe.Fori(0, 4) as i:
                    for j in range(4):
                        if j % 2 == 0:
                            pe.wait_ge(s_w[l][j // 2], (208, 144)[j // 2] + 16 * i)
                        pe.wait_ge(s_cev[l][j % 2], 2 * i + j // 2)
                        for k in range(KT):
                            if j == 0 and k >= 2 * GROUPS:
                                pe.wait_ge(s_om[l], k - 2 * GROUPS + 1)
                            for a, n in parts(nq):
                                ins = mm((B, A)[j % 2][:, a:a + n], w_slot[j // 2][:, k, (j % 2) * P:(j % 2) * P + P],
                                         mix[:, k, a:a + n], start=(k == 0), stop=(k == KT - 1))
                        ins.then_inc(s_cmm[l], 1)
                        if l == 1 and j >= 1:
                            out_turn(i, j - 1)
                    if l == 1:
                        out_turn(i, 3)


def shape_tables():
    pos = np.arange(SEQ)
    inv_freq = (10000.0 ** (-np.arange(ROPE // 4, dtype=np.float32) / np.float32(ROPE // 4))).astype(np.float32)
    ang_r = ((pos // GRID_W).astype(np.float32)[:, None] * inv_freq).astype(np.float32)
    ang_c = ((pos % GRID_W).astype(np.float32)[:, None] * inv_freq).astype(np.float32)
    ang = np.concatenate([ang_r, ang_r, ang_c, ang_c], axis=-1).astype(np.float64).T
    sign = np.where(np.arange(ROPE) % 32 < 16, -1.0, 1.0)[:, None]
    rope = np.zeros((P, TOK), np.float32)
    rope[:ROPE, :SEQ] = np.cos(ang)
    rope[ROPE:, :SEQ] = np.sin(ang) * sign
    rope[:ROPE, SEQ:] = 1.0

    def dft(n):
        a = 2.0 * np.pi * (np.outer(np.arange(n), np.arange(n)) % n) / n
        return np.cos(a), np.sin(a)

    cc, sc = dft(P)
    chan = np.concatenate([cc, sc], axis=1).astype(np.float32)

    def positions(n):
        a, b = dft(n)
        return (np.stack([a, -b]) / np.sqrt(n * P)).astype(np.float32)

    inv = np.zeros((GROUPS, TOK), np.float32)
    for g, w in enumerate((2, 4, 8, 16)):
        for a, n in ((0, SEQ), (SEQ, CTX)):
            t = np.arange(n)
            count = np.clip(t + w - w // 2, 0, n) - np.clip(t - w // 2, 0, n)
            inv[g, a:a + n] = 1.0 / count
    sel = np.zeros((P, 2), np.float32)
    for q in range(4):
        sel[32 * q, 0] = sel[32 * q + 1, 1] = 1.0
    half = np.eye(ROPE, dtype=np.float32)
    return {"k_ident": np.eye(P, dtype=np.float32), "k_sel": sel, "k_dup": np.tile(half, (2, 2)), "k_rope": rope,
            "k_chan": chan, "k_pos_lat": positions(SEQ), "k_pos_ctx": positions(CTX),
            "k_inv": np.tile(inv.reshape(1, -1), (P, 1))}


INPUTS = ["x", "c", "ctx", "c_ctx", "norm_w", "w_ada", "b_ada", "w_in", "pool_w", "pool_scale", "fnet_w", "q_norm_w",
          "w_uq", "kv_norm_w", "w_ukv", "q_head_norm_w", "k_head_norm_w", "w_out"]


def kernel(**inputs):
    from concourse import bacc
    from concourse.bass_utils import run_bass_kernel_spmd

    nc = bacc.Bacc("TRN2", target_bir_lowering=False, num_devices=1)
    arrays, args = {}, []
    tables = shape_tables()
    for name in INPUTS + list(tables):
        a = np.ascontiguousarray(inputs[name] if name in inputs else tables[name])
        arrays[f"in_{name}"] = a
        args.append(nc.dram_tensor(f"in_{name}", a.shape, F32, kind="ExternalInput").ap())
    out = nc.dram_tensor("out_x", (1, SEQ, D_MODEL), F32, kind="ExternalOutput").ap()
    build(nc, *args, out)
    r = run_bass_kernel_spmd(nc, [arrays], core_ids=[0])
    return r.results[0]["out_x"]
```

```python
from contextlib import ExitStack

import numpy as np

import concourse.bass as bass
from concourse import mybir

F32 = mybir.dt.float32
F32R = mybir.dt.float32r
ALU = mybir.AluOpType
ACT = mybir.ActivationFunctionType
AX_X = mybir.AxisListType.X

P = 128
D_MODEL = 2048
SEQ = 512
CTX = 256
TOK = SEQ + CTX
DEPTH = 2
KT = D_MODEL // P
GRID_W = 64
GROUPS = 4
HEADS = 8
NOPE = 128
ROPE = 64
HEAD = NOPE + ROPE
VDIM = 128
RANK = 512
RT = RANK // P
EPS = 1e-6
SM_SCALE = HEAD ** -0.5
TT = TOK // P
LT = SEQ // P
SLOT_N = 256

COL_POOL, COL_POOL_GATE, COL_FNET, COL_FNET_GATE = 0, 512, 1024, 1536
COL_CQ, COL_CKV, COL_KROPE, COL_MLA_GATE = 2048, 2560, 3072, 3136

PR_ADA, PR_NORM, PR_POOL, PR_QN, PR_KVN = 0, 48, 64, 68, 72
PR_QH, PR_QHR, PR_KH, PR_KHR, PR_N = 76, 77, 78, 79, 80

T_GATE, T_POOL, T_FNET, T_CQ, T_CKV, T_KROPE, T_MLA = 0, 8, 12, 16, 20, 24, 25
MM_IN = 33


class Link:

    def __init__(self, engine, sem, base=0):
        self.engine, self.sem, self.base, self.n = engine, sem, base, 0

    def __call__(self, ins):
        self.n += 1
        ins.then_inc(self.sem, 1)
        self.engine.wait_ge(self.sem, self.base + self.n)


def build(nc, x, c, ctx, c_ctx, norm_w, w_ada, b_ada, w_in, pool_w, pool_scale, fnet_w, q_norm_w,
          w_uq, kv_norm_w, w_ukv, q_head_norm_w, k_head_norm_w, w_out,
          k_ident, k_sel, k_dup, k_rope, k_chan, k_pos_lat, k_pos_ctx, k_inv, out):
    xt_dram = [nc.dram_tensor(f"xt{l}", (D_MODEL, TOK), F32, kind="Internal").ap()
               for l in range(DEPTH)]

    gate_dram = [nc.dram_tensor(f"gates{l}", (D_MODEL, TOK), F32, kind="Internal").ap() for l in range(DEPTH)]
    mix_dram = [nc.dram_tensor(f"mixed{l}", (D_MODEL // 2, TOK), F32, kind="Internal").ap() for l in range(DEPTH)]

    with ExitStack() as stack:
        def sb(name, n):
            return stack.enter_context(nc.sbuf_tensor(name, [P, n], F32))

        def sem(name):
            return stack.enter_context(nc.semaphore(name))

        def per_layer(name):
            return [sem(f"{name}{l}") for l in range(DEPTH)]

        def pair(name):
            return [[sem(f"{name}{l}_{b}") for b in range(2)] for l in range(DEPTH)]

        base = (nc.sbuf_base + 63) // 64 * 64
        HALF = KT * TOK
        R_N, W_N, WH_N, C_N, F_N = 2 * HALF, 2 * KT * SLOT_N, 2 * KT * P, (2 * RT + 1) * TOK, 7424
        W_AT, WH_AT, C_AT, F_AT = R_N, R_N + W_N, R_N + W_N + WH_N, R_N + W_N + WH_N + C_N
        sb("regions", R_N + W_N + WH_N + C_N + F_N + 16)

        def place(name, at, n, dt=F32):
            return nc.alloc_sbuf_tensor_at(name, [P, n], dt, offset=base + 4 * at)

        R_, W_ = place("r_region", 0, R_N), place("w_region", W_AT, W_N)
        C_, F_ = place("c_region", C_AT, C_N), place("f_region", F_AT, F_N)

        def view(region, at, n, k=None):
            v = region[:, at:at + n]
            return v if k is None else v.rearrange("p (k n) -> p k n", k=k)

        act_hi = view(place("act_hi", 0, HALF, F32R), 0, HALF, KT)
        act_lo = view(place("act_lo", HALF, HALF, F32R), 0, HALF, KT)
        hi_f32 = act_hi.bitcast(F32)
        h = view(R_, HALF, HALF, KT)
        w_slot = [view(W_, b * KT * SLOT_N, KT * SLOT_N, KT) for b in range(2)]
        w_lo_ = place("w_lo", W_AT, W_N, F32R)
        w_lo = [view(w_lo_, b * KT * SLOT_N, KT * SLOT_N, KT) for b in range(2)]
        w_hi_ = place("w_hi", WH_AT, WH_N, F32R)
        w_hi = [view(w_hi_, b * KT * P, KT * P, KT) for b in range(2)]
        cq = view(C_, 0, RT * TOK, RT)
        ckv = view(C_, RT * TOK, RT * TOK, RT)
        ckk = view(C_, 0, 2 * RT * TOK, 2 * RT)
        kr = view(C_, 2 * RT * TOK, TOK)
        gate_out = view(C_, 0, 8 * TOK, 8)
        inv = [view(C_, b * TOK, TOK) for b in range(2)]
        gate_in = [view(C_, 1536 + b * TOK, TOK) for b in range(2)]
        PAD = 8
        PW = PAD + SEQ + 2 * PAD + CTX + PAD
        LAT0, CTX0 = PAD, PAD + SEQ + 2 * PAD
        pad_u = view(C_, 3072, PW)
        win = [view(C_, 3072 + PW, PW), view(C_, 3072 + 2 * PW, PW)]
        pooled = view(C_, 3072 + 3 * PW, TOK)
        x_nat = [view(R_, 8192 + b * D_MODEL, D_MODEL) for b in range(2)]
        ada_row = [view(F_, b * 512, 512) for b in range(2)]
        cond = view(F_, 1024, KT * 32, KT)
        ada_slot = [view(W_, 0, 4096, 8), view(W_, 4096, 4096, 8), view(R_, 0, 4096, 8), view(R_, 4096, 4096, 8)]
        par_row = [view(F_, 6144 + l * P, P) for l in range(DEPTH)]
        xt = [view(F_, b * TOK, TOK) for b in range(4)]
        sq = view(F_, 3072, TOK)
        sq_t = [view(F_, 3840 + b * TOK, TOK) for b in range(2)]
        n_diag = view(F_, 5376, TOK)
        o_nat = [view(F_, 6144 + b * 512, 512, LT) for b in range(2)]
        pos_lat = view(F_, 0, 2 * LT * SEQ).rearrange("p (s k n) -> p s k n", s=2, k=LT)
        pos_ctx = view(F_, 4096, 2 * 2 * CTX).rearrange("p (s k n) -> p s k n", s=2, k=2)
        chan = view(F_, 5120, 256)
        chan_w = view(F_, 5376, GROUPS * 256, GROUPS)
        fw = view(F_, 6400, GROUPS * P)
        pw = view(F_, 6912, GROUPS * P, GROUPS)
        f_u = [view(C_, 3072 + b * TOK, TOK) for b in range(2)]
        f_ab = view(C_, 4608, TT * 256, TT)
        kr_w = view(F_, 0, KT * P, KT)
        kr_lo = view(place("kr_lo", F_AT, KT * P, F32R), 0, KT * P, KT)
        prob = [view(F_, b * TOK, TOK) for b in range(2)]
        prob_t = view(F_, 1536, TT * SEQ, TT)
        prob_tc = view(F_, 4608, 2 * CTX, 2)
        sq_q, sq_k, diag = view(F_, 5120, TOK), view(F_, 5888, TOK), view(F_, 6656, TOK)
        u_kr, sq_c, q_diag = prob[0], [prob[1], diag], view(F_, 1536, TOK)
        gate_st = [view(F_, 2304 + b * TOK, TOK) for b in range(2)]
        kr_sq0 = view(F_, 3840, TOK)
        v_all = view(R_, 0, TT * HEADS * VDIM, TT)
        qn_hi, qr_hi = ([act_hi[:, 8 + 2 * j + b, :] for b in range(2)] for j in range(2))
        qn_lo, qr_lo = ([act_lo[:, 2 * j + b, :] for b in range(2)] for j in range(2))
        qr = [h[:, 2 + b, :] for b in range(2)]
        kn, kn_hi, kn_lo = h[:, 4, :], act_hi[:, 12, :], act_lo[:, 4, :]
        krh, krh_hi, krh_lo = h[:, 5, :], act_hi[:, 13, :], act_lo[:, 5, :]
        gate_h = [view(R_, HALF + (6 + b) * TOK, TOK) for b in range(2)]
        sq_r, kr_sq = view(R_, 15 * TOK, TOK), view(R_, HALF + 15 * TOK, TOK)
        vh = [view(R_, 14 * TOK, TOK, TT), view(W_, 7168, TOK, TT)]
        v_w = view(W_, 0, 4096, RT)
        wq = [view(W_, 4096 + b * 1536, 1024, RT) for b in range(2)]
        wk = [view(W_, 4096 + b * 1536 + 1024, 512, RT) for b in range(2)]
        wq_lo = [view(w_lo_, 4096 + b * 1536, 1024, RT) for b in range(2)]
        wk_lo = [view(w_lo_, 4096 + b * 1536 + 1024, 512, RT) for b in range(2)]
        cq_hi, wq_hi = view(w_hi_, 0, RT * TOK, RT), view(w_hi_, RT * TOK, 1024, RT)
        ckv_hi, wk_hi = view(w_lo_, 0, RT * TOK, RT), view(w_lo_, RT * TOK, 512, RT)
        ckk_lo = view(place("ckk_lo", C_AT, 2 * RT * TOK, F32R), 0, 2 * RT * TOK, 2 * RT)
        cq_lo, ckv_lo = ckk_lo[:, 0:RT], ckk_lo[:, RT:2 * RT]

        ident, dup, ones = sb("ident", P), sb("dup", P), sb("ones", P)
        sel = sb("sel", 2)
        rope = sb("rope", TOK)
        c_in = sb("c_in", 2 * KT)
        par = [sb(f"par{l}", PR_N) for l in range(DEPTH)]
        ada = [sb(f"ada{l}", 2 * 48) for l in range(DEPTH)]
        gain = [sb(f"gain{l}", 2 * KT) for l in range(DEPTH)]
        eps = sb("eps", 1)
        root, inv_root = sb("root", 12), sb("inv_root", 12)
        h_root = [sb(f"h_root{b}", 12) for b in range(2)]
        h_inv = [sb(f"h_inv{b}", 12) for b in range(2)]
        q_pos = [sb(f"q_pos{b}", 6) for b in range(2)]
        q_neg = [sb(f"q_neg{b}", 6) for b in range(2)]
        top, bias, total, inv_total = sb("top", 6), sb("bias", 6), sb("total", 6), sb("inv_total", 6)
        ada_v = [a[:, :].rearrange("p (t j) -> p t j", t=2) for a in ada]
        gain_v = [g[:, :].rearrange("p (t j) -> p t j", t=2) for g in gain]

        ps = [stack.enter_context(nc.psum_tensor(f"ps{i}", [P, 1024], F32)) for i in range(4)]
        A, B, C, D = ps

        def bank(i):
            return ps[i // 2][:, (i % 2) * 512:(i % 2) * 512 + 512]

        s_const, s_par, s_zero, s_cond = sem("s_const"), sem("s_par"), sem("s_zero"), sem("s_cond")
        s_xn = [sem(f"s_xn{b}") for b in range(2)]
        s_part, s_parc = sem("s_part"), sem("s_parc")
        s_xt, s_xt_dve, s_xt_act = sem("s_xt"), sem("s_xt_dve"), sem("s_xt_act")
        s_adw = [sem(f"s_adw{b}") for b in range(4)]
        s_ada_mm, s_ada_row, s_ada_col, s_ada_b = sem("s_ada_mm"), sem("s_ada_row"), sem("s_ada_col"), sem("s_ada_b")
        s_gain = sem("s_gain")
        s_spill = sem("s_spill")
        s_link = sem("s_link")
        s_sqt, s_sqa = per_layer("s_sqt"), per_layer("s_sqa")
        s_h = sem("s_h")
        s_ncol, s_nroot, s_ndiag, s_nrb, s_hx = map(sem, ("s_ncol", "s_nroot", "s_ndiag", "s_nrb", "s_hx"))
        s_w, s_mm, s_ev = pair("s_w"), per_layer("s_mm"), per_layer("s_ev")
        s_tab, s_inv = per_layer("s_tab"), [sem(f"s_inv{b}") for b in range(2)]
        s_pl, s_pmm, s_pg = per_layer("s_pl"), sem("s_pmm"), sem("s_pg")
        s_cw, s_cwc, s_fch, s_fpos, s_fg = map(sem, ("s_cw", "s_cwc", "s_fch", "s_fpos", "s_fg"))
        s_fab = per_layer("s_fab")
        s_kw, s_kws, s_ukr, s_krsq = map(sem, ("s_kw", "s_kws", "s_ukr", "s_krsq"))
        s_csq, s_csa, s_ccol, s_croot, s_crb, s_cn = map(sem, ("s_csq", "s_csa", "s_ccol", "s_croot", "s_crb", "s_cn"))
        s_cdiag = per_layer("s_cdiag")
        s_krm, s_kr, s_vmm, s_v = map(sem, ("s_krm", "s_kr", "s_vmm", "s_v"))
        s_wh = [sem(f"s_wh{b}") for b in range(2)]
        s_sw, s_eqn, s_ekn, s_qs, s_kn, s_diag = map(sem, ("s_sw", "s_eqn", "s_ekn", "s_qs", "s_kn", "s_diag"))
        s_s, s_nb, s_exp, s_sc, s_t, s_pt = map(per_layer, ("s_s", "s_nb", "s_exp", "s_sc", "s_t", "s_pt"))
        s_pqn, s_pqr, s_pkn, s_eqr, s_esr, s_addq, s_addk = map(
            sem, ("s_pqn", "s_pqr", "s_pkn", "s_eqr", "s_esr", "s_addq", "s_addk"))
        s_col, s_root, s_rb, s_pv, s_om, s_vh = map(sem, ("s_col", "s_root", "s_rb", "s_pv", "s_om", "s_vh"))
        s_xin = [sem(f"s_xin{b}") for b in range(4)]
        s_cmm, s_xnew = per_layer("s_cmm"), per_layer("s_xnew")
        s_whi, s_wlo = sem("s_whi"), sem("s_wlo")
        s_hhi, s_ghi = sem("s_hhi"), sem("s_ghi")
        s_gact, s_gst = sem("s_gact"), [sem(f"s_gst{b}") for b in range(2)]
        s_mgate = sem("s_mgate")
        s_gin, s_mst = [sem(f"s_gin{b}") for b in range(2)], [sem(f"s_mst{b}") for b in range(2)]
        s_ghin = [sem(f"s_ghin{b}") for b in range(2)]
        s_mi, s_mhi, s_mlo = [sem(f"s_mi{b}") for b in range(2)], sem("s_mhi"), sem("s_mlo")
        s_oml, s_ksq = sem("s_oml"), sem("s_ksq")
        s_chi, s_clo, s_wqh, s_wql = map(sem, ("s_chi", "s_clo", "s_wqh", "s_wql"))
        s_qnl, s_qrh, s_qrl, s_khi, s_klo = map(sem, ("s_qnl", "s_qrh", "s_qrl", "s_khi", "s_klo"))
        s_xr = [sem(f"s_xr{b}") for b in range(4)]
        s_xst = [sem(f"s_xst{b}") for b in range(4)]
        s_own = per_layer("s_own")
        s_otr, s_oev = sem("s_otr"), sem("s_oev")
        s_out = [sem(f"s_out{b}") for b in range(2)]

        SPLITS = MM_IN + KT

        N_CONST = 6
        N_PAR = 2 * (5 + 2 * 6)

        def q_tok(l):
            return TOK if l < DEPTH - 1 else SEQ

        def q_tiles(l):
            return q_tok(l) // P

        def parts(n):
            return [(a, min(n - a, 512)) for a in range(0, n, 512)]

        def at_of(n):
            return n - 1 if n > T_KROPE else n

        def w_cols(w, j):
            return w[j // 2][:, :, (j % 2) * P:(j % 2) * P + P]

        def seqs_of(l):
            return ((0, SEQ, LAT0), (SEQ, CTX, CTX0))[:1 if l else 2]

        W_OUT = (16 * (8 + RT), 16 * 8)

        block = stack.enter_context(nc.Block())

        @block.sync
        def _(sp):
            for dst, src in ((ident[:, :], k_ident), (dup[:, :], k_dup), (sel[:, :], k_sel), (rope[:, :], k_rope),
                             (c_in[:, 0:KT], c.rearrange("a (p k) -> (a p) k", k=KT)),
                             (c_in[:, KT:2 * KT], c_ctx.rearrange("(p k) -> p k", k=KT))):
                sp.dma_start(dst, src).then_inc(s_const, 16)
            for t in range(TT):
                if t >= 2:
                    sp.wait_ge(s_xt, 4 * (t - 1))
                src = x[0, t * P:(t + 1) * P, :] if t < LT else ctx[0, (t - LT) * P:(t - LT + 1) * P, :]
                sp.dma_start(x_nat[t % 2], src).then_inc(s_xn[t % 2], 16)

            def ada_load(l, i, s):
                src = w_ada[l].rearrange("(p k) n -> p k n", k=KT)
                sp.dma_start(ada_slot[s], src[:, (s % 2) * 8:(s % 2) * 8 + 8, bass.ds((2 * i + s // 2) * 512, 512)])\
                  .then_inc(s_adw[s], 16)

            for s in range(4):
                ada_load(0, 0, s)
            for i in range(1, 2):
                for s in range(4):
                    sp.wait_ge(s_ada_mm, 4 * i + s - 3)
                    ada_load(0, i, s)
            for l in range(DEPTH):
                with sp.Fori(2 - 2 * l, 6) as i:
                    for s in range(4):
                        sp.wait_ge(s_ada_mm, 24 * l + 4 * i + s - 3)
                        ada_load(l, i, s)

            for l in range(DEPTH):
                src = w_in[l].rearrange("(k p) n -> p k n", p=P)

                def load_in(m, col, done, b):
                    if m >= 2:
                        sp.wait_ge(s_mm[l], done)
                    sp.dma_start(w_slot[b], src[:, :, bass.ds(col, SLOT_N)]).then_inc(s_w[l][b], 16)

                if l == 0:
                    sp.wait_ge(s_ada_mm, 24 * DEPTH)
                else:
                    sp.wait_ge(s_cmm[l - 1], KT - 2)
                load_in(0, COL_POOL_GATE, 0, 0)
                if l > 0:
                    sp.wait_ge(s_cmm[l - 1], KT)
                load_in(1, COL_POOL_GATE + SLOT_N, 0, 1)
                load_in(2, COL_FNET_GATE, 2, 0)
                load_in(3, COL_FNET_GATE + SLOT_N, 4, 1)
                for m, col in ((4, COL_POOL), (6, COL_FNET), (8, COL_CQ), (10, COL_CKV)):
                    load_in(m, col, 2 * m - 2, 0)
                    load_in(m + 1, col + SLOT_N, 2 * m, 1)
                sp.wait_ge(s_fpos, (l + 1) * GROUPS)
                sp.dma_start(kr_w[:, :, 0:ROPE], src[:, :, COL_KROPE:COL_KROPE + ROPE]).then_inc(s_kw, 16)
                for j, done in enumerate((22, 24, 27, 29)):
                    load_in(12 + j, COL_MLA_GATE + j * SLOT_N, done, j % 2)
                sp.wait_ge(s_mm[l], 31)
                for k in range(RT):
                    src_v = w_ukv[l, k * P:(k + 1) * P, :].rearrange("p (h n) -> p h n", h=HEADS)[:, :, NOPE:]
                    sp.dma_start(v_w[:, k, :].rearrange("p (h n) -> p h n", h=HEADS), src_v).then_inc(s_w[l][0], 16)

                def head_load(hd, b):
                    sp.dma_start(wq[b][:, :, 0:HEAD],
                                 w_uq[l].rearrange("(k p) n -> p k n", p=P)[:, :, bass.ds(hd * HEAD, HEAD)]).then_inc(s_wh[b], 16)
                    sp.dma_start(wk[b],
                                 w_ukv[l].rearrange("(k p) n -> p k n", p=P)[:, :, bass.ds(hd * (NOPE + VDIM), NOPE)])\
                      .then_inc(s_wh[b], 16)

                sp.wait_ge(s_mm[l], MM_IN)
                for b in range(2):
                    head_load(b, b)
                with sp.Fori(1, HEADS // 2) as i:
                    for b in range(2):
                        sp.wait_ge(s_pkn, HEADS * l + 2 * i + b - 1)
                        head_load(2 * i + b, b)
                src_o = w_out[l].rearrange("(k p) n -> p k n", p=P)
                sp.wait_ge(s_pkn, HEADS * (l + 1))
                sp.dma_start(w_slot[0], src_o[:, :, 0:SLOT_N]).then_inc(s_w[l][0], 16)
                sp.wait_ge(s_pv, HEADS * (l + 1))
                sp.dma_start(w_slot[1], src_o[:, :, SLOT_N:2 * SLOT_N]).then_inc(s_w[l][1], 16)
                with sp.Fori(1, 4) as i:
                    for b in range(2):
                        sp.wait_ge(s_cmm[l], 4 * i + 2 * b - 2)
                        sp.dma_start(w_slot[b], src_o[:, :, bass.ds((2 * i + b) * SLOT_N, SLOT_N)]).then_inc(s_w[l][b], 16)

        @block.gpsimd
        def _(pool):
            for l in range(DEPTH):
                row = par_row[l]

                def load(r, n, src):
                    pool.dma_start(row[r:r + n, :], src.rearrange("(r n) -> r n", n=P)).then_inc(s_par, 16)

                load(PR_ADA, 48, b_ada[l])
                load(PR_NORM, KT, norm_w[l])
                load(PR_POOL, GROUPS, pool_scale[l])
                load(PR_QN, RT, q_norm_w[l])
                load(PR_KVN, RT, kv_norm_w[l])
                for r, src in ((PR_QH, q_head_norm_w[l]), (PR_KH, k_head_norm_w[l])):
                    load(r, 1, src[0:NOPE])
                    pool.dma_start(row[r + 1:r + 2, 0:ROPE], src[NOPE:HEAD].rearrange("(r n) -> r n", r=1)).then_inc(s_par, 16)
                    for q in range(4):
                        a = NOPE + 16 * (q ^ 1)
                        pool.dma_start(row[r + 1:r + 2, ROPE + 16 * q:ROPE + 16 * q + 16],
                                       src[a:a + 16].rearrange("(r n) -> r n", r=1)).then_inc(s_par, 16)
            pool.wait_ge(s_xt_dve, 2 * TT)
            pool.wait_ge(s_xt_act, 2 * TT)
            pool.dma_start(xt_dram[0].rearrange("(k p) t -> p k t", p=P), h).then_inc(s_spill, 16)

            for l in range(DEPTH):
                nt = q_tok(l)
                rows = gate_dram[l].rearrange("(k p) t -> p k t", p=P)

                pool.wait_ge(s_nrb, l + 1)
                pool.dma_start(pw, pool_w[l].rearrange("g c d -> c g d")).then_inc(s_tab[l], 16)
                pool.dma_start(fw.rearrange("p (g d) -> p g d", g=GROUPS), fnet_w[l].rearrange("g c d -> c g d")).then_inc(s_tab[l], 16)
                pool.dma_start(chan, k_chan).then_inc(s_tab[l], 16)
                for s in range(2):
                    pool.dma_start(pos_lat[:, s], k_pos_lat[s].rearrange("(k p) n -> p k n", p=P)).then_inc(s_tab[l], 16)
                    if l < DEPTH - 1:
                        pool.dma_start(pos_ctx[:, s], k_pos_ctx[s].rearrange("(k p) n -> p k n", p=P)).then_inc(s_tab[l], 16)

                for b in range(2):
                    pool.wait_ge(s_gact, 8 * l + 4 * b + 4)
                    pool.dma_start(rows[:, 4 * b:4 * b + 4, 0:nt], gate_out[:, 4 * b:4 * b + 4, 0:nt]).then_inc(s_gst[b], 16)
                for b in range(2):
                    pool.wait_ge(s_gst[b], 80 * l + 16)

                def group_in(g):
                    if g < GROUPS:
                        pool.dma_start(inv[g % 2], k_inv[:, g * TOK:(g + 1) * TOK]).then_inc(s_inv[g % 2], 16)
                    pool.dma_start(gate_in[g % 2][:, 0:nt], gate_dram[l][g * P:(g + 1) * P, 0:nt]).then_inc(s_gin[g % 2], 16)

                group_in(0)
                group_in(1)
                for g in range(2 * GROUPS):
                    if g < GROUPS:
                        pool.wait_ge(s_pg, GROUPS * l + g + 1)
                    else:
                        pool.wait_ge(s_fg, GROUPS * l + g - GROUPS + 1)
                    pool.dma_start(mix_dram[l][g * P:(g + 1) * P, 0:nt], gate_in[g % 2][:, 0:nt]).then_inc(s_mst[g % 2], 16)
                    if g + 2 < 2 * GROUPS:
                        pool.wait_ge(s_mst[g % 2], 64 * l + 16 * (g // 2) + 16)
                        group_in(g + 2)

                def swap(dst, src, s):
                    d = dst.rearrange("p k (a b c) -> p k a b c", a=2, b=2)
                    o = src.rearrange("p k (a b c) -> p k a b c", a=2, b=2)
                    for b in range(2):
                        nc.gpsimd.tensor_copy(d[:, :, :, b], o[:, :, :, 1 - b]).then_inc(s, 1)

                pool.wait_ge(s_kw, (l + 1) * 16)
                swap(kr_w[:, :, ROPE:P], kr_w[:, :, 0:ROPE], s_kws)

                for q in range(HEADS):
                    pool.wait_ge(s_mgate, HEADS * l + q + 1)
                    pool.dma_start(rows[:, 8 + q, 0:nt], gate_st[q % 2][:, 0:nt]).then_inc(s_gst[q % 2], 16)
                for b in range(2):
                    pool.wait_ge(s_gst[b], 80 * l + 80)
                pool.wait_ge(s_mm[l], MM_IN)

                def gate_load(hd):
                    pool.dma_start(gate_h[hd % 2][:, 0:nt], gate_dram[l][(8 + hd) * P:(9 + hd) * P, 0:nt]).then_inc(s_ghin[hd % 2], 16)

                gate_load(0)
                gate_load(1)
                for hd in range(HEADS):
                    b = hd % 2
                    pool.wait_ge(s_wh[b], 16 * HEADS * l + 32 * (hd // 2) + 32)
                    swap(wq[b][:, :, HEAD:HEAD + ROPE], wq[b][:, :, NOPE:HEAD], s_sw)
                    if hd == 0:
                        pool.wait_ge(s_v, (l + 1) * TT)
                    if hd >= 2:
                        pool.wait_ge(s_pv, HEADS * l + hd - 1)
                    nc.gpsimd.tensor_copy(vh[b], v_all[:, :, hd * VDIM:(hd + 1) * VDIM]).then_inc(s_vh, 1)
                    if hd >= 2:
                        pool.wait_ge(s_om, HEADS * l + hd - 1)
                        gate_load(hd)

                mixed = mix_dram[l].rearrange("(k p) t -> p k t", p=P)
                for b in range(2):
                    pool.wait_ge(s_mst[b], 64 * (l + 1))
                pool.wait_ge(s_s[l], HEADS * q_tiles(l))
                pool.dma_start(h[:, 0:6, 0:nt], mixed[:, 0:6, 0:nt]).then_inc(s_mi[0], 16)
                if l == 0:
                    pool.wait_ge(s_spill, 16)
                pool.wait_ge(s_pv, HEADS * (l + 1))
                for b in range(4):
                    pool.dma_start(xt[b][:, 0:nt], xt_dram[l][b * P:(b + 1) * P, 0:nt]).then_inc(s_xin[b], 16)
                pool.wait_ge(s_om, HEADS * (l + 1))
                pool.dma_start(h[:, 6:8, 0:nt], mixed[:, 6:8, 0:nt]).then_inc(s_mi[1], 16)

                def tile_out(i, b, load_next):
                    n = 4 * i + b
                    if l == 0:
                        pool.wait_ge(s_xnew[0], n + 1)
                        pool.dma_start(xt_dram[1][bass.ds(n * P, P), :], xt[b]).then_inc(s_xst[b], 16)
                        if load_next:
                            pool.wait_ge(s_sqt[1], n + 1)
                            pool.wait_ge(s_xst[b], 16 * i + 16)
                    else:
                        pool.wait_ge(s_oev, n + 1)
                    if load_next:
                        pool.dma_start(xt[b][:, 0:nt], xt_dram[l][bass.ds(n * P + 4 * P, P), 0:nt]).then_inc(s_xin[b], 16)
                    if l == 1:
                        pool.dma_start(out[0].rearrange("(t p) n -> p t n", p=P)[:, :, bass.ds(n * P, P)],
                                       o_nat[b % 2]).then_inc(s_out[b % 2], 16)

                with pool.Fori(0, 3) as i:
                    for b in range(4):
                        tile_out(i, b, True)
                for b in range(4):
                    tile_out(3, b, False)
                if l == 0:
                    for b in range(4):
                        pool.wait_ge(s_xst[b], 16 * KT // 4)
                    pool.wait_ge(s_cmm[0], KT)
                    for b in range(4):
                        pool.dma_start(h[:, 4 * b:4 * b + 4, :], xt_dram[1].rearrange("(k p) t -> p k t", p=P)[:, 4 * b:4 * b + 4, :])\
                            .then_inc(s_xr[b], 16)
            for b in range(2):
                pool.wait_ge(s_out[b], 16 * KT // 2)

        @block.scalar
        def _(act):
            def copy(o, i):
                return nc.scalar.activation(o, i, ACT.Copy)

            def square(o, i):
                return nc.scalar.activation(o, i, ACT.Square)

            act.wait_ge(s_zero, 3)
            act.wait_ge(s_const, 16 * N_CONST)
            for t in range(2):
                nc.scalar.activation(cond[:, :, t], c_in[:, t * KT:(t + 1) * KT], ACT.Silu).then_inc(s_cond, 1)
            with act.Fori(0, TT // 2) as i:
                for g in range(1, 8, 2):
                    act.wait_ge(s_xt, 8 * i + g + 1)
                    copy(h[:, 4 * (g % 4):4 * (g % 4) + 4, bass.ds((2 * i + g // 4) * P, P)],
                         bank(g % 4).rearrange("p (k t) -> p k t", k=4)).then_inc(s_xt_act, 1)
            act.wait_ge(s_xt_dve, 2 * TT)
            act.wait_ge(s_xt_act, 2 * TT)

            def stream_square(k, b):
                square(sq_t[b], h[:, bass.ds(k, 1), :].rearrange("p a t -> p (a t)")).then_inc(s_sqt[0], 1)

            stream_square(0, 0)
            stream_square(1, 1)
            with act.Fori(1, KT // 2) as i:
                for b in range(2):
                    act.wait_ge(s_sqa[0], 2 * i + b - 1)
                    stream_square(2 * i + b, b)

            def ada_copy(i, b):
                act.wait_ge(s_ada_mm, 4 * i + 2 * b + 2)
                copy(ada_row[b], C[:, b * 512:(b + 1) * 512]).then_inc(s_ada_row, 1)

            ada_copy(0, 0)
            ada_copy(0, 1)
            with act.Fori(1, 12) as i:
                for b in range(2):
                    act.wait_ge(s_ada_col, 2 * i + b - 1)
                    ada_copy(i, b)

            for l in range(DEPTH):
                nq = q_tok(l)
                qt_n = q_tiles(l)
                act.wait_ge(s_ncol, l + 1)
                nc.scalar.activation(root[:, 0:TT], A[:, 0:TT], ACT.Sqrt, bias=eps[:, 0:1], scale=1.0 / D_MODEL).then_inc(s_nroot, 1)
                act.wait_ge(s_gain, 2 * (l + 1))

                def split(n):
                    at = at_of(n)
                    if n == T_KROPE:
                        act.wait_ge(s_kws, 2 * (l + 1))
                        copy(w_hi[0], kr_w).then_inc(s_whi, 1)
                        return
                    if at % 2 == 0:
                        act.wait_ge(s_w[l][at % 4 // 2], 16 * (at // 4) + 16)
                    copy(w_hi[n % 2], w_cols(w_slot, at % 4)).then_inc(s_whi, 1)

                if l > 0:
                    act.wait_ge(s_cmm[l - 1], KT)
                split(0)
                for k in range(KT):
                    act.wait_ge(s_hx, 2 * (KT * l + k + 1))
                    for t, (a, n) in enumerate(((0, SEQ), (SEQ, CTX))):
                        nc.scalar.activation(act_hi[:, k, a:a + n], h[:, k, a:a + n], ACT.Identity,
                                             bias=ada[l][:, t * 48 + k:t * 48 + k + 1]).then_inc(s_hhi, 1)

                with act.Fori(0, 2) as i:
                    for j in range(4):
                        at = (j + 1) % 4
                        if at % 2 == 0:
                            act.wait_ge(s_w[l][at // 2], 16 * i + 16 + 16 * ((j + 1) // 4))
                        copy(w_hi[at % 2], w_cols(w_slot, at)).then_inc(s_whi, 1)
                        act.wait_ge(s_mm[l], 4 * i + j + 1)
                        nc.scalar.activation(gate_out[:, bass.ds(4 * i + j, 1), 0:nq].rearrange("p a t -> p (a t)"),
                                             ps[j % 2][:, 0:nq], ACT.Silu).then_inc(s_gact, 1)
                for n in range(T_POOL, T_FNET):
                    if n > T_POOL:
                        act.wait_ge(s_ev[l], n - T_POOL)
                    split(n + 1)
                act.wait_ge(s_cw, l + 1)
                for s in range(2):
                    copy(chan_w[:, :, s * P:(s + 1) * P], C[:, s * 512:(s + 1) * 512].rearrange("p (g d) -> p g d", g=GROUPS))\
                        .then_inc(s_cwc, 1)

                def fourier_ab(g):
                    act.wait_ge(s_fch, GROUPS * l + g + 1)
                    if g == 0:
                        act.wait_ge(s_pmm, (l + 1) * GROUPS)
                    else:
                        act.wait_ge(s_fpos, GROUPS * l + g)
                    copy(f_ab[:, 0:4, :], C[:, :].rearrange("p (t n) -> p t n", t=4)).then_inc(s_fab[l], 1)
                    if l == 0:
                        copy(f_ab[:, 4:6, :], D[:, 0:512].rearrange("p (t n) -> p t n", t=2)).then_inc(s_fab[l], 1)

                for j in range(GROUPS):
                    if j == 0:
                        act.wait_ge(s_ev[l], GROUPS)
                    split(T_FNET + j + 1)
                    act.wait_ge(s_mm[l], T_FNET + j + 1)
                    if j == 0:
                        act.wait_ge(s_pl[l], GROUPS * len(seqs_of(l)))
                    if j >= 2:
                        act.wait_ge(s_fch, GROUPS * l + j - 1)
                    copy(f_u[j % 2][:, 0:nq], ps[j % 2][:, 0:nq]).then_inc(s_ev[l], 1)
                    if j >= 1:
                        fourier_ab(j - 1)
                for j in range(2 * RT):
                    n = nq if j < RT else TOK
                    if j < 2 * RT - 1:
                        split(T_CQ + j + 1)
                    act.wait_ge(s_mm[l], T_CQ + j + 1)
                    if j == 2:
                        for b in range(2):
                            act.wait_ge(s_mst[b], 64 * (l + 1))
                    if j == RT:
                        act.wait_ge(s_fpos, (l + 1) * GROUPS)
                    copy(ckk[:, j, 0:n], ps[j % 2][:, 0:n]).then_inc(s_ev[l], 1)
                    if j == 0:
                        fourier_ab(GROUPS - 1)
                    if j == 2 * RT - 2:
                        split(T_KROPE)
                split(T_MLA)
                act.wait_ge(s_mm[l], T_KROPE + 1)
                act.wait_ge(s_ukr, l + 1)
                square(kr_sq0[0:ROPE, :], A[0:ROPE, 0:TOK]).then_inc(s_krsq, 1)
                split(T_MLA + 1)
                act.wait_ge(s_ev[l], GROUPS * 2 + 2 * RT)
                n_tmp = 0
                for j in range(2 * RT):
                    n = nq if j < RT else TOK
                    if j % RT == 0:
                        dst = (sq_q, sq_k)[j // RT]
                    else:
                        if n_tmp >= 2:
                            act.wait_ge(s_csa, 2 * (RT - 1) * l + n_tmp - 1)
                        dst = sq_c[n_tmp % 2]
                        n_tmp += 1
                    square(dst[:, 0:n], ckk[:, j, 0:n]).then_inc(s_csq, 1)

                def gate(n):
                    q = n - T_MLA
                    act.wait_ge(s_mm[l], n + 1)
                    if q >= 2:
                        act.wait_ge(s_gst[q % 2], 80 * l + 16 * (q // 2) + 16)
                    nc.scalar.activation(gate_st[q % 2][:, 0:nq], ps[n % 2][:, 0:nq], ACT.Silu).then_inc(s_mgate, 1)

                gate(T_MLA)
                split(T_MLA + 2)
                gate(T_MLA + 1)
                split(T_MLA + 3)
                act.wait_ge(s_ccol, l + 1)
                nc.scalar.activation(root[:, TT - qt_n:2 * TT], D[:, TT - qt_n:2 * TT], ACT.Sqrt,
                                     bias=eps[:, 0:1], scale=1.0 / RANK).then_inc(s_croot, 1)
                for n in range(T_MLA + 2, MM_IN):
                    gate(n)
                    if n + 2 < MM_IN:
                        split(n + 2)
                act.wait_ge(s_krm, l + 1)
                copy(kr, A[:, 0:TOK]).then_inc(s_kr, 1)

                def latent_high(j):
                    n = nq if j < RT else TOK
                    act.wait_ge(s_cn, 2 * RT * l + j + 1)
                    copy((cq_hi, ckv_hi)[j // RT][:, j % RT, 0:n], ckk[:, j, 0:n]).then_inc(s_chi, 1)

                def query_weights_high(p, b):
                    act.wait_ge(s_sw, 2 * HEADS * l + 2 * p + 2)
                    copy(wq_hi, wq[b]).then_inc(s_wqh, 1)

                def key_weights_high(b):
                    copy(wk_hi, wk[b]).then_inc(s_wqh, 1)

                for j in range(RT):
                    latent_high(j)
                for t in range(TT):
                    act.wait_ge(s_vmm, TT * l + t + 1)
                    copy(v_all[:, t, :], (B, A)[t % 2][:, :]).then_inc(s_v, 1)
                    if t == 1:
                        query_weights_high(0, 0)

                def queries(p, b):
                    act.wait_ge(s_pqn, HEADS * l + p + 1)
                    square(sq_q[:, 0:nq], C[:, 0:nq]).then_inc(s_eqn, 1)
                    nc.scalar.activation(qn_hi[b][:, 0:nq], C[:, 0:nq], ACT.Identity, scale=par[l][:, PR_QH:PR_QH + 1]).then_inc(s_eqn, 1)

                def rotary_squares(p, b):
                    act.wait_ge(s_eqr, HEADS * l + p + 1)
                    square(sq_r[0:ROPE, 0:nq], C[0:ROPE, 0:nq]).then_inc(s_esr, 1)
                    copy(qr_hi[b][:, 0:nq], qr[b][:, 0:nq]).then_inc(s_qrh, 1)

                def keys_high(p):
                    act.wait_ge(s_kn, 2 * HEADS * l + 2 * p + 1)
                    copy(kn_hi, kn).then_inc(s_khi, 1)
                    act.wait_ge(s_kn, 2 * HEADS * l + 2 * p + 2)
                    copy(krh_hi, krh).then_inc(s_khi, 1)

                def key_square(p):
                    act.wait_ge(s_pkn, HEADS * l + p + 1)
                    square(sq_k, C[:, 0:TOK]).then_inc(s_ekn, 1)

                def keys():
                    nc.scalar.activation(kn, C[:, 0:TOK], ACT.Identity, scale=par[l][:, PR_KH:PR_KH + 1]).then_inc(s_ekn, 1)

                def roots(p, b):
                    act.wait_ge(s_col, HEADS * l + p + 1)
                    nc.scalar.activation(h_root[b][:, TT - qt_n:2 * TT], C[:, TT - qt_n:2 * TT], ACT.Sqrt,
                                         bias=eps[:, 0:1], scale=1.0 / HEAD).then_inc(s_root, 1)

                def out_split(i, j, n):
                    if j % 2 == 0:
                        act.wait_ge(s_w[l][j // 2], W_OUT[j // 2] + 16 * i + 16)
                    copy(w_hi[j % 2], w_cols(w_slot, j)).then_inc(s_whi, 1)

                def attend(hd, b, proj, more=True):
                    p, pb = hd + 1, 1 - b

                    def exp(q):
                        lo = 0 if q < LT else SEQ
                        n = TOK if q < LT else CTX
                        act.wait_ge(s_nb[l], hd * qt_n + q + 1)
                        if q >= 2:
                            act.wait_ge(s_t[l], hd * qt_n + q - 1)
                        nc.scalar.activation(prob[q % 2][:, 0:n], ps[q % 2][:, 0:n], ACT.Exp, bias=bias[:, q:q + 1],
                                             scale=q_pos[b][:, q:q + 1], accum_out=total[:, q:q + 1]).then_inc(s_exp[l], 1)

                    def turned(q):
                        act.wait_ge(s_t[l], hd * qt_n + q + 1)
                        if q < LT:
                            if q == 0 and not (isinstance(hd, int) and hd == 0):
                                act.wait_ge(s_pv, HEADS * l + hd)
                            copy(prob_t[:, :, q * P:(q + 1) * P], D[:, 0:TOK].rearrange("p (k q) -> p k q", k=TT)).then_inc(s_pt[l], 1)
                        else:
                            q -= LT
                            copy(prob_tc[:, :, q * P:(q + 1) * P], D[:, q * 512:q * 512 + CTX].rearrange("p (k q) -> p k q", k=2))\
                                .then_inc(s_pt[l], 1)

                    if proj:
                        queries(p, pb)
                    act.wait_ge(s_qs, 2 * HEADS * l + 2 * hd + 2)
                    exp(0)
                    exp(1)
                    if proj:
                        rotary_squares(p, pb)
                    turned(0)
                    exp(2)
                    turned(1)
                    exp(3)
                    turned(2)
                    if qt_n > LT:
                        exp(4)
                        exp(5)
                        turned(3)
                    if proj:
                        key_square(p)
                    for q in range(3 if qt_n == LT else LT, qt_n):
                        turned(q)
                    if proj:
                        keys()
                        roots(p, pb)
                        if more:
                            query_weights_high(p + 1, b)
                            key_weights_high(b)
                        keys_high(p)

                for b in range(2):
                    act.wait_ge(s_gst[b], 80 * (l + 1))
                queries(0, 0)
                for j in range(RT, 2 * RT):
                    latent_high(j)
                key_weights_high(0)
                rotary_squares(0, 0)
                key_square(0)
                keys()
                roots(0, 0)
                query_weights_high(1, 1)
                key_weights_high(1)
                keys_high(0)
                attend(0, 0, True)
                attend(1, 1, True)
                with act.Fori(1, HEADS // 2 - 1) as i:
                    for b in range(2):
                        attend(2 * i + b, b, True)
                attend(HEADS - 2, 0, True, more=False)
                attend(HEADS - 1, 1, False)

                out_split(0, 0, 0)
                out_split(0, 1, 1)
                act.wait_ge(s_s[l], HEADS * qt_n)
                for hd in range(HEADS):
                    act.wait_ge(s_om, HEADS * l + hd + 1)
                    copy(act_hi[:, 8 + hd, 0:nq], h[:, 8 + hd, 0:nq]).then_inc(s_ghi, 1)
                act.wait_ge(s_vh, HEADS * (l + 1))
                for k in range(2 * GROUPS):
                    if k in (0, 6):
                        act.wait_ge(s_mi[k // 6], 16 * (l + 1))
                    copy(act_hi[:, k, 0:nq], h[:, k, 0:nq]).then_inc(s_mhi, 1)

                def out_tile(i, j, first=False, last=False):
                    n = 4 * i + j
                    if not (last and j >= 2):
                        act.wait_ge(s_cmm[l], n + 1)
                        out_split(i + (j + 2) // 4, (j + 2) % 4, n + 2)
                    if l == 0:
                        act.wait_ge(s_xnew[0], n + 1)
                        if not (first and j < 2):
                            act.wait_ge(s_sqa[1], n - 1)
                        square(sq_t[j % 2], xt[j]).then_inc(s_sqt[1], 1)
                    else:
                        act.wait_ge(s_otr, n + 1)
                        if not (first and j < 2):
                            act.wait_ge(s_out[j % 2], 32 * i + 16 * (j // 2))
                        copy(o_nat[j % 2], (C, D)[j % 2][:, 0:512].rearrange("p (t n) -> p t n", t=LT)).then_inc(s_oev, 1)

                for j in range(4):
                    out_tile(0, j, first=True)
                with act.Fori(1, 3) as i:
                    for j in range(4):
                        out_tile(i, j)
                for j in range(4):
                    out_tile(3, j, last=True)

        @block.vector
        def _(dve):
            link = Link(dve, s_link)
            tt, ts, stt = nc.vector.tensor_tensor, nc.vector.tensor_scalar, nc.vector.scalar_tensor_tensor
            nc.vector.memset(cond, 0.0).then_inc(s_zero, 1)
            nc.vector.memset(eps[:, :], EPS).then_inc(s_zero, 1)
            nc.vector.memset(ones[:, :], 1.0).then_inc(s_zero, 1)
            link(nc.vector.memset(sq, 0.0))
            with dve.Fori(0, TT // 2) as i:
                for g in range(0, 8, 2):
                    dve.wait_ge(s_xt, 8 * i + g + 1)
                    nc.vector.tensor_copy(h[:, 4 * (g % 4):4 * (g % 4) + 4, bass.ds((2 * i + g // 4) * P, P)],
                                          bank(g % 4).rearrange("p (k t) -> p k t", k=4)).then_inc(s_xt_dve, 1)
            dve.wait_ge(s_part, 2)
            for l in range(DEPTH):
                nc.vector.tensor_copy(par[l][:, :], ps[2 + l][:, 0:PR_N]).then_inc(s_parc, 1)
            dve.wait_ge(s_parc, 2)
            for b in range(2):
                dve.wait_ge(s_sqt[0], b + 1)
                if b:
                    dve.wait_ge(s_sqa[0], b)
                tt(sq, sq, sq_t[b], ALU.add).then_inc(s_sqa[0], 1)
            with dve.Fori(1, KT // 2) as i:
                for b in range(2):
                    dve.wait_ge(s_sqt[0], 2 * i + b + 1)
                    dve.wait_ge(s_sqa[0], 2 * i + b)
                    tt(sq, sq, sq_t[b], ALU.add).then_inc(s_sqa[0], 1)
            for l in range(DEPTH):
                with dve.Fori(0, 6) as i:
                    for b in range(2):
                        dve.wait_ge(s_ada_col, 12 * l + 2 * i + b + 1)
                        for t in range(2):
                            tt(ada_v[l][:, t, bass.ds(8 * i + 4 * b, 4)],
                               D[:, b * 512:b * 512 + 8].rearrange("p (j t) -> p t j", t=2)[:, t],
                               par[l][:, bass.ds(8 * i + 4 * b, 4)], ALU.add).then_inc(s_ada_b, 1)
                dve.wait_ge(s_ada_b, 24 * (l + 1))
                for t in range(2):
                    stt(gain_v[l][:, t], ada_v[l][:, t, KT:2 * KT], 1.0, par[l][:, PR_NORM:PR_NORM + KT],
                        ALU.add, ALU.mult).then_inc(s_gain, 1)

            for l in range(DEPTH):
                nq = q_tok(l)
                qt_n = q_tiles(l)
                dve.wait_ge(s_nroot, l + 1)
                link(nc.vector.reciprocal(inv_root[:, 0:TT], root[:, 0:TT]))
                for t in range(TT):
                    ts(n_diag[:, t * P:(t + 1) * P], ident[:, :], inv_root[:, t:t + 1], None, ALU.mult).then_inc(s_ndiag, 1)
                if l == 0:
                    dve.wait_ge(s_spill, 16)
                streams = ((0, SEQ), (SEQ, CTX))

                def w_low(n):
                    at = at_of(n)
                    dve.wait_ge(s_whi, SPLITS * l + n + 1)
                    if n == T_KROPE:
                        tt(kr_lo, kr_w, w_hi[0].bitcast(F32), ALU.subtract).then_inc(s_wlo, 1)
                    else:
                        tt(w_cols(w_lo, at % 4), w_cols(w_slot, at % 4), w_hi[n % 2].bitcast(F32), ALU.subtract).then_inc(s_wlo, 1)

                def stream_low(k):
                    dve.wait_ge(s_hhi, 2 * (KT * l + k + 1))
                    for t, (a, n) in enumerate(streams):
                        stt(act_lo[:, k, a:a + n], h[:, k, a:a + n], ada[l][:, t * 48 + k:t * 48 + k + 1], hi_f32[:, k, a:a + n],
                            ALU.add, ALU.subtract).then_inc(s_h, 1)

                w_low(0)
                dve.wait_ge(s_nrb, l + 1)
                for k in range(KT):
                    if l > 0 and k % 4 == 0:
                        dve.wait_ge(s_xr[k // 4], 16)
                    for t, (a, n) in enumerate(streams):
                        stt(h[:, k, a:a + n], h[:, k, a:a + n], gain[l][:, t * KT + k:t * KT + k + 1], D[:, a:a + n],
                            ALU.mult, ALU.mult).then_inc(s_hx, 1)
                    if k >= 2:
                        stream_low(k - 2)
                stream_low(KT - 2)
                stream_low(KT - 1)

                with dve.Fori(0, 2) as i:
                    for j in range(4):
                        at = (j + 1) % 4
                        dve.wait_ge(s_whi, SPLITS * l + 2 + 4 * i + j)
                        tt(w_cols(w_lo, at), w_cols(w_slot, at), w_hi[at % 2].bitcast(F32), ALU.subtract).then_inc(s_wlo, 1)

                for b in range(2):
                    dve.wait_ge(s_gst[b], 80 * l + 16)
                link(nc.vector.memset(pad_u, 0.0))
                seqs = seqs_of(l)
                width = PW if l == 0 else LAT0 + SEQ + PAD

                def pool_gate(g):
                    dve.wait_ge(s_pmm, GROUPS * l + g + 1)
                    dve.wait_ge(s_gin[g % 2], 64 * l + 16 * (g // 2) + 16)
                    stt(gate_in[g % 2][:, 0:nq], D[:, 0:nq], par[l][:, PR_POOL + g:PR_POOL + g + 1], gate_in[g % 2][:, 0:nq],
                        ALU.mult, ALU.mult).then_inc(s_pg, 1)

                for g in range(GROUPS):
                    w_low(T_POOL + g + 1)
                    dve.wait_ge(s_mm[l], T_POOL + g + 1)
                    if g >= 1:
                        dve.wait_ge(s_pl[l], g * len(seqs))
                    for k, (a, n, at) in enumerate(seqs):
                        ins = nc.vector.tensor_copy(pad_u[:, at:at + n], ps[g % 2][:, a:a + n])
                        if k < len(seqs) - 1:
                            link(ins)
                    ins.then_inc(s_ev[l], 1)
                    dve.wait_ge(s_ev[l], g + 1)
                    if g >= 1:
                        pool_gate(g - 1)
                    src, dst = pad_u, win[0]
                    link(tt(dst[:, 1:width], src[:, 0:width - 1], src[:, 1:width], ALU.add))
                    lo = 1
                    for lev in range(g):
                        step = 1 << lev
                        src, dst = dst, win[(lev + 1) % 2]
                        a, e = 2 << lev, width - (2 << lev) + 1
                        link(tt(dst[:, a:e], src[:, a - step:e - step], src[:, a + step:e + step], ALU.add))
                    if g >= 1:
                        dve.wait_ge(s_pmm, GROUPS * l + g)
                    dve.wait_ge(s_inv[g % 2], 32 * l + 16 * (g // 2) + 16)
                    for a, n, at in seqs:
                        link(tt(pooled[:, a:a + n], dst[:, at:at + n], inv[g % 2][:, a:a + n], ALU.mult))
                    for k, (a, n, at) in enumerate(seqs):
                        ins = tt(pooled[:, a:a + n], pooled[:, a:a + n], pad_u[:, at:at + n], ALU.subtract)
                        ins.then_inc(s_pl[l], 1)
                w_low(T_FNET + 1)
                pool_gate(GROUPS - 1)
                w_low(T_FNET + 2)
                w_low(T_FNET + 3)
                for g in range(GROUPS):
                    dve.wait_ge(s_fpos, GROUPS * l + g + 1)
                    dve.wait_ge(s_gin[g % 2], 64 * l + 16 * (g // 2) + 48)
                    tt(gate_in[g % 2][:, 0:nq], D[:, 0:nq], gate_in[g % 2][:, 0:nq], ALU.mult).then_inc(s_fg, 1)
                    w_low(T_CQ + g)
                for n in range(T_CKV, T_MLA + 1):
                    w_low(n)

                dve.wait_ge(s_mm[l], T_KROPE + 1)
                stt(u_kr, A[:, 0:TOK], par[l][:, PR_KHR:PR_KHR + 1], rope[:, :], ALU.mult, ALU.mult).then_inc(s_ukr, 1)
                w_low(T_MLA + 1)
                n_tmp = 0
                for j in range(2 * RT):
                    if j % RT:
                        n = nq if j < RT else TOK
                        acc = (sq_q, sq_k)[j // RT]
                        dve.wait_ge(s_csq, 2 * RT * l + j + 1)
                        if n_tmp:
                            dve.wait_ge(s_csa, 2 * (RT - 1) * l + n_tmp)
                        tt(acc[:, 0:n], acc[:, 0:n], sq_c[n_tmp % 2][:, 0:n], ALU.add).then_inc(s_csa, 1)
                        n_tmp += 1
                w_low(T_MLA + 2)
                dve.wait_ge(s_croot, l + 1)
                link(nc.vector.reciprocal(inv_root[:, TT - qt_n:2 * TT], root[:, TT - qt_n:2 * TT]))
                for t in range(qt_n):
                    ts(q_diag[:, t * P:(t + 1) * P], ident[:, :], inv_root[:, TT - qt_n + t:TT - qt_n + t + 1], None,
                       ALU.mult).then_inc(s_cdiag[l], 1)
                for t in range(TT):
                    ts(diag[:, t * P:(t + 1) * P], ident[:, :], inv_root[:, TT + t:TT + t + 1], None, ALU.mult).then_inc(s_cdiag[l], 1)
                w_low(T_MLA + 3)
                dve.wait_ge(s_crb, l + 1)
                for j in range(2 * RT):
                    n, src = (nq, C) if j < RT else (TOK, D)
                    stt(ckk[:, j, 0:n], ckk[:, j, 0:n], par[l][:, PR_QN + j:PR_QN + j + 1], src[:, 0:n],
                        ALU.mult, ALU.mult).then_inc(s_cn, 1)
                for n in range(T_MLA + 4, MM_IN):
                    w_low(n)
                dve.wait_ge(s_mm[l], MM_IN)
                dve.wait_ge(s_krsq, l + 1)
                nc.vector.tensor_copy(kr_sq[0:ROPE, :], kr_sq0[0:ROPE, :]).then_inc(s_ksq, 1)

                def latent_low(j):
                    n = nq if j < RT else TOK
                    if j == RT:
                        dve.wait_ge(s_vmm, TT * (l + 1))
                    dve.wait_ge(s_chi, 2 * RT * l + j + 1)
                    tt(ckk_lo[:, j, 0:n], ckk[:, j, 0:n], (cq_hi, ckv_hi)[j // RT][:, j % RT, 0:n].bitcast(F32),
                       ALU.subtract).then_inc(s_clo, 1)

                def query_weights_low(p, b):
                    dve.wait_ge(s_wqh, 2 * HEADS * l + 2 * p + 1)
                    tt(wq_lo[b], wq[b], wq_hi.bitcast(F32), ALU.subtract).then_inc(s_wql, 1)

                def key_weights_low(p, b):
                    dve.wait_ge(s_wqh, 2 * HEADS * l + 2 * p + 2)
                    tt(wk_lo[b], wk[b], wk_hi.bitcast(F32), ALU.subtract).then_inc(s_wql, 1)

                def queries_low(p, b):
                    dve.wait_ge(s_eqn, 2 * HEADS * l + 2 * p + 2)
                    stt(qn_lo[b][:, 0:nq], C[:, 0:nq], par[l][:, PR_QH:PR_QH + 1], qn_hi[b][:, 0:nq].bitcast(F32),
                        ALU.mult, ALU.subtract).then_inc(s_qnl, 1)

                for j in range(RT):
                    latent_low(j)

                def rotary(p, b):
                    dve.wait_ge(s_pqr, HEADS * l + p + 1)
                    stt(qr[b][:, 0:nq], C[:, 0:nq], par[l][:, PR_QHR:PR_QHR + 1], rope[:, 0:nq], ALU.mult, ALU.mult).then_inc(s_eqr, 1)
                    dve.wait_ge(s_esr, HEADS * l + p + 1)
                    dve.wait_ge(s_eqn, 2 * HEADS * l + 2 * p + 2)
                    tt(sq_q[0:ROPE, 0:nq], sq_q[0:ROPE, 0:nq], sq_r[0:ROPE, 0:nq], ALU.add).then_inc(s_addq, 1)
                    dve.wait_ge(s_qrh, HEADS * l + p + 1)
                    tt(qr_lo[b][:, 0:nq], qr[b][:, 0:nq], qr_hi[b][:, 0:nq].bitcast(F32), ALU.subtract).then_inc(s_qrl, 1)

                def key_squares(p):
                    dve.wait_ge(s_ekn, 2 * HEADS * l + 2 * p + 1)
                    tt(sq_k[0:ROPE, :], sq_k[0:ROPE, :], kr_sq[0:ROPE, :], ALU.add).then_inc(s_addk, 1)

                def inverses(p, b, own):
                    dve.wait_ge(s_root, HEADS * l + p + 1)
                    own(nc.vector.reciprocal(h_inv[b][:, TT - qt_n:2 * TT], h_root[b][:, TT - qt_n:2 * TT]))
                    ts(q_pos[b][:, 0:qt_n], h_inv[b][:, TT - qt_n:TT], SM_SCALE, None, ALU.mult).then_inc(s_qs, 1)
                    ts(q_neg[b][:, 0:qt_n], h_inv[b][:, TT - qt_n:TT], -SM_SCALE, None, ALU.mult).then_inc(s_qs, 1)
                    for t in range(TT):
                        ts(diag[:, t * P:(t + 1) * P], ident[:, :], h_inv[b][:, TT + t:TT + t + 1], None, ALU.mult).then_inc(s_diag, 1)

                def scale_keys(p, b):
                    dve.wait_ge(s_rb, HEADS * l + p + 1)
                    tt(kn, kn, B[:, 0:TOK], ALU.mult).then_inc(s_kn, 1)
                    tt(krh, kr, B[:, 0:TOK], ALU.mult).then_inc(s_kn, 1)

                def keys_low(p):
                    dve.wait_ge(s_khi, 2 * HEADS * l + 2 * p + 1)
                    tt(kn_lo, kn, kn_hi.bitcast(F32), ALU.subtract).then_inc(s_klo, 1)
                    dve.wait_ge(s_khi, 2 * HEADS * l + 2 * p + 2)
                    tt(krh_lo, krh, krh_hi.bitcast(F32), ALU.subtract).then_inc(s_klo, 1)

                GH = 16 * HEADS // 2

                def out_low(i, j):
                    dve.wait_ge(s_whi, SPLITS * l + MM_IN + 4 * i + j + 1)
                    tt(w_cols(w_lo, j), w_cols(w_slot, j), w_hi[j % 2].bitcast(F32), ALU.subtract).then_inc(s_wlo, 1)

                def attend(hd, b, proj, more=True):
                    p, pb = hd + 1, 1 - b
                    own = Link(dve, s_own[l], 1 + (2 * qt_n + 1) * hd)

                    def maxima(q):
                        n = TOK if q < LT else CTX
                        dve.wait_ge(s_s[l], hd * qt_n + q + 1)
                        own(nc.vector.tensor_reduce(top[:, q:q + 1], ps[q % 2][:, 0:n], AX_X, ALU.max))
                        tt(bias[:, q:q + 1], top[:, q:q + 1], q_neg[b][:, q:q + 1], ALU.mult).then_inc(s_nb[l], 1)

                    def normalise(q):
                        n = TOK if q < LT else CTX
                        dve.wait_ge(s_exp[l], hd * qt_n + q + 1)
                        own(nc.vector.reciprocal(inv_total[:, q:q + 1], total[:, q:q + 1]))
                        ts(prob[q % 2][:, 0:n], prob[q % 2][:, 0:n], inv_total[:, q:q + 1], None, ALU.mult).then_inc(s_sc[l], 1)

                    dve.wait_ge(s_qs, 2 * HEADS * l + 2 * hd + 2)
                    maxima(0)
                    if proj:
                        queries_low(p, pb)
                    maxima(1)
                    normalise(0)
                    if proj:
                        rotary(p, pb)
                    normalise(1)
                    maxima(2)
                    normalise(2)
                    maxima(3)
                    normalise(3)
                    for q in range(LT, qt_n):
                        maxima(q)
                    for q in range(LT, qt_n):
                        normalise(q)
                    if proj:
                        key_squares(p)
                    if proj:
                        inverses(p, pb, own)
                        if more:
                            query_weights_low(p + 1, b)
                            key_weights_low(p + 1, b)
                    dve.wait_ge(s_pv, HEADS * l + hd + 1)
                    dve.wait_ge(s_ghin[b], GH * l + 8 * (hd - b) + 16)
                    tt(h[:, bass.ds(8 + hd, 1), 0:nq].rearrange("p a t -> p (a t)"), A[:, 0:nq], gate_h[b][:, 0:nq],
                       ALU.mult).then_inc(s_om, 1)
                    if proj:
                        scale_keys(p, pb)
                        keys_low(p)

                dve.wait_ge(s_kr, l + 1)
                dve.wait_ge(s_ksq, l + 1)
                query_weights_low(0, 0)
                queries_low(0, 0)
                for j in range(RT, 2 * RT):
                    latent_low(j)
                key_weights_low(0, 0)
                rotary(0, 0)
                key_squares(0)
                inverses(0, 0, Link(dve, s_own[l]))
                query_weights_low(1, 1)
                key_weights_low(1, 1)
                scale_keys(0, 0)
                keys_low(0)
                attend(0, 0, True)
                attend(1, 1, True)
                with dve.Fori(1, HEADS // 2 - 1) as i:
                    for b in range(2):
                        attend(2 * i + b, b, True)
                attend(HEADS - 2, 0, True, more=False)
                attend(HEADS - 1, 1, False)

                out_low(0, 0)
                out_low(0, 1)
                for hd in range(HEADS):
                    dve.wait_ge(s_ghi, HEADS * l + hd + 1)
                    tt(act_lo[:, 8 + hd, 0:nq], h[:, 8 + hd, 0:nq], hi_f32[:, 8 + hd, 0:nq], ALU.subtract).then_inc(s_oml, 1)
                for k in range(2 * GROUPS):
                    dve.wait_ge(s_mhi, 2 * GROUPS * l + k + 1)
                    tt(act_lo[:, k, 0:nq], h[:, k, 0:nq], hi_f32[:, k, 0:nq], ALU.subtract).then_inc(s_mlo, 1)

                if l == 0:
                    link(nc.vector.memset(sq, 0.0))

                def out_tile(i, j, first=False, last=False):
                    n = 4 * i + j
                    src = (B, A)[j % 2]
                    dve.wait_ge(s_cmm[l], n + 1)
                    dve.wait_ge(s_xin[j], 64 * l + 16 * i + 16)
                    if l == 0:
                        stt(xt[j][:, SEQ:TOK], src[:, SEQ:TOK], ada[l][:, bass.ds(n + 48 + 2 * KT, 1)], xt[j][:, SEQ:TOK],
                            ALU.mult, ALU.add)
                    stt(xt[j][:, 0:SEQ], src[:, 0:SEQ], ada[l][:, bass.ds(n + 2 * KT, 1)], xt[j][:, 0:SEQ],
                        ALU.mult, ALU.add).then_inc(s_xnew[l], 1)
                    if not (last and j >= 2):
                        out_low(i + (j + 2) // 4, (j + 2) % 4)
                    if l == 0:
                        dve.wait_ge(s_sqt[1], n + 1)
                        if not (first and j == 0):
                            dve.wait_ge(s_sqa[1], n)
                        tt(sq, sq, sq_t[j % 2], ALU.add).then_inc(s_sqa[1], 1)

                for j in range(4):
                    out_tile(0, j, first=True)
                with dve.Fori(1, 3) as i:
                    for j in range(4):
                        out_tile(i, j)
                for j in range(4):
                    out_tile(3, j, last=True)

        @block.tensor
        def _(pe):
            mm, tr = nc.tensor.matmul, nc.tensor.transpose
            pe.wait_ge(s_const, 16 * N_CONST)

            def stream_in(i, first=False):
                for g in range(8):
                    if g % 4 == 0:
                        pe.wait_ge(s_xn[g // 4], 16 * i + 16)
                    if not (first and g < 4):
                        pe.wait_ge((s_xt_dve, s_xt_act)[g % 2], 4 * i + g // 2 - 1)
                    for j in range(4):
                        k = 4 * (g % 4) + j
                        ins = tr(bank(g % 4)[:, j * P:(j + 1) * P], x_nat[g // 4][:, k * P:(k + 1) * P], ident[:, :])
                    ins.then_inc(s_xt, 1)

            stream_in(0, first=True)
            with pe.Fori(1, TT // 2) as i:
                stream_in(i)
            pe.wait_ge(s_par, 16 * N_PAR)
            for l in range(DEPTH):
                tr(ps[2 + l][:, 0:PR_N], par_row[l][0:PR_N, :], ident[0:PR_N, 0:PR_N]).then_inc(s_part, 1)
            pe.wait_ge(s_parc, 2)
            pe.wait_ge(s_cond, 2)

            def ada_chunk(i, b, first=False):
                if not first:
                    pe.wait_ge(s_ada_row, 2 * i + b - 1)
                for hf in range(2):
                    s = 2 * b + hf
                    pe.wait_ge(s_adw[s], 16 * i + 16)
                    for k in range(8):
                        q = k % 4
                        ins = mm(C[32 * q:32 * q + 32, b * 512:(b + 1) * 512], cond[:, 8 * hf + k, :], ada_slot[s][:, k, :],
                                 start=(hf == 0 and k < 4), stop=(hf == 1 and k >= 4))
                    ins.then_inc(s_ada_mm, 1)
                pe.wait_ge(s_ada_row, 2 * i + b + 1)
                if not first:
                    pe.wait_ge(s_ada_b, 4 * i + 2 * b - 2)
                for j in range(4):
                    ins = mm(D[:, b * 512 + 2 * j:b * 512 + 2 * j + 2], ada_row[b][:, j * P:(j + 1) * P], sel[:, :],
                             start=True, stop=True)
                ins.then_inc(s_ada_col, 1)

            ada_chunk(0, 0, first=True)
            ada_chunk(0, 1, first=True)
            with pe.Fori(1, 12) as i:
                for b in range(2):
                    ada_chunk(i, b)

            for l in range(DEPTH):
                nq = q_tok(l)
                qt_n = q_tiles(l)
                pe.wait_ge(s_sqa[l], KT)
                for t in range(TT):
                    ins = mm(A[:, t:t + 1], sq[:, t * P:(t + 1) * P], ones[:, 0:1], start=True, stop=True)
                ins.then_inc(s_ncol, 1)
                pe.wait_ge(s_ndiag, (l + 1) * TT)
                if l == 0:
                    pe.wait_ge(s_ada_b, 48)
                for a, n in parts(TOK):
                    ins = mm(D[:, a:a + n], ones[:, :], n_diag[:, a:a + n], start=True, stop=True)
                ins.then_inc(s_nrb, 1)

                def products(dst, hi, lo, k, ntok, first, last):
                    for c, (w, a_) in enumerate(((hi, act_hi), (hi, act_lo), (lo, act_hi))):
                        for a, n in parts(ntok):
                            ins = mm(dst[:, a:a + n], w[:, k, :], a_[:, k, a:a + n], start=(first and c == 0), stop=(last and c == 2))
                    return ins

                def tile(hi, lo, b_ps, ntok, first=False):
                    for k in range(KT):
                        if first:
                            pe.wait_ge(s_h, 2 * KT * l + 2 * k + 2)
                        ins = products(ps[b_ps], hi, lo, k, ntok, k == 0, k == KT - 1)
                    ins.then_inc(s_mm[l], 1)

                pe.wait_ge(s_wlo, SPLITS * l + 1)
                tile(w_hi[0], w_cols(w_lo, 0), 0, nq, first=True)
                for n in range(1, 8):
                    pe.wait_ge(s_wlo, SPLITS * l + n + 1)
                    tile(w_hi[n % 2], w_cols(w_lo, n % 4), n % 2, nq)

                def in_tile(n, ntok):
                    pe.wait_ge(s_wlo, SPLITS * l + n + 1)
                    if n == T_KROPE + 2:
                        pe.wait_ge(s_krsq, l + 1)
                    tile(w_hi[n % 2], kr_lo if n == T_KROPE else w_cols(w_lo, at_of(n) % 4), n % 2, ntok)

                pe.wait_ge(s_tab[l], 16 * (7 if l == 0 else 5))
                for s in range(2):
                    ins = mm(C[:, s * 512:(s + 1) * 512], chan[:, s * P:(s + 1) * P], fw, start=True, stop=True)
                ins.then_inc(s_cw, 1)

                def pool_product(g):
                    pe.wait_ge(s_pl[l], (g + 1) * (1 if l else 2))
                    if g > 0:
                        pe.wait_ge(s_pg, GROUPS * l + g)
                    for a, n in parts(nq):
                        ins = mm(D[:, a:a + n], pw[:, g, :], pooled[:, a:a + n], start=True, stop=True)
                    ins.then_inc(s_pmm, 1)

                def fourier_channels(g):
                    n = T_FNET + g
                    pe.wait_ge(s_ev[l], GROUPS + g + 1)
                    if g == 0:
                        pe.wait_ge(s_cwc, (l + 1) * 2)
                    if g > 0:
                        pe.wait_ge(s_fab[l], g * (1 if l else 2))
                    for t in range(qt_n):
                        if t == LT:
                            pe.wait_ge(s_pg, (l + 1) * GROUPS)
                            if g > 0:
                                pe.wait_ge(s_fg, GROUPS * l + g)
                        dst = C[:, t * 256:(t + 1) * 256] if t < LT else D[:, (t - LT) * 256:(t - LT + 1) * 256]
                        ins = mm(dst, f_u[g % 2][:, t * P:(t + 1) * P], chan_w[:, g, :], start=True, stop=True)
                    ins.then_inc(s_fch, 1)

                def fourier_positions(g):
                    pe.wait_ge(s_fab[l], (g + 1) * (1 if l else 2))
                    pe.wait_ge(s_pg, (l + 1) * GROUPS)
                    if g > 0:
                        pe.wait_ge(s_fg, GROUPS * l + g)
                    for a, n, first_t, n_t, tab in ((0, SEQ, 0, LT, pos_lat), (SEQ, CTX, LT, 2, pos_ctx))[:1 if l else 2]:
                        for t in range(n_t):
                            for s in range(2):
                                ins = mm(D[:, a:a + n], f_ab[:, first_t + t, s * P:(s + 1) * P], tab[:, s, t, :],
                                         start=(t == 0 and s == 0), stop=(t == n_t - 1 and s == 1))
                    ins.then_inc(s_fpos, 1)

                for g in range(GROUPS):
                    in_tile(T_POOL + g, nq)
                    if g >= 1:
                        pool_product(g - 1)
                for m in range(GROUPS + 2):
                    in_tile(T_FNET + m, nq)
                    if m == 0:
                        pool_product(GROUPS - 1)
                    if m >= 2:
                        fourier_positions(m - 2)
                    if 1 <= m <= GROUPS:
                        fourier_channels(m - 1)
                for n in range(T_CQ + 2, T_KROPE):
                    in_tile(n, nq if n < T_CKV else TOK)
                in_tile(T_KROPE, TOK)
                in_tile(T_MLA, nq)
                in_tile(T_MLA + 1, nq)
                pe.wait_ge(s_csa, (l + 1) * (2 * (RT - 1)))
                pe.wait_ge(s_fg, (l + 1) * GROUPS)
                for t in range(qt_n):
                    mm(D[:, TT - qt_n + t:TT - qt_n + t + 1], sq_q[:, t * P:(t + 1) * P], ones[:, 0:1], start=True, stop=True)
                for t in range(TT):
                    ins = mm(D[:, TT + t:TT + t + 1], sq_k[:, t * P:(t + 1) * P], ones[:, 0:1], start=True, stop=True)
                ins.then_inc(s_ccol, 1)
                in_tile(T_MLA + 2, nq)
                pe.wait_ge(s_cdiag[l], qt_n + TT)
                for dst, src, ntok in ((C, q_diag, nq), (D, diag, TOK)):
                    for a, n in parts(ntok):
                        ins = mm(dst[:, a:a + n], ones[:, :], src[:, a:a + n], start=True, stop=True)
                ins.then_inc(s_crb, 1)
                for n in range(T_MLA + 3, MM_IN):
                    in_tile(n, nq)

                pe.wait_ge(s_mgate, HEADS * (l + 1))
                pe.wait_ge(s_ukr, l + 1)
                for a, n in parts(TOK):
                    ins = mm(A[:, a:a + n], dup[:, :], u_kr[:, a:a + n], start=True, stop=True)
                ins.then_inc(s_krm, 1)
                pe.wait_ge(s_cn, (l + 1) * (2 * RT))
                pe.wait_ge(s_w[l][0], W_OUT[0])
                for t in range(TT):
                    if t == 1:
                        pe.wait_ge(s_kr, l + 1)
                    if t >= 2:
                        pe.wait_ge(s_v, TT * l + t - 1)
                    for k in range(RT):
                        for a in range(0, HEADS * VDIM, 512):
                            ins = mm((B, A)[t % 2][:, a:a + 512], ckv[:, k, t * P:(t + 1) * P], v_w[:, k, a:a + 512],
                                     start=(k == 0), stop=(k == RT - 1))
                    ins.then_inc(s_vmm, 1)

                def project(hi, lo, src_hi, src_lo, ntok, done):
                    for k in range(RT):
                        for c, (w, src) in enumerate(((hi, src_hi), (hi, src_lo), (lo, src_hi))):
                            for a, n in parts(ntok):
                                ins = mm(C[:, a:a + n], w[:, k, :], src[:, k, a:a + n], start=(k == 0 and c == 0),
                                         stop=(k == RT - 1 and c == 2))
                    ins.then_inc(done, 1)

                def queries(p, b, first=False):
                    pe.wait_ge(s_wql, 2 * HEADS * l + 2 * p + 1)
                    if first:
                        pe.wait_ge(s_clo, 2 * RT * l + RT)
                    else:
                        pe.wait_ge(s_root, HEADS * l + p)
                    project(wq_hi[:, :, 0:NOPE], wq_lo[b][:, :, 0:NOPE], cq_hi, cq_lo, nq, s_pqn)

                def rotary(p, b):
                    pe.wait_ge(s_qnl, HEADS * l + p + 1)
                    project(wq_hi[:, :, NOPE:NOPE + P], wq_lo[b][:, :, NOPE:NOPE + P], cq_hi, cq_lo, nq, s_pqr)

                def keys(p, b):
                    pe.wait_ge(s_wql, 2 * HEADS * l + 2 * p + 2)
                    pe.wait_ge(s_esr, HEADS * l + p + 1)
                    project(wk_hi, wk_lo[b], ckv_hi, ckv_lo, TOK, s_pkn)

                def sums(p):
                    pe.wait_ge(s_addq, HEADS * l + p + 1)
                    pe.wait_ge(s_addk, HEADS * l + p + 1)
                    pe.wait_ge(s_ekn, 2 * HEADS * l + 2 * p + 2)
                    for t in range(qt_n):
                        mm(C[:, TT - qt_n + t:TT - qt_n + t + 1], sq_q[:, t * P:(t + 1) * P], ones[:, 0:1], start=True, stop=True)
                    for t in range(TT):
                        ins = mm(C[:, TT + t:TT + t + 1], sq_k[:, t * P:(t + 1) * P], ones[:, 0:1], start=True, stop=True)
                    ins.then_inc(s_col, 1)

                def key_row(p):
                    pe.wait_ge(s_diag, TT * HEADS * l + TT * p + TT)
                    for a, n in parts(TOK):
                        ins = mm(B[:, a:a + n], ones[:, :], diag[:, a:a + n], start=True, stop=True)
                    ins.then_inc(s_rb, 1)

                def attend(hd, b, proj, more=True):
                    p, pb = hd + 1, 1 - b

                    def scores(q):
                        if q == 0:
                            pe.wait_ge(s_klo, 2 * HEADS * l + 2 * hd + 2)
                            if not (isinstance(hd, int) and hd == 0):
                                pe.wait_ge(s_om, HEADS * l + hd)
                        if q >= 2:
                            pe.wait_ge(s_exp[l], hd * qt_n + q - 1)
                        for a, n, o in (((0, 512, 0), (512, CTX, 512)) if q < LT else ((SEQ, CTX, 0),)):
                            for c, (wq_, mk) in enumerate((
                                    (qn_hi[b], kn_hi), (qn_hi[b], kn_lo), (qn_lo[b], kn_hi),
                                    (qr_hi[b], krh_hi), (qr_hi[b], krh_lo), (qr_lo[b], krh_hi))):
                                ins = mm(ps[q % 2][:, o:o + n], wq_[:, q * P:(q + 1) * P], mk[:, a:a + n], start=(c == 0), stop=(c == 5))
                        ins.then_inc(s_s[l], 1)

                    def turn(q):
                        pe.wait_ge(s_sc[l], hd * qt_n + q + 1)
                        if q > 0:
                            pe.wait_ge(s_pt[l], hd * qt_n + min(q, LT))
                        at = 0 if q <= LT else 512
                        for t in range(TT if q < LT else 2):
                            ins = tr(D[:, at + t * P:at + (t + 1) * P], prob[q % 2][:, t * P:(t + 1) * P], ident[:, :])
                        ins.then_inc(s_t[l], 1)

                    if proj:
                        queries(p, pb)
                    scores(0)
                    scores(1)
                    if proj:
                        rotary(p, pb)
                    turn(0)
                    scores(2)
                    turn(1)
                    scores(3)
                    turn(2)
                    if qt_n > LT:
                        scores(4)
                        scores(5)
                        turn(3)
                    if proj:
                        keys(p, pb)
                    for q in range(3 if qt_n == LT else LT, qt_n):
                        turn(q)
                    pe.wait_ge(s_pt[l], hd * qt_n + qt_n)
                    pe.wait_ge(s_vh, HEADS * l + hd + 1)
                    for t in range(TT):
                        if t == TT // 2 and proj:
                            sums(p)
                        ins = mm(A[:, 0:SEQ], vh[b][:, t, :], prob_t[:, t, :], start=(t == 0), stop=(t == TT - 1))
                    if qt_n > LT:
                        for t in range(2):
                            ins = mm(A[:, SEQ:TOK], vh[b][:, LT + t, :], prob_tc[:, t, :], start=(t == 0), stop=(t == 1))
                    ins.then_inc(s_pv, 1)
                    if proj:
                        key_row(p)

                queries(0, 0, first=True)
                rotary(0, 0)
                keys(0, 0)
                sums(0)
                pe.wait_ge(s_v, (l + 1) * TT)
                key_row(0)
                attend(0, 0, True)
                attend(1, 1, True)
                with pe.Fori(1, HEADS // 2 - 1) as i:
                    for b in range(2):
                        attend(2 * i + b, b, True)
                attend(HEADS - 2, 0, True, more=False)
                attend(HEADS - 1, 1, False)

                def out_turn(i, j, first=False):
                    pe.wait_ge(s_xnew[1], 4 * i + j + 1)
                    if not (first and j < 2):
                        pe.wait_ge(s_oev, 4 * i + j - 1)
                    for t in range(LT):
                        ins = tr((C, D)[j % 2][:, t * P:(t + 1) * P], xt[j][:, t * P:(t + 1) * P], ident[:, :])
                    ins.then_inc(s_otr, 1)

                def out_tiles(i, first=False):
                    for j in range(4):
                        pe.wait_ge(s_wlo, SPLITS * l + MM_IN + 4 * i + j + 1)
                        for m in range(KT):
                            k = (m + 8) % KT
                            if first and j == 0:
                                if k >= 8:
                                    pe.wait_ge(s_oml, HEADS * l + k - 7)
                                else:
                                    pe.wait_ge(s_mlo, 2 * GROUPS * l + k + 1)
                            ins = products((B, A)[j % 2], w_hi[j % 2], w_cols(w_lo, j), k, nq, m == 0, m == KT - 1)
                        ins.then_inc(s_cmm[l], 1)
                        if l == 1 and j >= 1:
                            out_turn(i, j - 1, first)
                    if l == 1:
                        out_turn(i, 3, first)

                out_tiles(0, first=True)
                with pe.Fori(1, 4) as i:
                    out_tiles(i)


def shape_tables():
    pos = np.arange(SEQ)
    inv_freq = (10000.0 ** (-np.arange(ROPE // 4, dtype=np.float32) / np.float32(ROPE // 4))).astype(np.float32)
    ang_r = ((pos // GRID_W).astype(np.float32)[:, None] * inv_freq).astype(np.float32)
    ang_c = ((pos % GRID_W).astype(np.float32)[:, None] * inv_freq).astype(np.float32)
    ang = np.concatenate([ang_r, ang_r, ang_c, ang_c], axis=-1).astype(np.float64).T
    sign = np.where(np.arange(ROPE) % 32 < 16, -1.0, 1.0)[:, None]
    rope = np.zeros((P, TOK), np.float32)
    rope[:ROPE, :SEQ] = np.cos(ang)
    rope[ROPE:, :SEQ] = np.sin(ang) * sign
    rope[:ROPE, SEQ:] = 1.0

    def dft(n):
        a = 2.0 * np.pi * (np.outer(np.arange(n), np.arange(n)) % n) / n
        return np.cos(a), np.sin(a)

    cc, sc = dft(P)
    chan = np.concatenate([cc, sc], axis=1).astype(np.float32)

    def positions(n):
        a, b = dft(n)
        return (np.stack([a, -b]) / np.sqrt(n * P)).astype(np.float32)

    inv = np.zeros((GROUPS, TOK), np.float32)
    for g, w in enumerate((2, 4, 8, 16)):
        for a, n in ((0, SEQ), (SEQ, CTX)):
            t = np.arange(n)
            count = np.clip(t + w - w // 2, 0, n) - np.clip(t - w // 2, 0, n)
            inv[g, a:a + n] = 1.0 / count
    sel = np.zeros((P, 2), np.float32)
    for q in range(4):
        sel[32 * q, 0] = sel[32 * q + 1, 1] = 1.0
    half = np.eye(ROPE, dtype=np.float32)
    return {"k_ident": np.eye(P, dtype=np.float32), "k_sel": sel, "k_dup": np.tile(half, (2, 2)), "k_rope": rope,
            "k_chan": chan, "k_pos_lat": positions(SEQ), "k_pos_ctx": positions(CTX),
            "k_inv": np.tile(inv.reshape(1, -1), (P, 1))}


INPUTS = ["x", "c", "ctx", "c_ctx", "norm_w", "w_ada", "b_ada", "w_in", "pool_w", "pool_scale", "fnet_w", "q_norm_w",
          "w_uq", "kv_norm_w", "w_ukv", "q_head_norm_w", "k_head_norm_w", "w_out"]


def kernel(**inputs):
    from concourse import bacc
    from concourse.bass_utils import run_bass_kernel_spmd

    nc = bacc.Bacc("TRN2", target_bir_lowering=False, num_devices=1)
    arrays, args = {}, []
    tables = shape_tables()
    for name in INPUTS + list(tables):
        a = np.ascontiguousarray(inputs[name] if name in inputs else tables[name])
        arrays[f"in_{name}"] = a
        args.append(nc.dram_tensor(f"in_{name}", a.shape, F32, kind="ExternalInput").ap())
    out = nc.dram_tensor("out_x", (1, SEQ, D_MODEL), F32, kind="ExternalOutput").ap()
    build(nc, *args, out)
    r = run_bass_kernel_spmd(nc, [arrays], core_ids=[0])
    return r.results[0]["out_x"]
```

```python
from contextlib import ExitStack

import numpy as np

import concourse.bass as bass
from concourse import mybir

F32 = mybir.dt.float32
F32R = mybir.dt.float32r
ALU = mybir.AluOpType
ACT = mybir.ActivationFunctionType
AX_X = mybir.AxisListType.X

P = 128
D_MODEL = 2048
SEQ = 512
CTX = 256
TOK = SEQ + CTX
DEPTH = 2
KT = D_MODEL // P
GRID_W = 64
GROUPS = 4
HEADS = 8
NOPE = 128
ROPE = 64
HEAD = NOPE + ROPE
VDIM = 128
RANK = 512
RT = RANK // P
EPS = 1e-6
SM_SCALE = HEAD ** -0.5
TT = TOK // P
LT = SEQ // P
SLOT_N = 256

COL_POOL, COL_POOL_GATE, COL_FNET, COL_FNET_GATE = 0, 512, 1024, 1536
COL_CQ, COL_CKV, COL_KROPE, COL_MLA_GATE = 2048, 2560, 3072, 3136

PR_ADA, PR_NORM, PR_POOL, PR_QN, PR_KVN = 0, 48, 64, 68, 72
PR_QH, PR_QHR, PR_KH, PR_KHR, PR_N = 76, 77, 78, 79, 80

T_GATE, T_POOL, T_FNET, T_CQ, T_CKV, T_KROPE, T_MLA = 0, 8, 12, 16, 20, 24, 25
MM_IN = 33


class Link:

    def __init__(self, engine, sem, base=0):
        self.engine, self.sem, self.base, self.n = engine, sem, base, 0

    def __call__(self, ins):
        self.n += 1
        ins.then_inc(self.sem, 1)
        self.engine.wait_ge(self.sem, self.base + self.n)


def build(nc, x, c, ctx, c_ctx, norm_w, w_ada, b_ada, w_in, pool_w, pool_scale, fnet_w, q_norm_w,
          w_uq, kv_norm_w, w_ukv, q_head_norm_w, k_head_norm_w, w_out,
          k_ident, k_sel, k_dup, k_rope, k_chan, k_pos_lat, k_pos_ctx, k_inv, out):
    xt_dram = [nc.dram_tensor(f"xt{l}", (D_MODEL, TOK), F32, kind="Internal").ap()
               for l in range(DEPTH)]

    gate_dram = [nc.dram_tensor(f"gates{l}", (D_MODEL, TOK), F32, kind="Internal").ap() for l in range(DEPTH)]
    mix_dram = [nc.dram_tensor(f"mixed{l}", (D_MODEL // 2, TOK), F32, kind="Internal").ap() for l in range(DEPTH)]

    with ExitStack() as stack:
        def sb(name, n):
            return stack.enter_context(nc.sbuf_tensor(name, [P, n], F32))

        def sem(name):
            return stack.enter_context(nc.semaphore(name))

        def per_layer(name):
            return [sem(f"{name}{l}") for l in range(DEPTH)]

        def pair(name):
            return [[sem(f"{name}{l}_{b}") for b in range(2)] for l in range(DEPTH)]

        base = (nc.sbuf_base + 63) // 64 * 64
        HALF = KT * TOK
        R_N, W_N, WH_N, C_N, F_N = 2 * HALF, 2 * KT * SLOT_N, 2 * KT * P, (2 * RT + 1) * TOK, 7424
        W_AT, WH_AT, C_AT, F_AT = R_N, R_N + W_N, R_N + W_N + WH_N, R_N + W_N + WH_N + C_N
        sb("regions", R_N + W_N + WH_N + C_N + F_N + 16)

        def place(name, at, n, dt=F32):
            return nc.alloc_sbuf_tensor_at(name, [P, n], dt, offset=base + 4 * at)

        R_, W_ = place("r_region", 0, R_N), place("w_region", W_AT, W_N)
        C_, F_ = place("c_region", C_AT, C_N), place("f_region", F_AT, F_N)

        def view(region, at, n, k=None):
            v = region[:, at:at + n]
            return v if k is None else v.rearrange("p (k n) -> p k n", k=k)

        act_hi = view(place("act_hi", 0, HALF, F32R), 0, HALF, KT)
        act_lo = view(place("act_lo", HALF, HALF, F32R), 0, HALF, KT)
        hi_f32 = act_hi.bitcast(F32)
        h = view(R_, HALF, HALF, KT)
        w_slot = [view(W_, b * KT * SLOT_N, KT * SLOT_N, KT) for b in range(2)]
        w_lo_ = place("w_lo", W_AT, W_N, F32R)
        w_lo = [view(w_lo_, b * KT * SLOT_N, KT * SLOT_N, KT) for b in range(2)]
        w_hi_ = place("w_hi", WH_AT, WH_N, F32R)
        w_hi = [view(w_hi_, b * KT * P, KT * P, KT) for b in range(2)]
        cq = view(C_, 0, RT * TOK, RT)
        ckv = view(C_, RT * TOK, RT * TOK, RT)
        ckk = view(C_, 0, 2 * RT * TOK, 2 * RT)
        kr = view(C_, 2 * RT * TOK, TOK)
        gate_out = view(C_, 0, 8 * TOK, 8)
        groups_in = view(C_, 0, 2 * GROUPS * TOK, 2 * GROUPS)
        inv = [view(C_, b * TOK, TOK) for b in range(2)]
        gate_in = [view(C_, 1536 + b * TOK, TOK) for b in range(2)]
        PAD = 8
        PW = PAD + SEQ + 2 * PAD + CTX + PAD
        LAT0, CTX0 = PAD, PAD + SEQ + 2 * PAD
        pad_u = view(C_, 3072, PW)
        win = [view(C_, 3072 + PW, PW), view(C_, 3072 + 2 * PW, PW)]
        pooled = view(C_, 3072 + 3 * PW, TOK)
        x_nat = [view(R_, 8192 + b * D_MODEL, D_MODEL) for b in range(2)]
        ada_row = [view(F_, b * 512, 512) for b in range(2)]
        cond = view(F_, 6400, KT * 32, KT)
        ada_slot = [view(W_, 0, 4096, 8), view(W_, 4096, 4096, 8), view(R_, 0, 4096, 8), view(R_, 4096, 4096, 8)]
        ada_part = [view(F_, b * 2048, 2048, 4) for b in range(2)]
        ada_row1 = view(F_, 4608, 512)
        par_row = [view(F_, 6144 + l * P, P) for l in range(DEPTH)]
        xt = [view(F_, b * TOK, TOK) for b in range(4)]
        sq = view(F_, 3072, TOK)
        sq_t = [view(F_, 3840 + b * TOK, TOK) for b in range(2)]
        n_diag = view(F_, 5376, TOK)
        o_nat = [view(F_, 6144 + b * 512, 512, LT) for b in range(2)]
        pos_lat = view(F_, 0, 2 * LT * SEQ).rearrange("p (s k n) -> p s k n", s=2, k=LT)
        pos_ctx = view(F_, 4096, 2 * 2 * CTX).rearrange("p (s k n) -> p s k n", s=2, k=2)
        chan = view(F_, 5120, 256)
        chan_w = view(F_, 5376, GROUPS * 256, GROUPS)
        fw = view(F_, 6400, GROUPS * P)
        pw = view(F_, 6912, GROUPS * P, GROUPS)
        f_u = [view(C_, 3072 + b * TOK, TOK) for b in range(2)]
        f_ab = view(C_, 4608, TT * 256, TT)
        kr_w = view(F_, 0, KT * P, KT)
        kr_lo = view(place("kr_lo", F_AT, KT * P, F32R), 0, KT * P, KT)
        prob = [view(F_, b * TOK, TOK) for b in range(2)]
        prob_t = view(F_, 1536, TT * SEQ, TT)
        prob_tc = view(F_, 4608, 2 * CTX, 2)
        sq_q, sq_k, diag = view(F_, 5120, TOK), view(F_, 5888, TOK), view(F_, 6656, TOK)
        u_kr, sq_c, q_diag = prob[0], [prob[1], diag], view(F_, 1536, TOK)
        gate_st = [view(F_, 2304 + b * TOK, TOK) for b in range(2)]
        kr_sq0 = view(F_, 3840, TOK)
        v_all = view(R_, 0, TT * HEADS * VDIM, TT)
        qn_hi, qr_hi = ([act_hi[:, 8 + 2 * j + b, :] for b in range(2)] for j in range(2))
        qn_lo, qr_lo = ([act_lo[:, 2 * j + b, :] for b in range(2)] for j in range(2))
        qr = [h[:, 2 + b, :] for b in range(2)]
        kn, kn_hi, kn_lo = h[:, 4, :], act_hi[:, 12, :], act_lo[:, 4, :]
        krh, krh_hi, krh_lo = h[:, 5, :], act_hi[:, 13, :], act_lo[:, 5, :]
        gate_h = [view(R_, HALF + (6 + b) * TOK, TOK) for b in range(2)]
        sq_r, kr_sq = view(R_, 15 * TOK, TOK), view(R_, HALF + 15 * TOK, TOK)
        vh = [view(R_, 14 * TOK, TOK, TT), view(W_, 7168, TOK, TT)]
        v_w = view(W_, 0, 4096, RT)
        wq = [view(W_, 4096 + b * 1536, 1024, RT) for b in range(2)]
        wk = [view(W_, 4096 + b * 1536 + 1024, 512, RT) for b in range(2)]
        wq_lo = [view(w_lo_, 4096 + b * 1536, 1024, RT) for b in range(2)]
        wk_lo = [view(w_lo_, 4096 + b * 1536 + 1024, 512, RT) for b in range(2)]
        cq_hi, wq_hi = view(w_hi_, 0, RT * TOK, RT), view(w_hi_, RT * TOK, 1024, RT)
        ckv_hi, wk_hi = view(w_lo_, 0, RT * TOK, RT), view(w_lo_, RT * TOK, 512, RT)
        ckk_lo = view(place("ckk_lo", C_AT, 2 * RT * TOK, F32R), 0, 2 * RT * TOK, 2 * RT)
        cq_lo, ckv_lo = ckk_lo[:, 0:RT], ckk_lo[:, RT:2 * RT]

        ident, dup, ones = sb("ident", P), sb("dup", P), sb("ones", P)
        sel = sb("sel", 2)
        rope = sb("rope", TOK)
        c_in = sb("c_in", 2 * KT)
        par = [sb(f"par{l}", PR_N) for l in range(DEPTH)]
        ada = [sb(f"ada{l}", 2 * 48) for l in range(DEPTH)]
        gain = [sb(f"gain{l}", 2 * KT) for l in range(DEPTH)]
        eps = sb("eps", 1)
        root, inv_root = sb("root", 12), sb("inv_root", 12)
        h_root = [sb(f"h_root{b}", 12) for b in range(2)]
        h_inv = [sb(f"h_inv{b}", 12) for b in range(2)]
        q_pos = [sb(f"q_pos{b}", 6) for b in range(2)]
        q_neg = [sb(f"q_neg{b}", 6) for b in range(2)]
        top, bias, total, inv_total = sb("top", 6), sb("bias", 6), sb("total", 6), sb("inv_total", 6)
        ada_v = [a[:, :].rearrange("p (t j) -> p t j", t=2) for a in ada]
        gain_v = [g[:, :].rearrange("p (t j) -> p t j", t=2) for g in gain]

        ps = [stack.enter_context(nc.psum_tensor(f"ps{i}", [P, 1024], F32)) for i in range(4)]
        A, B, C, D = ps

        def bank(i):
            return ps[i // 2][:, (i % 2) * 512:(i % 2) * 512 + 512]

        consts_loaded, params_loaded, zeros_set, cond_ready = sem("consts_loaded"), sem("params_loaded"), sem("zeros_set"), sem("cond_ready")
        tokens_loaded = [sem(f"tokens_loaded{b}") for b in range(2)]
        params_turned, params_copied = sem("params_turned"), sem("params_copied")
        tokens_turned, tokens_copied_dve, tokens_copied_act = sem("tokens_turned"), sem("tokens_copied_dve"), sem("tokens_copied_act")
        w_ada_loaded = [sem(f"w_ada_loaded{b}") for b in range(4)]
        ada_multiplied, ada_row_copied, ada_column_ready, ada_added = sem("ada_multiplied"), sem("ada_row_copied"), sem("ada_column_ready"), sem("ada_added")
        gain_ready = sem("gain_ready")
        stream_spilled = sem("stream_spilled")
        dve_own = sem("dve_own")
        stream_squared, stream_square_added = per_layer("stream_squared"), per_layer("stream_square_added")
        stream_low_ready = sem("stream_low_ready")
        (stream_sums_ready, stream_root_ready, stream_diag_ready, stream_row_ready, stream_scaled) = map(sem, (
            "stream_sums_ready", "stream_root_ready", "stream_diag_ready", "stream_row_ready",
            "stream_scaled"))
        w_loaded, in_tile_done, in_tile_copied = pair("w_loaded"), per_layer("in_tile_done"), per_layer("in_tile_copied")
        pool_w_loaded = sem("pool_w_loaded")
        tables_loaded, inv_loaded = per_layer("tables_loaded"), [sem(f"inv_loaded{b}") for b in range(2)]
        pooled_ready, pool_product_done, pool_gated = per_layer("pooled_ready"), sem("pool_product_done"), sem("pool_gated")
        (chan_w_done, chan_w_copied, fourier_channels_done, fourier_positions_done, fourier_gated) = map(sem, (
            "chan_w_done", "chan_w_copied", "fourier_channels_done", "fourier_positions_done",
            "fourier_gated"))
        fourier_ab_copied = per_layer("fourier_ab_copied")
        (kr_w_loaded, kr_w_swapped, rotary_key_read, rotary_key_squared) = map(sem, (
            "kr_w_loaded", "kr_w_swapped", "rotary_key_read", "rotary_key_squared"))
        (latent_squared, latent_square_added, latent_sums_ready, latent_root_ready, latent_rows_ready,
         latent_normed) = map(sem, (
            "latent_squared", "latent_square_added", "latent_sums_ready", "latent_root_ready",
            "latent_rows_ready", "latent_normed"))
        latent_diag_ready = per_layer("latent_diag_ready")
        (rotary_key_summed, rotary_key_ready, values_multiplied, values_copied) = map(sem, (
            "rotary_key_summed", "rotary_key_ready", "values_multiplied", "values_copied"))
        head_w_loaded = [sem(f"head_w_loaded{b}") for b in range(2)]
        (head_w_swapped, query_copied, key_copied, softmax_scale_ready, key_scaled, key_diag_ready) = map(sem, (
            "head_w_swapped", "query_copied", "key_copied", "softmax_scale_ready", "key_scaled",
            "key_diag_ready"))
        scores_ready, max_ready, exp_ready, probs_normalised, probs_turned, probs_copied = map(per_layer, ("scores_ready", "max_ready", "exp_ready", "probs_normalised", "probs_turned", "probs_copied"))
        query_projected, query_rotary_projected, key_projected, query_rotated, query_rotary_squared, query_squares_ready, key_squares_ready = map(
            sem, ("query_projected", "query_rotary_projected", "key_projected", "query_rotated", "query_rotary_squared", "query_squares_ready", "key_squares_ready"))
        (head_sums_ready, head_roots_ready, key_row_ready, attended, head_gated, head_values_ready) = map(sem, (
            "head_sums_ready", "head_roots_ready", "key_row_ready", "attended", "head_gated",
            "head_values_ready"))
        residual_loaded = [sem(f"residual_loaded{b}") for b in range(4)]
        out_tile_done, new_stream_ready = per_layer("out_tile_done"), per_layer("new_stream_ready")
        w_high_ready, w_low_ready = sem("w_high_ready"), sem("w_low_ready")
        stream_high_ready, head_high_ready = sem("stream_high_ready"), sem("head_high_ready")
        group_gate_ready, gate_stored = sem("group_gate_ready"), [sem(f"gate_stored{b}") for b in range(2)]
        head_gate_ready = sem("head_gate_ready")
        gate_loaded, group_stored = [sem(f"gate_loaded{b}") for b in range(2)], [sem(f"group_stored{b}") for b in range(2)]
        head_gate_loaded = [sem(f"head_gate_loaded{b}") for b in range(2)]
        groups_loaded, group_high_ready, group_low_ready = sem("groups_loaded"), sem("group_high_ready"), sem("group_low_ready")
        head_low_ready, key_square_moved = sem("head_low_ready"), sem("key_square_moved")
        (latent_high_ready, latent_low_ready, head_w_high_ready, head_w_low_ready) = map(sem, (
            "latent_high_ready", "latent_low_ready", "head_w_high_ready", "head_w_low_ready"))
        (query_low_ready, query_rotary_high_ready, query_rotary_low_ready, key_high_ready, key_low_ready) = map(sem, (
            "query_low_ready", "query_rotary_high_ready", "query_rotary_low_ready", "key_high_ready",
            "key_low_ready"))
        stream_loaded = [sem(f"stream_loaded{b}") for b in range(4)]
        new_stream_stored = [sem(f"new_stream_stored{b}") for b in range(4)]
        dve_own_head = per_layer("dve_own_head")
        out_turned, out_copied = sem("out_turned"), sem("out_copied")
        out_stored = [sem(f"out_stored{b}") for b in range(2)]

        SPLITS = MM_IN + KT

        N_CONST = 6
        N_PAR = 2 * (5 + 2 * 6)

        def q_tok(l):
            return TOK if l < DEPTH - 1 else SEQ

        def q_tiles(l):
            return q_tok(l) // P

        def parts(n):
            return [(a, min(n - a, 512)) for a in range(0, n, 512)]

        def at_of(n):
            return n - 1 if n > T_KROPE else n

        def w_cols(w, j):
            return w[j // 2][:, :, (j % 2) * P:(j % 2) * P + P]

        def seqs_of(l):
            return ((0, SEQ, LAT0), (SEQ, CTX, CTX0))[:1 if l else 2]

        streams = ((0, SEQ), (SEQ, CTX))

        def stream_at(l, k, t):
            return 2 * KT * l + (2 * k + t + 1 if l == 0 else KT * t + k + 1)

        def ada_cols(i):
            return D[:, 960 + 8 * (i % 2):968 + 8 * (i % 2)]

        ADA_CHUNKS = 3 * D_MODEL // 512
        ADA_0 = 2 * ADA_CHUNKS

        W_OUT = (16 * (8 + RT), 16 * 8)

        block = stack.enter_context(nc.Block())

        @block.sync
        def _(sp):
            for dst, src in ((ident[:, :], k_ident), (dup[:, :], k_dup), (sel[:, :], k_sel), (rope[:, :], k_rope),
                             (c_in[:, 0:KT], c.rearrange("a (p k) -> (a p) k", k=KT)),
                             (c_in[:, KT:2 * KT], c_ctx.rearrange("(p k) -> p k", k=KT))):
                sp.dma_start(dst, src).then_inc(consts_loaded, 16)

            def ada_load(l, i, s):
                src = w_ada[l].rearrange("(p k) n -> p k n", k=KT)
                sp.dma_start(ada_slot[s], src[:, (s % 2) * 8:(s % 2) * 8 + 8, bass.ds((2 * i + s // 2) * 512, 512)])\
                  .then_inc(w_ada_loaded[s], 16)

            for t in range(TT):
                if t >= 2:
                    sp.wait_ge(tokens_turned, 4 * (t - 1))
                src = x[0, t * P:(t + 1) * P, :] if t < LT else ctx[0, (t - LT) * P:(t - LT + 1) * P, :]
                sp.dma_start(x_nat[t % 2], src).then_inc(tokens_loaded[t % 2], 16)
                if 1 <= t <= 4:
                    ada_load(0, 0, t - 1)

            for s in range(4):
                sp.wait_ge(ada_multiplied, s + 1)
                ada_load(0, 1, s)
            with sp.Fori(2, 6) as i:
                for s in range(4):
                    sp.wait_ge(ada_multiplied, 4 * i + s - 3)
                    ada_load(0, i, s)

            for l in range(DEPTH):
                src = w_in[l].rearrange("(k p) n -> p k n", p=P)

                def load_in(m, col, done, b):
                    if m >= 2:
                        sp.wait_ge(in_tile_done[l], done)
                    sp.dma_start(w_slot[b], src[:, :, bass.ds(col, SLOT_N)]).then_inc(w_loaded[l][b], 16)

                if l == 0:
                    sp.wait_ge(ada_multiplied, ADA_0 - 3)
                else:
                    sp.wait_ge(out_tile_done[l - 1], KT - 2)
                load_in(0, COL_POOL_GATE, 0, 0)
                if l == 0:
                    sp.wait_ge(ada_multiplied, ADA_0 - 2)
                else:
                    sp.wait_ge(out_tile_done[l - 1], KT)
                load_in(1, COL_POOL_GATE + SLOT_N, 0, 1)
                cols = [COL_POOL_GATE, COL_POOL_GATE + SLOT_N, COL_FNET_GATE, COL_FNET_GATE + SLOT_N]
                for col in (COL_POOL, COL_FNET, COL_CQ, COL_CKV):
                    cols += [col, col + SLOT_N]
                if l == 0:
                    src_a = w_ada[1].rearrange("(p k) n -> p k n", k=KT)
                    sp.wait_ge(stream_sums_ready, 1)
                    for i in range(ADA_CHUNKS):
                        for q in range(4):
                            if q == 2 and i % 2 == 0 and i >= 2:
                                m = i // 2 + 1
                                load_in(m, cols[m], 2 * m - 2, m % 2)
                            if 4 * i + q >= 2:
                                sp.wait_ge(ada_multiplied, ADA_0 + 4 * i + q - 1)
                            sp.dma_start(ada_part[q % 2], src_a[:, 4 * q:4 * q + 4, i * 512:(i + 1) * 512]).then_inc(w_ada_loaded[q % 2], 16)
                for m in range(7 if l == 0 else 2, 12):
                    load_in(m, cols[m], 2 * m - 2, m % 2)
                sp.wait_ge(fourier_positions_done, (l + 1) * GROUPS)
                sp.dma_start(kr_w[:, :, 0:ROPE], src[:, :, COL_KROPE:COL_KROPE + ROPE]).then_inc(kr_w_loaded, 16)
                for j, done in enumerate((22, 24, 27, 29)):
                    load_in(12 + j, COL_MLA_GATE + j * SLOT_N, done, j % 2)
                sp.wait_ge(in_tile_done[l], 31)
                for k in range(RT):
                    src_v = w_ukv[l, k * P:(k + 1) * P, :].rearrange("p (h n) -> p h n", h=HEADS)[:, :, NOPE:]
                    sp.dma_start(v_w[:, k, :].rearrange("p (h n) -> p h n", h=HEADS), src_v).then_inc(w_loaded[l][0], 16)

                def head_load(hd, b):
                    sp.dma_start(wq[b][:, :, 0:HEAD],
                                 w_uq[l].rearrange("(k p) n -> p k n", p=P)[:, :, bass.ds(hd * HEAD, HEAD)]).then_inc(head_w_loaded[b], 16)
                    sp.dma_start(wk[b],
                                 w_ukv[l].rearrange("(k p) n -> p k n", p=P)[:, :, bass.ds(hd * (NOPE + VDIM), NOPE)])\
                      .then_inc(head_w_loaded[b], 16)

                sp.wait_ge(in_tile_done[l], MM_IN)
                for b in range(2):
                    head_load(b, b)
                with sp.Fori(1, HEADS // 2) as i:
                    for b in range(2):
                        sp.wait_ge(key_projected, HEADS * l + 2 * i + b - 1)
                        head_load(2 * i + b, b)
                src_o = w_out[l].rearrange("(k p) n -> p k n", p=P)
                sp.wait_ge(key_projected, HEADS * (l + 1))
                sp.dma_start(w_slot[0], src_o[:, :, 0:SLOT_N]).then_inc(w_loaded[l][0], 16)
                sp.wait_ge(attended, HEADS * (l + 1))
                sp.dma_start(w_slot[1], src_o[:, :, SLOT_N:2 * SLOT_N]).then_inc(w_loaded[l][1], 16)
                with sp.Fori(1, 4) as i:
                    for b in range(2):
                        sp.wait_ge(out_tile_done[l], 4 * i + 2 * b - 2)
                        sp.dma_start(w_slot[b], src_o[:, :, bass.ds((2 * i + b) * SLOT_N, SLOT_N)]).then_inc(w_loaded[l][b], 16)

        @block.gpsimd
        def _(pool):
            pool.wait_ge(tokens_copied_dve, 2 * TT)
            pool.wait_ge(tokens_copied_act, 2 * TT)
            pool.dma_start(xt_dram[0].rearrange("(k p) t -> p k t", p=P), h).then_inc(stream_spilled, 16)

            for l in range(DEPTH):
                nt = q_tok(l)
                rows = gate_dram[l].rearrange("(k p) t -> p k t", p=P)

                pool.wait_ge(stream_row_ready, l + 1)
                pool.dma_start(pw, pool_w[l].rearrange("g c d -> c g d")).then_inc(pool_w_loaded, 16)

                def fourier_tables():
                    pool.dma_start(fw.rearrange("p (g d) -> p g d", g=GROUPS), fnet_w[l].rearrange("g c d -> c g d")).then_inc(tables_loaded[l], 16)
                    pool.dma_start(chan, k_chan).then_inc(tables_loaded[l], 16)
                    if l == 0:
                        pool.wait_ge(ada_column_ready, 2 * ADA_CHUNKS)
                    for s in range(2):
                        pool.dma_start(pos_lat[:, s], k_pos_lat[s].rearrange("(k p) n -> p k n", p=P)).then_inc(tables_loaded[l], 16)
                        if l < DEPTH - 1:
                            pool.dma_start(pos_ctx[:, s], k_pos_ctx[s].rearrange("(k p) n -> p k n", p=P)).then_inc(tables_loaded[l], 16)

                if l > 0:
                    fourier_tables()

                for b in range(2):
                    pool.wait_ge(group_gate_ready, 8 * l + 4 * b + 4)
                    pool.dma_start(rows[:, 4 * b:4 * b + 4, 0:nt], gate_out[:, 4 * b:4 * b + 4, 0:nt]).then_inc(gate_stored[b], 16)
                for b in range(2):
                    pool.wait_ge(gate_stored[b], 80 * l + 16)

                def group_in(g):
                    if g < GROUPS:
                        pool.dma_start(inv[g % 2], k_inv[:, g * TOK:(g + 1) * TOK]).then_inc(inv_loaded[g % 2], 16)
                    pool.dma_start(gate_in[g % 2][:, 0:nt], gate_dram[l][g * P:(g + 1) * P, 0:nt]).then_inc(gate_loaded[g % 2], 16)

                group_in(0)
                group_in(1)
                for g in range(2 * GROUPS):
                    if g == 2 and l == 0:
                        pool.wait_ge(ada_multiplied, ADA_0 + 4 * ADA_CHUNKS)
                        fourier_tables()
                    if g < GROUPS:
                        pool.wait_ge(pool_gated, GROUPS * l + g + 1)
                    else:
                        pool.wait_ge(fourier_gated, GROUPS * l + g - GROUPS + 1)
                    pool.dma_start(mix_dram[l][g * P:(g + 1) * P, 0:nt], gate_in[g % 2][:, 0:nt]).then_inc(group_stored[g % 2], 16)
                    if g + 2 < 2 * GROUPS:
                        pool.wait_ge(group_stored[g % 2], 64 * l + 16 * (g // 2) + 16)
                        group_in(g + 2)

                def swap(dst, src, s):
                    d = dst.rearrange("p k (a b c) -> p k a b c", a=2, b=2)
                    o = src.rearrange("p k (a b c) -> p k a b c", a=2, b=2)
                    for b in range(2):
                        nc.gpsimd.tensor_copy(d[:, :, :, b], o[:, :, :, 1 - b]).then_inc(s, 1)

                pool.wait_ge(kr_w_loaded, (l + 1) * 16)
                swap(kr_w[:, :, ROPE:P], kr_w[:, :, 0:ROPE], kr_w_swapped)

                for q in range(HEADS):
                    pool.wait_ge(head_gate_ready, HEADS * l + q + 1)
                    pool.dma_start(rows[:, 8 + q, 0:nt], gate_st[q % 2][:, 0:nt]).then_inc(gate_stored[q % 2], 16)
                for b in range(2):
                    pool.wait_ge(gate_stored[b], 80 * l + 80)
                pool.wait_ge(in_tile_done[l], MM_IN)

                def gate_load(hd):
                    pool.dma_start(gate_h[hd % 2][:, 0:nt], gate_dram[l][(8 + hd) * P:(9 + hd) * P, 0:nt]).then_inc(head_gate_loaded[hd % 2], 16)

                gate_load(0)
                gate_load(1)
                for hd in range(HEADS):
                    b = hd % 2
                    pool.wait_ge(head_w_loaded[b], 16 * HEADS * l + 32 * (hd // 2) + 32)
                    swap(wq[b][:, :, HEAD:HEAD + ROPE], wq[b][:, :, NOPE:HEAD], head_w_swapped)
                    if hd == 0:
                        pool.wait_ge(values_copied, (l + 1) * TT)
                    if hd >= 2:
                        pool.wait_ge(attended, HEADS * l + hd - 1)
                    nc.gpsimd.tensor_copy(vh[b], v_all[:, :, hd * VDIM:(hd + 1) * VDIM]).then_inc(head_values_ready, 1)
                    if hd >= 2:
                        pool.wait_ge(head_gated, HEADS * l + hd - 1)
                        gate_load(hd)

                mixed = mix_dram[l].rearrange("(k p) t -> p k t", p=P)
                for b in range(2):
                    pool.wait_ge(group_stored[b], 64 * (l + 1))
                pool.wait_ge(key_projected, HEADS * (l + 1))
                pool.dma_start(groups_in[:, :, 0:nt], mixed[:, :, 0:nt]).then_inc(groups_loaded, 16)
                if l == 0:
                    pool.wait_ge(stream_spilled, 16)
                pool.wait_ge(attended, HEADS * (l + 1))
                for b in range(4):
                    pool.dma_start(xt[b][:, 0:nt], xt_dram[l][b * P:(b + 1) * P, 0:nt]).then_inc(residual_loaded[b], 16)

                def tile_out(i, b, load_next):
                    n = 4 * i + b
                    if l == 0:
                        pool.wait_ge(new_stream_ready[0], n + 1)
                        pool.dma_start(xt_dram[1][bass.ds(n * P, P), :], xt[b]).then_inc(new_stream_stored[b], 16)
                        if load_next:
                            pool.wait_ge(stream_squared[1], n + 1)
                            pool.wait_ge(new_stream_stored[b], 16 * i + 16)
                    else:
                        pool.wait_ge(out_copied, n + 1)
                    if load_next:
                        pool.dma_start(xt[b][:, 0:nt], xt_dram[l][bass.ds(n * P + 4 * P, P), 0:nt]).then_inc(residual_loaded[b], 16)
                    if l == 1:
                        pool.dma_start(out[0].rearrange("(t p) n -> p t n", p=P)[:, :, bass.ds(n * P, P)],
                                       o_nat[b % 2]).then_inc(out_stored[b % 2], 16)

                with pool.Fori(0, 3) as i:
                    for b in range(4):
                        tile_out(i, b, True)

                def stream_back(b):
                    for a in range(4):
                        pool.wait_ge(new_stream_stored[a], 16 * b + 16)
                    pool.dma_start(h[:, 4 * b:4 * b + 4, :], xt_dram[1].rearrange("(k p) t -> p k t", p=P)[:, 4 * b:4 * b + 4, :])\
                        .then_inc(stream_loaded[b], 16)

                for b in range(3):
                    tile_out(3, b, False)
                if l == 0:
                    pool.wait_ge(out_tile_done[0], KT)
                    for b in range(3):
                        stream_back(b)
                tile_out(3, 3, False)
                if l == 0:
                    stream_back(3)
            for b in range(2):
                pool.wait_ge(out_stored[b], 16 * KT // 2)

        @block.scalar
        def _(act):
            def copy(o, i):
                return nc.scalar.activation(o, i, ACT.Copy)

            def square(o, i):
                return nc.scalar.activation(o, i, ACT.Square)

            for l in range(DEPTH):
                row = par_row[l]

                def load(r, n, src):
                    act.dma_start(row[r:r + n, :], src.rearrange("(r n) -> r n", n=P)).then_inc(params_loaded, 16)

                load(PR_ADA, 48, b_ada[l])
                load(PR_NORM, KT, norm_w[l])
                load(PR_POOL, GROUPS, pool_scale[l])
                load(PR_QN, RT, q_norm_w[l])
                load(PR_KVN, RT, kv_norm_w[l])
                for r, src in ((PR_QH, q_head_norm_w[l]), (PR_KH, k_head_norm_w[l])):
                    load(r, 1, src[0:NOPE])
                    act.dma_start(row[r + 1:r + 2, 0:ROPE], src[NOPE:HEAD].rearrange("(r n) -> r n", r=1)).then_inc(params_loaded, 16)
                    for q in range(4):
                        a = NOPE + 16 * (q ^ 1)
                        act.dma_start(row[r + 1:r + 2, ROPE + 16 * q:ROPE + 16 * q + 16],
                                       src[a:a + 16].rearrange("(r n) -> r n", r=1)).then_inc(params_loaded, 16)
            act.wait_ge(zeros_set, 3)
            act.wait_ge(consts_loaded, 16 * N_CONST)
            for t in range(2):
                nc.scalar.activation(cond[:, :, t], c_in[:, t * KT:(t + 1) * KT], ACT.Silu).then_inc(cond_ready, 1)
            with act.Fori(0, TT // 2) as i:
                for g in range(1, 8, 2):
                    act.wait_ge(tokens_turned, 8 * i + g + 1)
                    copy(h[:, 4 * (g % 4):4 * (g % 4) + 4, bass.ds((2 * i + g // 4) * P, P)],
                         bank(g % 4).rearrange("p (k t) -> p k t", k=4)).then_inc(tokens_copied_act, 1)
            act.wait_ge(tokens_copied_dve, 2 * TT)
            act.wait_ge(tokens_copied_act, 2 * TT)

            def stream_square(k, b):
                square(sq_t[b], h[:, bass.ds(k, 1), :].rearrange("p a t -> p (a t)")).then_inc(stream_squared[0], 1)

            stream_square(0, 0)
            stream_square(1, 1)
            with act.Fori(1, KT // 2) as i:
                for b in range(2):
                    act.wait_ge(stream_square_added[0], 2 * i + b - 1)
                    stream_square(2 * i + b, b)

            def ada_copy(i, b):
                act.wait_ge(ada_multiplied, 4 * i + 2 * b + 2)
                copy(ada_row[b], C[:, b * 512:(b + 1) * 512]).then_inc(ada_row_copied, 1)

            ada_copy(0, 0)
            ada_copy(0, 1)
            with act.Fori(1, ADA_CHUNKS // 2) as i:
                for b in range(2):
                    act.wait_ge(ada_column_ready, 2 * i + b - 1)
                    ada_copy(i, b)

            for l in range(DEPTH):
                nq = q_tok(l)
                qt_n = q_tiles(l)
                act.wait_ge(stream_sums_ready, l + 1)
                nc.scalar.activation(root[:, 0:TT], A[:, 0:TT], ACT.Sqrt, bias=eps[:, 0:1], scale=1.0 / D_MODEL).then_inc(stream_root_ready, 1)
                act.wait_ge(gain_ready, 2 * (l + 1))

                def split(n):
                    at = at_of(n)
                    if n == T_KROPE:
                        act.wait_ge(kr_w_swapped, 2 * (l + 1))
                        copy(w_hi[0], kr_w).then_inc(w_high_ready, 1)
                        return
                    if at % 2 == 0:
                        act.wait_ge(w_loaded[l][at % 4 // 2], 16 * (at // 4) + 16)
                    copy(w_hi[n % 2], w_cols(w_slot, at % 4)).then_inc(w_high_ready, 1)

                if l == 0:
                    split(0)
                split(1)

                def stream_high(k, t):
                    a, n = streams[t]
                    act.wait_ge(stream_scaled, stream_at(l, k, t))
                    nc.scalar.activation(act_hi[:, k, a:a + n], h[:, k, a:a + n], ACT.Identity,
                                         bias=ada[l][:, t * 48 + k:t * 48 + k + 1]).then_inc(stream_high_ready, 1)

                for k in range(KT):
                    for t in range(2 if l == 0 else 1):
                        stream_high(k, t)

                def ada_row_copy(i, b):
                    act.wait_ge(ada_multiplied, ADA_0 + 4 * i + 4)
                    copy(ada_row1, C[:, b * 512:(b + 1) * 512]).then_inc(ada_row_copied, 1)

                for n in range(T_POOL):
                    if n > 0:
                        split(n + 1)
                    if l == 1 and n in (1, 2):
                        for k in range(8 * (n - 1), 8 * n):
                            stream_high(k, 1)
                    act.wait_ge(in_tile_done[l], n + 1)
                    nc.scalar.activation(gate_out[:, n, 0:nq], ps[n % 2][:, 0:nq], ACT.Silu).then_inc(group_gate_ready, 1)
                    if l == 0:
                        ada_row_copy(n, n % 2)
                for n in range(T_POOL, T_FNET):
                    if n > T_POOL:
                        act.wait_ge(in_tile_copied[l], n - T_POOL)
                    split(n + 1)
                    if l == 0:
                        ada_row_copy(n, n % 2)
                def fourier_ab(g):
                    act.wait_ge(fourier_channels_done, GROUPS * l + g + 1)
                    if g == 0:
                        act.wait_ge(pool_product_done, (l + 1) * GROUPS)
                    else:
                        act.wait_ge(fourier_positions_done, GROUPS * l + g)
                    copy(f_ab[:, 0:4, :], C[:, :].rearrange("p (t n) -> p t n", t=4)).then_inc(fourier_ab_copied[l], 1)
                    if l == 0:
                        copy(f_ab[:, 4:6, :], D[:, 0:512].rearrange("p (t n) -> p t n", t=2)).then_inc(fourier_ab_copied[l], 1)

                for j in range(GROUPS):
                    if j == 0:
                        act.wait_ge(in_tile_copied[l], GROUPS)
                    split(T_FNET + j + 1)
                    act.wait_ge(in_tile_done[l], T_FNET + j + 1)
                    if j == 0:
                        act.wait_ge(pooled_ready[l], GROUPS * len(seqs_of(l)))
                    if j >= 2:
                        act.wait_ge(fourier_channels_done, GROUPS * l + j - 1)
                    copy(f_u[j % 2][:, 0:nq], ps[j % 2][:, 0:nq]).then_inc(in_tile_copied[l], 1)
                    if j == 0:
                        act.wait_ge(chan_w_done, l + 1)
                        for s in range(2):
                            copy(chan_w[:, :, s * P:(s + 1) * P], C[:, s * 512:(s + 1) * 512].rearrange("p (g d) -> p g d", g=GROUPS))\
                                .then_inc(chan_w_copied, 1)
                    if j >= 1:
                        fourier_ab(j - 1)
                for j in range(2 * RT):
                    n = nq if j < RT else TOK
                    if j < 2 * RT - 1:
                        split(T_CQ + j + 1)
                    act.wait_ge(in_tile_done[l], T_CQ + j + 1)
                    if j == 2:
                        for b in range(2):
                            act.wait_ge(group_stored[b], 64 * (l + 1))
                    if j == RT:
                        act.wait_ge(fourier_positions_done, (l + 1) * GROUPS)
                    copy(ckk[:, j, 0:n], ps[j % 2][:, 0:n]).then_inc(in_tile_copied[l], 1)
                    if j == 0:
                        fourier_ab(GROUPS - 1)
                    if j == 2 * RT - 2:
                        split(T_KROPE)
                split(T_MLA)
                act.wait_ge(in_tile_done[l], T_KROPE + 1)
                act.wait_ge(rotary_key_read, l + 1)
                square(kr_sq0[0:ROPE, :], A[0:ROPE, 0:TOK]).then_inc(rotary_key_squared, 1)
                split(T_MLA + 1)
                act.wait_ge(in_tile_copied[l], GROUPS * 2 + 2 * RT)
                n_tmp = 0
                for j in range(2 * RT):
                    n = nq if j < RT else TOK
                    if j % RT == 0:
                        dst = (sq_q, sq_k)[j // RT]
                    else:
                        if n_tmp >= 2:
                            act.wait_ge(latent_square_added, 2 * (RT - 1) * l + n_tmp - 1)
                        dst = sq_c[n_tmp % 2]
                        n_tmp += 1
                    square(dst[:, 0:n], ckk[:, j, 0:n]).then_inc(latent_squared, 1)

                def gate(n):
                    q = n - T_MLA
                    act.wait_ge(in_tile_done[l], n + 1)
                    if q >= 2:
                        act.wait_ge(gate_stored[q % 2], 80 * l + 16 * (q // 2) + 16)
                    nc.scalar.activation(gate_st[q % 2][:, 0:nq], ps[n % 2][:, 0:nq], ACT.Silu).then_inc(head_gate_ready, 1)

                gate(T_MLA)
                split(T_MLA + 2)
                gate(T_MLA + 1)
                split(T_MLA + 3)
                act.wait_ge(latent_sums_ready, l + 1)
                nc.scalar.activation(root[:, TT - qt_n:2 * TT], D[:, TT - qt_n:2 * TT], ACT.Sqrt,
                                     bias=eps[:, 0:1], scale=1.0 / RANK).then_inc(latent_root_ready, 1)
                for n in range(T_MLA + 2, MM_IN):
                    gate(n)
                    if n + 2 < MM_IN:
                        split(n + 2)
                act.wait_ge(rotary_key_summed, l + 1)
                copy(kr, A[:, 0:TOK]).then_inc(rotary_key_ready, 1)

                def latent_high(j):
                    n = nq if j < RT else TOK
                    act.wait_ge(latent_normed, 2 * RT * l + j + 1)
                    copy((cq_hi, ckv_hi)[j // RT][:, j % RT, 0:n], ckk[:, j, 0:n]).then_inc(latent_high_ready, 1)

                def query_weights_high(p, b):
                    act.wait_ge(head_w_swapped, 2 * HEADS * l + 2 * p + 2)
                    copy(wq_hi, wq[b]).then_inc(head_w_high_ready, 1)

                def key_weights_high(b):
                    copy(wk_hi, wk[b]).then_inc(head_w_high_ready, 1)

                for j in range(RT):
                    latent_high(j)
                for t in range(TT):
                    act.wait_ge(values_multiplied, TT * l + t + 1)
                    copy(v_all[:, t, :], (B, A)[t % 2][:, :]).then_inc(values_copied, 1)
                    if t == 1:
                        query_weights_high(0, 0)

                def queries(p, b):
                    act.wait_ge(query_projected, HEADS * l + p + 1)
                    square(sq_q[:, 0:nq], C[:, 0:nq]).then_inc(query_copied, 1)
                    nc.scalar.activation(qn_hi[b][:, 0:nq], C[:, 0:nq], ACT.Identity, scale=par[l][:, PR_QH:PR_QH + 1]).then_inc(query_copied, 1)

                def rotary_squares(p, b):
                    act.wait_ge(query_rotated, HEADS * l + p + 1)
                    square(sq_r[0:ROPE, 0:nq], C[0:ROPE, 0:nq]).then_inc(query_rotary_squared, 1)
                    copy(qr_hi[b][:, 0:nq], qr[b][:, 0:nq]).then_inc(query_rotary_high_ready, 1)

                def keys_high(p):
                    act.wait_ge(key_scaled, 2 * HEADS * l + 2 * p + 1)
                    copy(kn_hi, kn).then_inc(key_high_ready, 1)
                    act.wait_ge(key_scaled, 2 * HEADS * l + 2 * p + 2)
                    copy(krh_hi, krh).then_inc(key_high_ready, 1)

                def key_square(p):
                    act.wait_ge(key_projected, HEADS * l + p + 1)
                    square(sq_k, C[:, 0:TOK]).then_inc(key_copied, 1)

                def keys():
                    nc.scalar.activation(kn, C[:, 0:TOK], ACT.Identity, scale=par[l][:, PR_KH:PR_KH + 1]).then_inc(key_copied, 1)

                def roots(p, b):
                    act.wait_ge(head_sums_ready, HEADS * l + p + 1)
                    nc.scalar.activation(h_root[b][:, TT - qt_n:2 * TT], C[:, TT - qt_n:2 * TT], ACT.Sqrt,
                                         bias=eps[:, 0:1], scale=1.0 / HEAD).then_inc(head_roots_ready, 1)

                def out_split(i, j, n):
                    if j % 2 == 0:
                        act.wait_ge(w_loaded[l][j // 2], W_OUT[j // 2] + 16 * i + 16)
                    copy(w_hi[j % 2], w_cols(w_slot, j)).then_inc(w_high_ready, 1)

                def attend(hd, b, proj, more=True):
                    p, pb = hd + 1, 1 - b

                    def exp(q):
                        n = TOK if q < LT else CTX
                        act.wait_ge(max_ready[l], hd * qt_n + q + 1)
                        if q >= 2:
                            act.wait_ge(probs_turned[l], hd * qt_n + q - 1)
                        nc.scalar.activation(prob[q % 2][:, 0:n], ps[q % 2][:, 0:n], ACT.Exp, bias=bias[:, q:q + 1],
                                             scale=q_pos[b][:, q:q + 1], accum_out=total[:, q:q + 1]).then_inc(exp_ready[l], 1)

                    def turned(q):
                        act.wait_ge(probs_turned[l], hd * qt_n + q + 1)
                        if q < LT:
                            if q == 0 and not (isinstance(hd, int) and hd == 0):
                                act.wait_ge(attended, HEADS * l + hd)
                            copy(prob_t[:, :, q * P:(q + 1) * P], D[:, 0:TOK].rearrange("p (k q) -> p k q", k=TT)).then_inc(probs_copied[l], 1)
                        else:
                            q -= LT
                            copy(prob_tc[:, :, q * P:(q + 1) * P], D[:, q * 512:q * 512 + CTX].rearrange("p (k q) -> p k q", k=2))\
                                .then_inc(probs_copied[l], 1)

                    if proj:
                        queries(p, pb)
                    act.wait_ge(softmax_scale_ready, 2 * HEADS * l + 2 * hd + 2)
                    exp(0)
                    exp(1)
                    turned(0)
                    if proj:
                        rotary_squares(p, pb)
                    exp(2)
                    turned(1)
                    exp(3)
                    turned(2)
                    if qt_n > LT:
                        exp(4)
                    turned(3)
                    if proj:
                        key_square(p)
                    else:
                        out_split(0, 0, 0)
                    if qt_n > LT:
                        exp(5)
                        turned(4)
                    if proj:
                        keys()
                    if qt_n > LT:
                        turned(5)
                    if proj:
                        roots(p, pb)
                        if more:
                            query_weights_high(p + 1, b)
                            key_weights_high(b)
                        keys_high(p)

                for b in range(2):
                    act.wait_ge(gate_stored[b], 80 * (l + 1))
                queries(0, 0)
                for j in range(RT, 2 * RT):
                    latent_high(j)
                key_weights_high(0)
                rotary_squares(0, 0)
                key_square(0)
                keys()
                roots(0, 0)
                query_weights_high(1, 1)
                key_weights_high(1)
                keys_high(0)
                attend(0, 0, True)
                attend(1, 1, True)
                with act.Fori(1, HEADS // 2 - 1) as i:
                    for b in range(2):
                        attend(2 * i + b, b, True)
                attend(HEADS - 2, 0, True, more=False)
                attend(HEADS - 1, 1, False)

                out_split(0, 1, 1)

                def head_high(hd):
                    act.wait_ge(head_gated, HEADS * l + hd + 1)
                    copy(act_hi[:, 8 + hd, 0:nq], h[:, 8 + hd, 0:nq]).then_inc(head_high_ready, 1)

                def group_high(k):
                    if k == 0:
                        act.wait_ge(groups_loaded, 16 * (l + 1))
                    copy(act_hi[:, k, 0:nq], groups_in[:, k, 0:nq]).then_inc(group_high_ready, 1)

                act.wait_ge(scores_ready[l], HEADS * qt_n)
                for hd in range(HEADS - 1):
                    head_high(hd)
                act.wait_ge(head_values_ready, HEADS * (l + 1))
                for k in range(6):
                    group_high(k)
                head_high(HEADS - 1)
                for k in range(6, 2 * GROUPS):
                    group_high(k)

                def out_tile(i, j, first=False, last=False):
                    n = 4 * i + j
                    if not (last and j >= 2):
                        act.wait_ge(out_tile_done[l], n + 1)
                        out_split(i + (j + 2) // 4, (j + 2) % 4, n + 2)
                    if l == 0:
                        act.wait_ge(new_stream_ready[0], n + 1)
                        if not (first and j < 2):
                            act.wait_ge(stream_square_added[1], n - 1)
                        square(sq_t[j % 2], xt[j]).then_inc(stream_squared[1], 1)
                        if last and j == 2:
                            act.wait_ge(w_loaded[1][0], 16)
                            copy(w_hi[0], w_cols(w_slot, 0)).then_inc(w_high_ready, 1)
                    else:
                        act.wait_ge(out_turned, n + 1)
                        if not (first and j < 2):
                            act.wait_ge(out_stored[j % 2], 32 * i + 16 * (j // 2))
                        copy(o_nat[j % 2], (C, D)[j % 2][:, 0:512].rearrange("p (t n) -> p t n", t=LT)).then_inc(out_copied, 1)

                for j in range(4):
                    out_tile(0, j, first=True)
                with act.Fori(1, 3) as i:
                    for j in range(4):
                        out_tile(i, j)
                for j in range(4):
                    out_tile(3, j, last=True)

        @block.vector
        def _(dve):
            link = Link(dve, dve_own)
            tt, ts, stt = nc.vector.tensor_tensor, nc.vector.tensor_scalar, nc.vector.scalar_tensor_tensor
            nc.vector.memset(cond, 0.0).then_inc(zeros_set, 1)
            nc.vector.memset(eps[:, :], EPS).then_inc(zeros_set, 1)
            nc.vector.memset(ones[:, :], 1.0).then_inc(zeros_set, 1)
            link(nc.vector.memset(sq, 0.0))
            with dve.Fori(0, TT // 2) as i:
                for g in range(0, 8, 2):
                    dve.wait_ge(tokens_turned, 8 * i + g + 1)
                    nc.vector.tensor_copy(h[:, 4 * (g % 4):4 * (g % 4) + 4, bass.ds((2 * i + g // 4) * P, P)],
                                          bank(g % 4).rearrange("p (k t) -> p k t", k=4)).then_inc(tokens_copied_dve, 1)
            dve.wait_ge(params_turned, 2)
            for l in range(DEPTH):
                nc.vector.tensor_copy(par[l][:, :], ps[2 + l][:, 0:PR_N]).then_inc(params_copied, 1)
            dve.wait_ge(params_copied, 2)
            for b in range(2):
                dve.wait_ge(stream_squared[0], b + 1)
                if b:
                    dve.wait_ge(stream_square_added[0], b)
                tt(sq, sq, sq_t[b], ALU.add).then_inc(stream_square_added[0], 1)
            with dve.Fori(1, KT // 2) as i:
                for b in range(2):
                    dve.wait_ge(stream_squared[0], 2 * i + b + 1)
                    dve.wait_ge(stream_square_added[0], 2 * i + b)
                    tt(sq, sq, sq_t[b], ALU.add).then_inc(stream_square_added[0], 1)

            def ada_gain(l):
                for t in range(2):
                    stt(gain_v[l][:, t], ada_v[l][:, t, KT:2 * KT], 1.0, par[l][:, PR_NORM:PR_NORM + KT],
                        ALU.add, ALU.mult).then_inc(gain_ready, 1)

            with dve.Fori(0, ADA_CHUNKS // 2) as i:
                for b in range(2):
                    dve.wait_ge(ada_column_ready, 2 * i + b + 1)
                    for t in range(2):
                        tt(ada_v[0][:, t, bass.ds(8 * i + 4 * b, 4)],
                           D[:, b * 512:b * 512 + 8].rearrange("p (j t) -> p t j", t=2)[:, t],
                           par[0][:, bass.ds(8 * i + 4 * b, 4)], ALU.add).then_inc(ada_added, 1)
            dve.wait_ge(ada_added, ADA_0)
            ada_gain(0)

            for l in range(DEPTH):
                nq = q_tok(l)
                qt_n = q_tiles(l)
                dve.wait_ge(stream_root_ready, l + 1)
                link(nc.vector.reciprocal(inv_root[:, 0:TT], root[:, 0:TT]))
                for t in range(TT):
                    ts(n_diag[:, t * P:(t + 1) * P], ident[:, :], inv_root[:, t:t + 1], None, ALU.mult).then_inc(stream_diag_ready, 1)
                if l == 0:
                    dve.wait_ge(stream_spilled, 16)

                def w_low(n):
                    at = at_of(n)
                    dve.wait_ge(w_high_ready, SPLITS * l + n + 1)
                    if n == T_KROPE:
                        tt(kr_lo, kr_w, w_hi[0].bitcast(F32), ALU.subtract).then_inc(w_low_ready, 1)
                    else:
                        tt(w_cols(w_lo, at % 4), w_cols(w_slot, at % 4), w_hi[n % 2].bitcast(F32), ALU.subtract).then_inc(w_low_ready, 1)

                def stream_scale(k, t):
                    a, n = streams[t]
                    stt(h[:, k, a:a + n], h[:, k, a:a + n], gain[l][:, t * KT + k:t * KT + k + 1], D[:, a:a + n],
                        ALU.mult, ALU.mult).then_inc(stream_scaled, 1)

                def stream_low(k, t):
                    a, n = streams[t]
                    dve.wait_ge(stream_high_ready, stream_at(l, k, t))
                    stt(act_lo[:, k, a:a + n], h[:, k, a:a + n], ada[l][:, t * 48 + k:t * 48 + k + 1], hi_f32[:, k, a:a + n],
                        ALU.add, ALU.subtract).then_inc(stream_low_ready, 1)

                if l == 0:
                    w_low(0)
                w_low(1)
                dve.wait_ge(stream_row_ready, l + 1)
                n_t = 2 if l == 0 else 1
                for k in range(KT + 2):
                    if k < KT:
                        if l > 0 and k % 4 == 0:
                            dve.wait_ge(stream_loaded[k // 4], 16)
                        for t in range(n_t):
                            stream_scale(k, t)
                    if k >= 2:
                        for t in range(n_t):
                            stream_low(k - 2, t)
                if l == 1:
                    for k in range(KT):
                        stream_scale(k, 1)

                def ada_add(i):
                    dve.wait_ge(ada_column_ready, ADA_CHUNKS + i + 1)
                    for t in range(2):
                        tt(ada_v[1][:, t, 4 * i:4 * i + 4], ada_cols(i).rearrange("p (j t) -> p t j", t=2)[:, t],
                           par[1][:, 4 * i:4 * i + 4], ALU.add).then_inc(ada_added, 1)

                for n in range(T_POOL):
                    if n > 0:
                        w_low(n + 1)
                    if l == 0 and n > 0:
                        ada_add(n - 1)
                    if l == 1 and n in (1, 2):
                        for k in range(8 * (n - 1), 8 * n):
                            stream_low(k, 1)

                w_low(T_POOL + 1)
                for b in range(2):
                    dve.wait_ge(gate_stored[b], 80 * l + 16)
                link(nc.vector.memset(pad_u, 0.0))
                seqs = seqs_of(l)
                width = PW if l == 0 else LAT0 + SEQ + PAD

                def pool_gate(g):
                    dve.wait_ge(pool_product_done, GROUPS * l + g + 1)
                    dve.wait_ge(gate_loaded[g % 2], 64 * l + 16 * (g // 2) + 16)
                    stt(gate_in[g % 2][:, 0:nq], D[:, 0:nq], par[l][:, PR_POOL + g:PR_POOL + g + 1], gate_in[g % 2][:, 0:nq],
                        ALU.mult, ALU.mult).then_inc(pool_gated, 1)

                for g in range(GROUPS):
                    if g >= 1:
                        w_low(T_POOL + g + 1)
                    if l == 0:
                        ada_add(T_POOL + g - 1)
                    dve.wait_ge(in_tile_done[l], T_POOL + g + 1)
                    if g >= 1:
                        dve.wait_ge(pooled_ready[l], g * len(seqs))
                    for k, (a, n, at) in enumerate(seqs):
                        ins = nc.vector.tensor_copy(pad_u[:, at:at + n], ps[g % 2][:, a:a + n])
                        if k < len(seqs) - 1:
                            link(ins)
                    ins.then_inc(in_tile_copied[l], 1)
                    dve.wait_ge(in_tile_copied[l], g + 1)
                    if g >= 1:
                        pool_gate(g - 1)
                    src, dst = pad_u, win[0]
                    link(tt(dst[:, 1:width], src[:, 0:width - 1], src[:, 1:width], ALU.add))
                    lo = 1
                    for lev in range(g):
                        step = 1 << lev
                        src, dst = dst, win[(lev + 1) % 2]
                        a, e = 2 << lev, width - (2 << lev) + 1
                        link(tt(dst[:, a:e], src[:, a - step:e - step], src[:, a + step:e + step], ALU.add))
                    if g >= 1:
                        dve.wait_ge(pool_product_done, GROUPS * l + g)
                    dve.wait_ge(inv_loaded[g % 2], 32 * l + 16 * (g // 2) + 16)
                    for a, n, at in seqs:
                        link(tt(pooled[:, a:a + n], dst[:, at:at + n], inv[g % 2][:, a:a + n], ALU.mult))
                    for k, (a, n, at) in enumerate(seqs):
                        ins = tt(pooled[:, a:a + n], pooled[:, a:a + n], pad_u[:, at:at + n], ALU.subtract)
                        ins.then_inc(pooled_ready[l], 1)
                w_low(T_FNET + 1)
                if l == 0:
                    ada_add(ADA_CHUNKS - 1)
                    dve.wait_ge(ada_added, ADA_0 + 2 * ADA_CHUNKS)
                    ada_gain(1)
                pool_gate(GROUPS - 1)
                w_low(T_FNET + 2)
                w_low(T_FNET + 3)
                for g in range(GROUPS):
                    dve.wait_ge(fourier_positions_done, GROUPS * l + g + 1)
                    dve.wait_ge(gate_loaded[g % 2], 64 * l + 16 * (g // 2) + 48)
                    tt(gate_in[g % 2][:, 0:nq], D[:, 0:nq], gate_in[g % 2][:, 0:nq], ALU.mult).then_inc(fourier_gated, 1)
                    w_low(T_CQ + g)
                for n in range(T_CKV, T_MLA + 1):
                    w_low(n)

                dve.wait_ge(in_tile_done[l], T_KROPE + 1)
                stt(u_kr, A[:, 0:TOK], par[l][:, PR_KHR:PR_KHR + 1], rope[:, :], ALU.mult, ALU.mult).then_inc(rotary_key_read, 1)
                w_low(T_MLA + 1)
                n_tmp = 0
                for j in range(2 * RT):
                    if j % RT:
                        n = nq if j < RT else TOK
                        acc = (sq_q, sq_k)[j // RT]
                        dve.wait_ge(latent_squared, 2 * RT * l + j + 1)
                        if n_tmp:
                            dve.wait_ge(latent_square_added, 2 * (RT - 1) * l + n_tmp)
                        tt(acc[:, 0:n], acc[:, 0:n], sq_c[n_tmp % 2][:, 0:n], ALU.add).then_inc(latent_square_added, 1)
                        n_tmp += 1
                w_low(T_MLA + 2)
                dve.wait_ge(latent_root_ready, l + 1)
                link(nc.vector.reciprocal(inv_root[:, TT - qt_n:2 * TT], root[:, TT - qt_n:2 * TT]))
                for t in range(qt_n):
                    ts(q_diag[:, t * P:(t + 1) * P], ident[:, :], inv_root[:, TT - qt_n + t:TT - qt_n + t + 1], None,
                       ALU.mult).then_inc(latent_diag_ready[l], 1)
                for t in range(TT):
                    ts(diag[:, t * P:(t + 1) * P], ident[:, :], inv_root[:, TT + t:TT + t + 1], None, ALU.mult).then_inc(latent_diag_ready[l], 1)
                w_low(T_MLA + 3)
                dve.wait_ge(latent_rows_ready, l + 1)
                for j in range(2 * RT):
                    n, src = (nq, C) if j < RT else (TOK, D)
                    stt(ckk[:, j, 0:n], ckk[:, j, 0:n], par[l][:, PR_QN + j:PR_QN + j + 1], src[:, 0:n],
                        ALU.mult, ALU.mult).then_inc(latent_normed, 1)
                for n in range(T_MLA + 4, MM_IN):
                    w_low(n)
                dve.wait_ge(in_tile_done[l], MM_IN)
                dve.wait_ge(rotary_key_squared, l + 1)
                nc.vector.tensor_copy(kr_sq[0:ROPE, :], kr_sq0[0:ROPE, :]).then_inc(key_square_moved, 1)

                def latent_low(j):
                    n = nq if j < RT else TOK
                    if j == RT:
                        dve.wait_ge(values_multiplied, TT * (l + 1))
                    dve.wait_ge(latent_high_ready, 2 * RT * l + j + 1)
                    tt(ckk_lo[:, j, 0:n], ckk[:, j, 0:n], (cq_hi, ckv_hi)[j // RT][:, j % RT, 0:n].bitcast(F32),
                       ALU.subtract).then_inc(latent_low_ready, 1)

                def query_weights_low(p, b):
                    dve.wait_ge(head_w_high_ready, 2 * HEADS * l + 2 * p + 1)
                    tt(wq_lo[b], wq[b], wq_hi.bitcast(F32), ALU.subtract).then_inc(head_w_low_ready, 1)

                def key_weights_low(p, b):
                    dve.wait_ge(head_w_high_ready, 2 * HEADS * l + 2 * p + 2)
                    tt(wk_lo[b], wk[b], wk_hi.bitcast(F32), ALU.subtract).then_inc(head_w_low_ready, 1)

                def queries_low(p, b):
                    dve.wait_ge(query_copied, 2 * HEADS * l + 2 * p + 2)
                    stt(qn_lo[b][:, 0:nq], C[:, 0:nq], par[l][:, PR_QH:PR_QH + 1], qn_hi[b][:, 0:nq].bitcast(F32),
                        ALU.mult, ALU.subtract).then_inc(query_low_ready, 1)

                for j in range(RT):
                    latent_low(j)

                def rotary(p, b):
                    dve.wait_ge(query_rotary_projected, HEADS * l + p + 1)
                    stt(qr[b][:, 0:nq], C[:, 0:nq], par[l][:, PR_QHR:PR_QHR + 1], rope[:, 0:nq], ALU.mult, ALU.mult).then_inc(query_rotated, 1)

                def rotary_square_sum(p):
                    dve.wait_ge(query_rotary_squared, HEADS * l + p + 1)
                    dve.wait_ge(query_copied, 2 * HEADS * l + 2 * p + 2)
                    tt(sq_q[0:ROPE, 0:nq], sq_q[0:ROPE, 0:nq], sq_r[0:ROPE, 0:nq], ALU.add).then_inc(query_squares_ready, 1)

                def rotary_low(p, b):
                    dve.wait_ge(query_rotary_high_ready, HEADS * l + p + 1)
                    tt(qr_lo[b][:, 0:nq], qr[b][:, 0:nq], qr_hi[b][:, 0:nq].bitcast(F32), ALU.subtract).then_inc(query_rotary_low_ready, 1)

                def key_squares(p):
                    dve.wait_ge(key_copied, 2 * HEADS * l + 2 * p + 1)
                    tt(sq_k[0:ROPE, :], sq_k[0:ROPE, :], kr_sq[0:ROPE, :], ALU.add).then_inc(key_squares_ready, 1)

                def inverses(p, b, own):
                    dve.wait_ge(head_roots_ready, HEADS * l + p + 1)
                    own(nc.vector.reciprocal(h_inv[b][:, TT - qt_n:2 * TT], h_root[b][:, TT - qt_n:2 * TT]))
                    ts(q_pos[b][:, 0:qt_n], h_inv[b][:, TT - qt_n:TT], SM_SCALE, None, ALU.mult).then_inc(softmax_scale_ready, 1)
                    ts(q_neg[b][:, 0:qt_n], h_inv[b][:, TT - qt_n:TT], -SM_SCALE, None, ALU.mult).then_inc(softmax_scale_ready, 1)
                    for t in range(TT):
                        ts(diag[:, t * P:(t + 1) * P], ident[:, :], h_inv[b][:, TT + t:TT + t + 1], None, ALU.mult).then_inc(key_diag_ready, 1)

                def scale_keys(p, b):
                    dve.wait_ge(key_row_ready, HEADS * l + p + 1)
                    tt(kn, kn, B[:, 0:TOK], ALU.mult).then_inc(key_scaled, 1)
                    tt(krh, kr, B[:, 0:TOK], ALU.mult).then_inc(key_scaled, 1)

                def keys_low(p):
                    dve.wait_ge(key_high_ready, 2 * HEADS * l + 2 * p + 1)
                    tt(kn_lo, kn, kn_hi.bitcast(F32), ALU.subtract).then_inc(key_low_ready, 1)
                    dve.wait_ge(key_high_ready, 2 * HEADS * l + 2 * p + 2)
                    tt(krh_lo, krh, krh_hi.bitcast(F32), ALU.subtract).then_inc(key_low_ready, 1)

                GH = 16 * HEADS // 2

                def head_low(hd):
                    dve.wait_ge(head_high_ready, HEADS * l + hd + 1)
                    tt(act_lo[:, 8 + hd, 0:nq], h[:, 8 + hd, 0:nq], hi_f32[:, 8 + hd, 0:nq], ALU.subtract).then_inc(head_low_ready, 1)

                def out_low(i, j):
                    dve.wait_ge(w_high_ready, SPLITS * l + MM_IN + 4 * i + j + 1)
                    tt(w_cols(w_lo, j), w_cols(w_slot, j), w_hi[j % 2].bitcast(F32), ALU.subtract).then_inc(w_low_ready, 1)

                def attend(hd, b, proj, more=True):
                    p, pb = hd + 1, 1 - b
                    own = Link(dve, dve_own_head[l], 1 + (2 * qt_n + 1) * hd)

                    def maxima(q):
                        n = TOK if q < LT else CTX
                        dve.wait_ge(scores_ready[l], hd * qt_n + q + 1)
                        own(nc.vector.tensor_reduce(top[:, q:q + 1], ps[q % 2][:, 0:n], AX_X, ALU.max))
                        tt(bias[:, q:q + 1], top[:, q:q + 1], q_neg[b][:, q:q + 1], ALU.mult).then_inc(max_ready[l], 1)

                    def normalise(q):
                        n = TOK if q < LT else CTX
                        dve.wait_ge(exp_ready[l], hd * qt_n + q + 1)
                        own(nc.vector.reciprocal(inv_total[:, q:q + 1], total[:, q:q + 1]))
                        ts(prob[q % 2][:, 0:n], prob[q % 2][:, 0:n], inv_total[:, q:q + 1], None, ALU.mult).then_inc(probs_normalised[l], 1)

                    dve.wait_ge(softmax_scale_ready, 2 * HEADS * l + 2 * hd + 2)
                    maxima(0)
                    if proj:
                        queries_low(p, pb)
                    maxima(1)
                    normalise(0)
                    if proj:
                        rotary(p, pb)
                    normalise(1)
                    maxima(2)
                    if proj:
                        rotary_square_sum(p)
                    normalise(2)
                    maxima(3)
                    if proj:
                        rotary_low(p, pb)
                    normalise(3)
                    if qt_n > LT:
                        maxima(4)
                        normalise(4)
                        maxima(5)
                    if proj:
                        key_squares(p)
                    else:
                        out_low(0, 0)
                    if qt_n > LT:
                        normalise(5)
                    if proj:
                        inverses(p, pb, own)
                        if more:
                            query_weights_low(p + 1, b)
                            key_weights_low(p + 1, b)
                    if not proj:
                        out_low(0, 1)
                        for j in range(HEADS - 1):
                            head_low(j)
                    dve.wait_ge(attended, HEADS * l + hd + 1)
                    dve.wait_ge(head_gate_loaded[b], GH * l + 8 * (hd - b) + 16)
                    tt(h[:, bass.ds(8 + hd, 1), 0:nq].rearrange("p a t -> p (a t)"), A[:, 0:nq], gate_h[b][:, 0:nq],
                       ALU.mult).then_inc(head_gated, 1)
                    if proj:
                        scale_keys(p, pb)
                        keys_low(p)

                dve.wait_ge(rotary_key_ready, l + 1)
                dve.wait_ge(key_square_moved, l + 1)
                query_weights_low(0, 0)
                queries_low(0, 0)
                for j in range(RT, 2 * RT):
                    latent_low(j)
                key_weights_low(0, 0)
                rotary(0, 0)
                rotary_square_sum(0)
                rotary_low(0, 0)
                key_squares(0)
                inverses(0, 0, Link(dve, dve_own_head[l]))
                query_weights_low(1, 1)
                key_weights_low(1, 1)
                scale_keys(0, 0)
                keys_low(0)
                attend(0, 0, True)
                attend(1, 1, True)
                with dve.Fori(1, HEADS // 2 - 1) as i:
                    for b in range(2):
                        attend(2 * i + b, b, True)
                attend(HEADS - 2, 0, True, more=False)
                attend(HEADS - 1, 1, False)

                def group_low(k):
                    dve.wait_ge(group_high_ready, 2 * GROUPS * l + k + 1)
                    tt(act_lo[:, k, 0:nq], groups_in[:, k, 0:nq], hi_f32[:, k, 0:nq], ALU.subtract).then_inc(group_low_ready, 1)

                for k in range(6):
                    group_low(k)
                head_low(HEADS - 1)
                for k in range(6, 2 * GROUPS):
                    group_low(k)

                if l == 0:
                    link(nc.vector.memset(sq, 0.0))

                def out_tile(i, j, first=False, last=False):
                    n = 4 * i + j
                    src = (B, A)[j % 2]
                    dve.wait_ge(out_tile_done[l], n + 1)
                    dve.wait_ge(residual_loaded[j], 64 * l + 16 * i + 16)
                    if l == 0:
                        stt(xt[j][:, SEQ:TOK], src[:, SEQ:TOK], ada[l][:, bass.ds(n + 48 + 2 * KT, 1)], xt[j][:, SEQ:TOK],
                            ALU.mult, ALU.add)
                    stt(xt[j][:, 0:SEQ], src[:, 0:SEQ], ada[l][:, bass.ds(n + 2 * KT, 1)], xt[j][:, 0:SEQ],
                        ALU.mult, ALU.add).then_inc(new_stream_ready[l], 1)
                    if not (last and j >= 2):
                        out_low(i + (j + 2) // 4, (j + 2) % 4)
                    if l == 0:
                        dve.wait_ge(stream_squared[1], n + 1)
                        if not (first and j == 0):
                            dve.wait_ge(stream_square_added[1], n)
                        tt(sq, sq, sq_t[j % 2], ALU.add).then_inc(stream_square_added[1], 1)
                        if last and j == 2:
                            dve.wait_ge(w_high_ready, SPLITS + 1)
                            tt(w_cols(w_lo, 0), w_cols(w_slot, 0), w_hi[0].bitcast(F32), ALU.subtract).then_inc(w_low_ready, 1)

                for j in range(4):
                    out_tile(0, j, first=True)
                with dve.Fori(1, 3) as i:
                    for j in range(4):
                        out_tile(i, j)
                for j in range(4):
                    out_tile(3, j, last=True)

        @block.tensor
        def _(pe):
            mm, tr = nc.tensor.matmul, nc.tensor.transpose
            pe.wait_ge(consts_loaded, 16 * N_CONST)

            def stream_in(i, first=False):
                for g in range(8):
                    if g % 4 == 0:
                        pe.wait_ge(tokens_loaded[g // 4], 16 * i + 16)
                    if not (first and g < 4):
                        pe.wait_ge((tokens_copied_dve, tokens_copied_act)[g % 2], 4 * i + g // 2 - 1)
                    for j in range(4):
                        k = 4 * (g % 4) + j
                        ins = tr(bank(g % 4)[:, j * P:(j + 1) * P], x_nat[g // 4][:, k * P:(k + 1) * P], ident[:, :])
                    ins.then_inc(tokens_turned, 1)

            stream_in(0, first=True)
            with pe.Fori(1, TT // 2) as i:
                stream_in(i)
            pe.wait_ge(params_loaded, 16 * N_PAR)
            for l in range(DEPTH):
                tr(ps[2 + l][:, 0:PR_N], par_row[l][0:PR_N, :], ident[0:PR_N, 0:PR_N]).then_inc(params_turned, 1)
            pe.wait_ge(params_copied, 2)
            pe.wait_ge(cond_ready, 2)

            def ada_chunk(i, b, first=False):
                if not first:
                    pe.wait_ge(ada_row_copied, 2 * i + b - 1)
                for hf in range(2):
                    s = 2 * b + hf
                    pe.wait_ge(w_ada_loaded[s], 16 * i + 16)
                    for k in range(8):
                        q = k % 4
                        ins = mm(C[32 * q:32 * q + 32, b * 512:(b + 1) * 512], cond[:, 8 * hf + k, :], ada_slot[s][:, k, :],
                                 start=(hf == 0 and k < 4), stop=(hf == 1 and k >= 4))
                    ins.then_inc(ada_multiplied, 1)
                pe.wait_ge(ada_row_copied, 2 * i + b + 1)
                if not first:
                    pe.wait_ge(ada_added, 4 * i + 2 * b - 2)
                for j in range(4):
                    ins = mm(D[:, b * 512 + 2 * j:b * 512 + 2 * j + 2], ada_row[b][:, j * P:(j + 1) * P], sel[:, :],
                             start=True, stop=True)
                ins.then_inc(ada_column_ready, 1)

            ada_chunk(0, 0, first=True)
            ada_chunk(0, 1, first=True)
            with pe.Fori(1, ADA_CHUNKS // 2) as i:
                for b in range(2):
                    ada_chunk(i, b)

            for l in range(DEPTH):
                nq = q_tok(l)
                qt_n = q_tiles(l)
                pe.wait_ge(stream_square_added[l], KT)
                for t in range(TT):
                    ins = mm(A[:, t:t + 1], sq[:, t * P:(t + 1) * P], ones[:, 0:1], start=True, stop=True)
                ins.then_inc(stream_sums_ready, 1)
                pe.wait_ge(stream_diag_ready, (l + 1) * TT)
                if l == 0:
                    pe.wait_ge(ada_added, ADA_0)
                for a, n in parts(TOK):
                    ins = mm(D[:, a:a + n], ones[:, :], n_diag[:, a:a + n], start=True, stop=True)
                ins.then_inc(stream_row_ready, 1)

                def products(dst, hi, lo, k, ntok, first, last):
                    for c, (w, a_) in enumerate(((hi, act_hi), (hi, act_lo), (lo, act_hi))):
                        for a, n in parts(ntok):
                            ins = mm(dst[:, a:a + n], w[:, k, :], a_[:, k, a:a + n], start=(first and c == 0), stop=(last and c == 2))
                    return ins

                def ada_quarter(i, q):
                    pe.wait_ge(w_ada_loaded[q % 2], 16 * (ADA_0 // 4) + 32 * i + 16 * (q // 2) + 16)
                    for k in range(4):
                        ins = mm(C[32 * k:32 * k + 32, (i % 2) * 512:(i % 2) * 512 + 512], cond[:, 4 * q + k, :], ada_part[q % 2][:, k, :],
                                 start=(q == 0), stop=(q == 3))
                    ins.then_inc(ada_multiplied, 1)

                def ada_turn(i):
                    pe.wait_ge(ada_row_copied, ADA_CHUNKS + i + 1)
                    if i >= 1:
                        pe.wait_ge(ada_added, ADA_0 + 2 * i)
                    if i > T_POOL:
                        pe.wait_ge(pool_gated, i - T_POOL)
                    for j in range(4):
                        ins = mm(ada_cols(i)[:, 2 * j:2 * j + 2], ada_row1[:, j * P:(j + 1) * P], sel[:, :], start=True, stop=True)
                    ins.then_inc(ada_column_ready, 1)

                def tile(hi, lo, b_ps, ntok, first=False, chunk=None):
                    for k in range(8 if chunk == 1 else 0, KT):
                        if first:
                            pe.wait_ge(stream_low_ready, stream_at(l, k, 1 - l))
                            if k < 8:
                                products(ps[1], w_hi[1], w_cols(w_lo, 1), k, ntok, k == 0, False)
                        ins = products(ps[b_ps], hi, lo, k, ntok, k == 0, k == KT - 1)
                        if l == 0 and chunk is not None:
                            if chunk == 1 and k % 2 == 1:
                                ada_quarter(1, (k - 8) // 2)
                            elif chunk != 1 and k % 4 == 2 and chunk < ADA_CHUNKS:
                                ada_quarter(chunk, k // 4)
                            if k == (12 if chunk == 1 else 8) and 1 <= chunk <= ADA_CHUNKS:
                                ada_turn(chunk - 1)
                    ins.then_inc(in_tile_done[l], 1)

                pe.wait_ge(w_low_ready, SPLITS * l + 2)
                tile(w_hi[0], w_cols(w_lo, 0), 0, nq, first=True, chunk=0)
                for n in range(1, 8):
                    pe.wait_ge(w_low_ready, SPLITS * l + n + 1)
                    tile(w_hi[n % 2], w_cols(w_lo, n % 4), n % 2, nq, chunk=n)

                def in_tile(n, ntok):
                    pe.wait_ge(w_low_ready, SPLITS * l + n + 1)
                    if n == T_KROPE + 2:
                        pe.wait_ge(rotary_key_squared, l + 1)
                    tile(w_hi[n % 2], kr_lo if n == T_KROPE else w_cols(w_lo, at_of(n) % 4), n % 2, ntok, chunk=n)


                def pool_product(g):
                    pe.wait_ge(pooled_ready[l], (g + 1) * (1 if l else 2))
                    if g == 0:
                        pe.wait_ge(pool_w_loaded, 16 * (l + 1))
                    else:
                        pe.wait_ge(pool_gated, GROUPS * l + g)
                    if l == 0:
                        pe.wait_ge(ada_added, ADA_0 + 2 * (T_POOL + g + 1))
                    for a, n in parts(nq):
                        ins = mm(D[:, a:a + n], pw[:, g, :], pooled[:, a:a + n], start=True, stop=True)
                    ins.then_inc(pool_product_done, 1)

                def fourier_channels(g):
                    n = T_FNET + g
                    pe.wait_ge(in_tile_copied[l], GROUPS + g + 1)
                    if g == 0:
                        pe.wait_ge(chan_w_copied, (l + 1) * 2)
                    if g > 0:
                        pe.wait_ge(fourier_ab_copied[l], g * (1 if l else 2))
                    for t in range(qt_n):
                        if t == LT:
                            pe.wait_ge(pool_gated, (l + 1) * GROUPS)
                            if g > 0:
                                pe.wait_ge(fourier_gated, GROUPS * l + g)
                        dst = C[:, t * 256:(t + 1) * 256] if t < LT else D[:, (t - LT) * 256:(t - LT + 1) * 256]
                        ins = mm(dst, f_u[g % 2][:, t * P:(t + 1) * P], chan_w[:, g, :], start=True, stop=True)
                    ins.then_inc(fourier_channels_done, 1)

                def fourier_positions(g):
                    pe.wait_ge(fourier_ab_copied[l], (g + 1) * (1 if l else 2))
                    pe.wait_ge(pool_gated, (l + 1) * GROUPS)
                    if g > 0:
                        pe.wait_ge(fourier_gated, GROUPS * l + g)
                    for a, n, first_t, n_t, tab in ((0, SEQ, 0, LT, pos_lat), (SEQ, CTX, LT, 2, pos_ctx))[:1 if l else 2]:
                        for t in range(n_t):
                            for s in range(2):
                                ins = mm(D[:, a:a + n], f_ab[:, first_t + t, s * P:(s + 1) * P], tab[:, s, t, :],
                                         start=(t == 0 and s == 0), stop=(t == n_t - 1 and s == 1))
                    ins.then_inc(fourier_positions_done, 1)

                for g in range(GROUPS):
                    in_tile(T_POOL + g, nq)
                    if g >= 1:
                        pool_product(g - 1)
                for m in range(GROUPS + 2):
                    in_tile(T_FNET + m, nq)
                    if m == 0:
                        pool_product(GROUPS - 1)
                        pe.wait_ge(tables_loaded[l], 16 * (6 if l == 0 else 4))
                        for s in range(2):
                            ins = mm(C[:, s * 512:(s + 1) * 512], chan[:, s * P:(s + 1) * P], fw, start=True, stop=True)
                        ins.then_inc(chan_w_done, 1)
                    if m >= 2:
                        fourier_positions(m - 2)
                    if 1 <= m <= GROUPS:
                        fourier_channels(m - 1)
                for n in range(T_CQ + 2, T_KROPE):
                    in_tile(n, nq if n < T_CKV else TOK)
                in_tile(T_KROPE, TOK)
                in_tile(T_MLA, nq)
                in_tile(T_MLA + 1, nq)
                pe.wait_ge(latent_square_added, (l + 1) * (2 * (RT - 1)))
                pe.wait_ge(fourier_gated, (l + 1) * GROUPS)
                for t in range(qt_n):
                    mm(D[:, TT - qt_n + t:TT - qt_n + t + 1], sq_q[:, t * P:(t + 1) * P], ones[:, 0:1], start=True, stop=True)
                for t in range(TT):
                    ins = mm(D[:, TT + t:TT + t + 1], sq_k[:, t * P:(t + 1) * P], ones[:, 0:1], start=True, stop=True)
                ins.then_inc(latent_sums_ready, 1)
                in_tile(T_MLA + 2, nq)
                pe.wait_ge(latent_diag_ready[l], qt_n + TT)
                for dst, src, ntok in ((C, q_diag, nq), (D, diag, TOK)):
                    for a, n in parts(ntok):
                        ins = mm(dst[:, a:a + n], ones[:, :], src[:, a:a + n], start=True, stop=True)
                ins.then_inc(latent_rows_ready, 1)
                for n in range(T_MLA + 3, MM_IN):
                    in_tile(n, nq)

                pe.wait_ge(head_gate_ready, HEADS * (l + 1))
                pe.wait_ge(rotary_key_read, l + 1)
                for a, n in parts(TOK):
                    ins = mm(A[:, a:a + n], dup[:, :], u_kr[:, a:a + n], start=True, stop=True)
                ins.then_inc(rotary_key_summed, 1)
                pe.wait_ge(latent_normed, (l + 1) * (2 * RT))
                pe.wait_ge(w_loaded[l][0], W_OUT[0])
                for t in range(TT):
                    if t == 1:
                        pe.wait_ge(rotary_key_ready, l + 1)
                    if t >= 2:
                        pe.wait_ge(values_copied, TT * l + t - 1)
                    for k in range(RT):
                        for a in range(0, HEADS * VDIM, 512):
                            ins = mm((B, A)[t % 2][:, a:a + 512], ckv[:, k, t * P:(t + 1) * P], v_w[:, k, a:a + 512],
                                     start=(k == 0), stop=(k == RT - 1))
                    ins.then_inc(values_multiplied, 1)

                def project(hi, lo, src_hi, src_lo, ntok, done, ks=range(RT)):
                    for k in ks:
                        for c, (w, src) in enumerate(((hi, src_hi), (hi, src_lo), (lo, src_hi))):
                            for a, n in parts(ntok):
                                ins = mm(C[:, a:a + n], w[:, k, :], src[:, k, a:a + n], start=(k == 0 and c == 0),
                                         stop=(k == RT - 1 and c == 2))
                    if k == RT - 1:
                        ins.then_inc(done, 1)

                def queries(p, b, first=False):
                    pe.wait_ge(head_w_low_ready, 2 * HEADS * l + 2 * p + 1)
                    if first:
                        pe.wait_ge(latent_low_ready, 2 * RT * l + RT)
                    else:
                        pe.wait_ge(head_roots_ready, HEADS * l + p)
                    project(wq_hi[:, :, 0:NOPE], wq_lo[b][:, :, 0:NOPE], cq_hi, cq_lo, nq, query_projected)

                def rotary(p, b):
                    pe.wait_ge(query_low_ready, HEADS * l + p + 1)
                    project(wq_hi[:, :, NOPE:NOPE + P], wq_lo[b][:, :, NOPE:NOPE + P], cq_hi, cq_lo, nq, query_rotary_projected)

                def keys(p, b, ks):
                    if ks[0] == 0:
                        pe.wait_ge(head_w_low_ready, 2 * HEADS * l + 2 * p + 2)
                        pe.wait_ge(query_rotary_squared, HEADS * l + p + 1)
                    project(wk_hi, wk_lo[b], ckv_hi, ckv_lo, TOK, key_projected, ks)

                def sums(p):
                    pe.wait_ge(query_squares_ready, HEADS * l + p + 1)
                    pe.wait_ge(key_squares_ready, HEADS * l + p + 1)
                    pe.wait_ge(key_copied, 2 * HEADS * l + 2 * p + 2)
                    for t in range(qt_n):
                        mm(C[:, TT - qt_n + t:TT - qt_n + t + 1], sq_q[:, t * P:(t + 1) * P], ones[:, 0:1], start=True, stop=True)
                    for t in range(TT):
                        ins = mm(C[:, TT + t:TT + t + 1], sq_k[:, t * P:(t + 1) * P], ones[:, 0:1], start=True, stop=True)
                    ins.then_inc(head_sums_ready, 1)

                def key_row(p):
                    pe.wait_ge(key_diag_ready, TT * HEADS * l + TT * p + TT)
                    for a, n in parts(TOK):
                        ins = mm(B[:, a:a + n], ones[:, :], diag[:, a:a + n], start=True, stop=True)
                    ins.then_inc(key_row_ready, 1)

                def attend(hd, b, proj, more=True):
                    p, pb = hd + 1, 1 - b

                    def scores(q):
                        if q == 0:
                            pe.wait_ge(key_low_ready, 2 * HEADS * l + 2 * hd + 1)
                            if not (isinstance(hd, int) and hd == 0):
                                pe.wait_ge(head_gated, HEADS * l + hd)
                        if q >= 2:
                            pe.wait_ge(exp_ready[l], hd * qt_n + q - 1)
                        key_parts = ((0, 512, 0), (512, CTX, 512)) if q < LT else ((SEQ, CTX, 0),)
                        for half, (q_hi, q_lo, k_hi, k_lo) in enumerate((
                                (qn_hi[b], qn_lo[b], kn_hi, kn_lo), (qr_hi[b], qr_lo[b], krh_hi, krh_lo))):
                            if q == 0 and half == 1:
                                pe.wait_ge(key_low_ready, 2 * HEADS * l + 2 * hd + 2)
                            for c, (w, m) in enumerate(((q_hi, k_hi), (q_hi, k_lo), (q_lo, k_hi))):
                                for a, n, o in key_parts:
                                    ins = mm(ps[q % 2][:, o:o + n], w[:, q * P:(q + 1) * P], m[:, a:a + n],
                                             start=(half == 0 and c == 0), stop=(half == 1 and c == 2))
                        ins.then_inc(scores_ready[l], 1)

                    def turn(q):
                        pe.wait_ge(probs_normalised[l], hd * qt_n + q + 1)
                        if q > 0:
                            pe.wait_ge(probs_copied[l], hd * qt_n + min(q, LT))
                        at = 0 if q <= LT else 512
                        for t in range(TT if q < LT else 2):
                            ins = tr(D[:, at + t * P:at + (t + 1) * P], prob[q % 2][:, t * P:(t + 1) * P], ident[:, :])
                        ins.then_inc(probs_turned[l], 1)

                    if proj:
                        queries(p, pb)
                    scores(0)
                    scores(1)
                    if proj:
                        rotary(p, pb)
                    turn(0)
                    scores(2)
                    turn(1)
                    scores(3)
                    turn(2)
                    if qt_n > LT:
                        scores(4)
                    if proj:
                        keys(p, pb, range(0, RT // 2))
                    turn(3)
                    if proj:
                        keys(p, pb, range(RT // 2, RT))
                    if qt_n > LT:
                        scores(5)
                        turn(4)
                    pe.wait_ge(probs_copied[l], hd * qt_n + LT)
                    pe.wait_ge(head_values_ready, HEADS * l + hd + 1)
                    for t in range(TT):
                        if t == TT // 2:
                            if qt_n > LT:
                                turn(5)
                            if proj:
                                sums(p)
                        ins = mm(A[:, 0:SEQ], vh[b][:, t, :], prob_t[:, t, :], start=(t == 0), stop=(t == TT - 1))
                    if qt_n > LT:
                        pe.wait_ge(probs_copied[l], hd * qt_n + qt_n)
                        for t in range(2):
                            ins = mm(A[:, SEQ:TOK], vh[b][:, LT + t, :], prob_tc[:, t, :], start=(t == 0), stop=(t == 1))
                    ins.then_inc(attended, 1)
                    if proj:
                        key_row(p)

                queries(0, 0, first=True)
                rotary(0, 0)
                keys(0, 0, range(RT))
                sums(0)
                pe.wait_ge(values_copied, (l + 1) * TT)
                key_row(0)
                attend(0, 0, True)
                attend(1, 1, True)
                with pe.Fori(1, HEADS // 2 - 1) as i:
                    for b in range(2):
                        attend(2 * i + b, b, True)
                attend(HEADS - 2, 0, True, more=False)
                attend(HEADS - 1, 1, False)

                def out_turn(i, j, first=False):
                    pe.wait_ge(new_stream_ready[1], 4 * i + j + 1)
                    if not (first and j < 2):
                        pe.wait_ge(out_copied, 4 * i + j - 1)
                    for t in range(LT):
                        ins = tr((C, D)[j % 2][:, t * P:(t + 1) * P], xt[j][:, t * P:(t + 1) * P], ident[:, :])
                    ins.then_inc(out_turned, 1)

                OUT_ORDER = (*range(8, 15), *range(0, 6), 15, 6, 7)

                def out_tiles(i, first=False):
                    for j in range(4):
                        pe.wait_ge(w_low_ready, SPLITS * l + MM_IN + 4 * i + j + 1)
                        for m, k in enumerate(OUT_ORDER):
                            if first and j == 0:
                                if k >= 8:
                                    pe.wait_ge(head_low_ready, HEADS * l + k - 7)
                                else:
                                    pe.wait_ge(group_low_ready, 2 * GROUPS * l + k + 1)
                            ins = products((B, A)[j % 2], w_hi[j % 2], w_cols(w_lo, j), k, nq, m == 0, m == KT - 1)
                        ins.then_inc(out_tile_done[l], 1)
                        if l == 1 and j >= 1:
                            out_turn(i, j - 1, first)
                    if l == 1:
                        out_turn(i, 3, first)

                out_tiles(0, first=True)
                with pe.Fori(1, 4) as i:
                    out_tiles(i)


def shape_tables():
    pos = np.arange(SEQ)
    inv_freq = (10000.0 ** (-np.arange(ROPE // 4, dtype=np.float32) / np.float32(ROPE // 4))).astype(np.float32)
    ang_r = ((pos // GRID_W).astype(np.float32)[:, None] * inv_freq).astype(np.float32)
    ang_c = ((pos % GRID_W).astype(np.float32)[:, None] * inv_freq).astype(np.float32)
    ang = np.concatenate([ang_r, ang_r, ang_c, ang_c], axis=-1).astype(np.float64).T
    sign = np.where(np.arange(ROPE) % 32 < 16, -1.0, 1.0)[:, None]
    rope = np.zeros((P, TOK), np.float32)
    rope[:ROPE, :SEQ] = np.cos(ang)
    rope[ROPE:, :SEQ] = np.sin(ang) * sign
    rope[:ROPE, SEQ:] = 1.0

    def dft(n):
        a = 2.0 * np.pi * (np.outer(np.arange(n), np.arange(n)) % n) / n
        return np.cos(a), np.sin(a)

    cc, sc = dft(P)
    chan = np.concatenate([cc, sc], axis=1).astype(np.float32)

    def positions(n):
        a, b = dft(n)
        return (np.stack([a, -b]) / np.sqrt(n * P)).astype(np.float32)

    inv = np.zeros((GROUPS, TOK), np.float32)
    for g, w in enumerate((2, 4, 8, 16)):
        for a, n in ((0, SEQ), (SEQ, CTX)):
            t = np.arange(n)
            count = np.clip(t + w - w // 2, 0, n) - np.clip(t - w // 2, 0, n)
            inv[g, a:a + n] = 1.0 / count
    sel = np.zeros((P, 2), np.float32)
    for q in range(4):
        sel[32 * q, 0] = sel[32 * q + 1, 1] = 1.0
    half = np.eye(ROPE, dtype=np.float32)
    return {"k_ident": np.eye(P, dtype=np.float32), "k_sel": sel, "k_dup": np.tile(half, (2, 2)), "k_rope": rope,
            "k_chan": chan, "k_pos_lat": positions(SEQ), "k_pos_ctx": positions(CTX),
            "k_inv": np.tile(inv.reshape(1, -1), (P, 1))}


INPUTS = ["x", "c", "ctx", "c_ctx", "norm_w", "w_ada", "b_ada", "w_in", "pool_w", "pool_scale", "fnet_w", "q_norm_w",
          "w_uq", "kv_norm_w", "w_ukv", "q_head_norm_w", "k_head_norm_w", "w_out"]


def kernel(**inputs):
    from concourse import bacc
    from concourse.bass_utils import run_bass_kernel_spmd

    nc = bacc.Bacc("TRN2", target_bir_lowering=False, num_devices=1)
    arrays, args = {}, []
    tables = shape_tables()
    for name in INPUTS + list(tables):
        a = np.ascontiguousarray(inputs[name] if name in inputs else tables[name])
        arrays[f"in_{name}"] = a
        args.append(nc.dram_tensor(f"in_{name}", a.shape, F32, kind="ExternalInput").ap())
    out = nc.dram_tensor("out_x", (1, SEQ, D_MODEL), F32, kind="ExternalOutput").ap()
    build(nc, *args, out)
    r = run_bass_kernel_spmd(nc, [arrays], core_ids=[0])
    return r.results[0]["out_x"]
```
